# Optimizing a Trainium2 kernel written in Bass

```python
import jax, jax.numpy as jnp
from jax import lax
import numpy as np

D_MODEL = 1024
BATCH = 1
SEQ = 256
DEPTH = 2

N_MIXERS = 3
EPS = 1e-6

RET_HEADS = 4
RET_QK_DIM = D_MODEL // RET_HEADS
RET_V_DIM = 2 * RET_QK_DIM
RET_CHUNK = 128
RET_ROPE_BASE = 10000.0
RET_IN = 2 * RET_HEADS * RET_QK_DIM + 2 * RET_HEADS * RET_V_DIM

GM_CHUNK = 128
GM_FFN = 6 * D_MODEL
GM_HALF = GM_FFN // 2
GM_GROUPS = 4
GM_GROUP_DIM = GM_HALF // GM_GROUPS

GRID_W = 64
NA_HEADS = 32
NA_HEAD_DIM = D_MODEL // NA_HEADS
NA_WIN_ROWS = 8
NA_WIN_COLS = 16

N_GROUPS = 4
EXPERTS_PER_GROUP = 4
N_EXPERTS = N_GROUPS * EXPERTS_PER_GROUP
TOP_K = 2
D_EXPERT = 512

kernel_name = 'hybrid_retention_gmlp_natten_grouped_moe_encoder'

def _rmsnorm(x, g):
    xf = x.astype(jnp.float32)
    y = xf * lax.rsqrt(jnp.mean(xf * xf, axis=-1, keepdims=True) + EPS)
    return (y * g.astype(jnp.float32)).astype(x.dtype)

def _layernorm(x, g, b):
    xf = x.astype(jnp.float32)
    mu = jnp.mean(xf, axis=-1, keepdims=True)
    var = jnp.mean(jnp.square(xf - mu), axis=-1, keepdims=True)
    y = (xf - mu) * lax.rsqrt(var + EPS)
    return (y * g.astype(jnp.float32) + b.astype(jnp.float32)).astype(x.dtype)

def _rotary(x, pos):
    half = x.shape[-1] // 2
    inv_freq = RET_ROPE_BASE ** (-jnp.arange(half, dtype=jnp.float32) / half)
    ang = pos[:, None] * inv_freq[None, :]
    cos = jnp.cos(ang)[None, :, None, :].astype(x.dtype)
    sin = jnp.sin(ang)[None, :, None, :].astype(x.dtype)
    x1, x2 = x[..., :half], x[..., half:]
    return jnp.concatenate([x1 * cos - x2 * sin, x1 * sin + x2 * cos], axis=-1)

def _retention_causal(q, k, v, log_gamma, include_diag):
    bsz, nh, seq, dk = q.shape
    dv = v.shape[-1]
    n_chunks = seq // RET_CHUNK
    qc = q.reshape(bsz, nh, n_chunks, RET_CHUNK, dk)
    kc = k.reshape(bsz, nh, n_chunks, RET_CHUNK, dk)
    vc = v.reshape(bsz, nh, n_chunks, RET_CHUNK, dv)
    idx = jnp.arange(RET_CHUNK, dtype=jnp.float32)
    diff = idx[:, None] - idx[None, :]
    mask = (diff >= 0) if include_diag else (diff > 0)
    decay = jnp.where(mask[None], jnp.exp(log_gamma[:, None, None] * jnp.where(mask, diff, 0.0)[None]), 0.0)
    scores = jnp.einsum('bhncd,bhnmd->bhncm', qc, kc) * decay[None, :, None]
    inner = jnp.einsum('bhncm,bhnme->bhnce', scores, vc)
    xi = jnp.exp(log_gamma[:, None] * (idx[None, :] + 1.0))
    zeta = jnp.exp(log_gamma[:, None] * (RET_CHUNK - 1.0 - idx[None, :]))
    chunk_decay = jnp.exp(log_gamma * RET_CHUNK)

    def step(state, inp):
        q_i, k_i, v_i = inp
        cross = jnp.einsum('bhcd,bhde->bhce', q_i, state) * xi[None, :, :, None]
        state = state * chunk_decay[None, :, None, None] + jnp.einsum(
            'bhcd,bhce->bhde', k_i, v_i * zeta[None, :, :, None])
        return state, cross

    state0 = jnp.zeros((bsz, nh, dk, dv), jnp.float32)
    _, cross = lax.scan(step, state0, (jnp.moveaxis(qc, 2, 0), jnp.moveaxis(kc, 2, 0), jnp.moveaxis(vc, 2, 0)))
    out = inner + jnp.moveaxis(cross, 0, 2)
    return out.reshape(bsz, nh, seq, dv)

def _retention_mixer(h, w_in, decay_logit, w_out):
    bsz, seq, _ = h.shape
    nq = RET_HEADS * RET_QK_DIM
    nv = RET_HEADS * RET_V_DIM
    proj = h @ w_in
    q = proj[..., :nq].reshape(bsz, seq, RET_HEADS, RET_QK_DIM)
    k = proj[..., nq:2 * nq].reshape(bsz, seq, RET_HEADS, RET_QK_DIM)
    v = proj[..., 2 * nq:2 * nq + nv].reshape(bsz, seq, RET_HEADS, RET_V_DIM)
    gate = proj[..., 2 * nq + nv:]
    pos = jnp.arange(seq, dtype=jnp.float32)
    q = _rotary(q, pos)
    k = _rotary(k, pos) * (RET_QK_DIM ** -0.5)
    q, k, v = (jnp.swapaxes(t, 1, 2) for t in (q, k, v))
    log_gamma = jax.nn.log_sigmoid(decay_logit.astype(jnp.float32))
    fwd = _retention_causal(q, k, v, log_gamma[0], True)
    bwd = jnp.flip(_retention_causal(jnp.flip(q, 2), jnp.flip(k, 2), jnp.flip(v, 2), log_gamma[1], False), 2)
    o = (fwd + bwd).astype(jnp.float32)
    o = o * lax.rsqrt(jnp.mean(o * o, axis=-1, keepdims=True) + EPS)
    o = jnp.swapaxes(o, 1, 2).reshape(bsz, seq, nv).astype(h.dtype)
    return (jax.nn.silu(gate) * o) @ w_out

def _gmlp_mixer(h, w_in, ln_g, ln_b, w_s, b_s, w_out):
    bsz, seq, _ = h.shape
    n_chunks = seq // GM_CHUNK
    z = jax.nn.gelu(h @ w_in, approximate=False)
    u, v = z[..., :GM_HALF], z[..., GM_HALF:]
    v = _layernorm(v, ln_g, ln_b).reshape(bsz, n_chunks, GM_CHUNK, GM_GROUPS, GM_GROUP_DIM)
    mixed = jnp.einsum('gts,bnsgc->bntgc', w_s, v) + jnp.swapaxes(b_s, 0, 1)[None, None, :, :, None]
    return (u * mixed.reshape(bsz, seq, GM_HALF)) @ w_out

def _neighbourhood_mixer(h, w_qkv, rpb, w_out):
    bsz, seq, _ = h.shape
    rows = seq // GRID_W
    kr = min(NA_WIN_ROWS, rows)
    kc = NA_WIN_COLS
    qkv = (h @ w_qkv).reshape(bsz, rows, GRID_W, 3, NA_HEADS, NA_HEAD_DIM)
    q = qkv[:, :, :, 0] * (NA_HEAD_DIM ** -0.5)
    k = qkv[:, :, :, 1]
    v = qkv[:, :, :, 2]
    col = jnp.arange(GRID_W)
    col_idx = jnp.clip(col - kc // 2, 0, GRID_W - kc)[:, None] + jnp.arange(kc)[None, :]
    rpb_cols = rpb[:, :, col_idx - col[:, None] + kc - 1]

    def row_block(args):
        r, q_row = args
        r0 = jnp.clip(r - kr // 2, 0, rows - kr)
        k_win = lax.dynamic_slice_in_dim(k, r0, kr, axis=1)[:, :, col_idx]
        v_win = lax.dynamic_slice_in_dim(v, r0, kr, axis=1)[:, :, col_idx]
        row_off = r0 + jnp.arange(kr) - r + NA_WIN_ROWS - 1
        bias = jnp.transpose(rpb_cols[:, row_off], (0, 2, 1, 3)).astype(jnp.float32)
        s = jnp.einsum('bqhd,brqchd->bhqrc', q_row, k_win).astype(jnp.float32) + bias[None]
        p = jax.nn.softmax(s.reshape(bsz, NA_HEADS, GRID_W, kr * kc), axis=-1)
        p = p.reshape(bsz, NA_HEADS, GRID_W, kr, kc).astype(v.dtype)
        return jnp.einsum('bhqrc,brqchd->bqhd', p, v_win)

    out = lax.map(row_block, (jnp.arange(rows, dtype=jnp.int32), jnp.moveaxis(q, 1, 0)))
    out = jnp.moveaxis(out, 0, 1).reshape(bsz, seq, D_MODEL)
    return out @ w_out

def _grouped_moe(h, router_w, router_b, w_gate_up, w_down):
    bsz, seq, d = h.shape
    t = h.reshape(bsz * seq, d)
    scores = jax.nn.sigmoid((t @ router_w).astype(jnp.float32))
    biased = scores + router_b.astype(jnp.float32)
    grp_top = lax.top_k(biased.reshape(-1, N_GROUPS, EXPERTS_PER_GROUP), TOP_K)[0]
    grp_sel = jnp.argmax(jnp.sum(grp_top, axis=-1), axis=-1)
    in_grp = (jnp.arange(N_EXPERTS) // EXPERTS_PER_GROUP)[None, :] == grp_sel[:, None]
    _, top_idx = lax.top_k(jnp.where(in_grp, biased, -jnp.inf), TOP_K)
    sel = jnp.take_along_axis(scores, top_idx, axis=-1)
    w = sel / jnp.sum(sel, axis=-1, keepdims=True)
    gates = jnp.sum(jax.nn.one_hot(top_idx, N_EXPERTS, dtype=jnp.float32) * w[..., None], axis=1).astype(t.dtype)
    y = jnp.zeros_like(t)
    for e in range(N_EXPERTS):
        gu = t @ w_gate_up[e]
        hid = jax.nn.silu(gu[:, :D_EXPERT]) * gu[:, D_EXPERT:]
        y = y + gates[:, e:e + 1] * (hid @ w_down[e])
    return y.reshape(bsz, seq, d)

def setup_inputs(seed: int = 0) -> dict:
    key = jax.random.key(seed)
    ks = jax.random.split(key, 24)
    f32 = jnp.float32
    n_ret = len(range(0, DEPTH, N_MIXERS))
    n_gm = len(range(1, DEPTH, N_MIXERS))
    n_na = len(range(2, DEPTH, N_MIXERS))

    def nrm(k, shape, scale):
        return jax.random.normal(k, shape, f32) * scale

    base_logit = np.log(2.0 ** (5.0 + np.arange(RET_HEADS)) - 1.0).astype(np.float32)
    return {
        'x': nrm(ks[0], (BATCH, SEQ, D_MODEL), 1.0),
        'c': nrm(ks[1], (BATCH, D_MODEL), 1.0),
        'norm_g': 1.0 + nrm(ks[2], (DEPTH, 2, D_MODEL), 0.02),
        'final_g': 1.0 + nrm(ks[3], (D_MODEL,), 0.02),
        'w_ada': nrm(ks[4], (DEPTH, D_MODEL, 6 * D_MODEL), 0.5 * D_MODEL ** -0.5),
        'b_ada': nrm(ks[5], (DEPTH, 6 * D_MODEL), 0.02),
        'ret_w_in': nrm(ks[6], (n_ret, D_MODEL, RET_IN), D_MODEL ** -0.5),
        'ret_decay_logit': jnp.asarray(base_logit)[None, None, :] + nrm(ks[7], (n_ret, 2, RET_HEADS), 0.1),
        'ret_w_out': nrm(ks[8], (n_ret, RET_HEADS * RET_V_DIM, D_MODEL), (RET_HEADS * RET_V_DIM) ** -0.5),
        'gm_w_in': nrm(ks[9], (n_gm, D_MODEL, GM_FFN), D_MODEL ** -0.5),
        'gm_ln_g': 1.0 + nrm(ks[10], (n_gm, GM_HALF), 0.02),
        'gm_ln_b': nrm(ks[11], (n_gm, GM_HALF), 0.02),
        'gm_w_s': nrm(ks[12], (n_gm, GM_GROUPS, GM_CHUNK, GM_CHUNK), GM_CHUNK ** -0.5),
        'gm_b_s': 1.0 + nrm(ks[13], (n_gm, GM_GROUPS, GM_CHUNK), 0.1),
        'gm_w_out': nrm(ks[14], (n_gm, GM_HALF, D_MODEL), GM_HALF ** -0.5),
        'na_w_qkv': nrm(ks[15], (n_na, D_MODEL, 3 * D_MODEL), D_MODEL ** -0.5),
        'na_rpb': nrm(ks[16], (n_na, NA_HEADS, 2 * NA_WIN_ROWS - 1, 2 * NA_WIN_COLS - 1), 0.05),
        'na_w_out': nrm(ks[17], (n_na, D_MODEL, D_MODEL), D_MODEL ** -0.5),
        'router_w': nrm(ks[18], (D_MODEL, N_EXPERTS), D_MODEL ** -0.5),
        'router_b': nrm(ks[19], (N_EXPERTS,), 0.01),
        'moe_w_gate_up': nrm(ks[20], (DEPTH, N_EXPERTS, D_MODEL, 2 * D_EXPERT), D_MODEL ** -0.5),
        'moe_w_down': nrm(ks[21], (DEPTH, N_EXPERTS, D_EXPERT, D_MODEL), D_EXPERT ** -0.5),
    }

def reference(x, c, norm_g, final_g, w_ada, b_ada, ret_w_in, ret_decay_logit, ret_w_out,
              gm_w_in, gm_ln_g, gm_ln_b, gm_w_s, gm_b_s, gm_w_out, na_w_qkv, na_rpb, na_w_out,
              router_w, router_b, moe_w_gate_up, moe_w_down):
    c_act = jax.nn.silu(c)
    for i in range(DEPTH):
        kind, j = i % N_MIXERS, i // N_MIXERS
        mod = c_act @ w_ada[i] + b_ada[i]
        sh1, sc1, g1, sh2, sc2, g2 = [m[:, None, :] for m in jnp.split(mod, 6, axis=-1)]
        h = _rmsnorm(x, norm_g[i, 0]) * (1 + sc1) + sh1
        if kind == 0:
            y = _retention_mixer(h, ret_w_in[j], ret_decay_logit[j], ret_w_out[j])
        elif kind == 1:
            y = _gmlp_mixer(h, gm_w_in[j], gm_ln_g[j], gm_ln_b[j], gm_w_s[j], gm_b_s[j], gm_w_out[j])
        else:
            y = _neighbourhood_mixer(h, na_w_qkv[j], na_rpb[j], na_w_out[j])
        x = x + g1 * y
        h = _rmsnorm(x, norm_g[i, 1]) * (1 + sc2) + sh2
        x = x + g2 * _grouped_moe(h, router_w, router_b, moe_w_gate_up[i], moe_w_down[i])
    return _rmsnorm(x, final_g)


_drawn_inputs = setup_inputs


def setup_inputs(seed=0):
    import zlib

    import numpy as np

    out = dict(_drawn_inputs(seed))
    spreads = {}
    factors = {}
    for name, (base, spread) in spreads.items():
        noise = np.random.default_rng([zlib.crc32(name.encode()), seed]).standard_normal(out[name].shape)
        drawn = base * np.exp(spread * noise) if base else spread * noise
        out[name] = __import__('jax').numpy.asarray(drawn.astype(out[name].dtype))
    for name, factor in factors.items():
        out[name] = (out[name] * factor).astype(out[name].dtype)
    return out
```

```python
from contextlib import ExitStack

import concourse.bass as bass
from concourse import mybir

F32 = mybir.dt.float32
F32R = mybir.dt.float32r
I32 = mybir.dt.int32
ALU = mybir.AluOpType
ACT = mybir.ActivationFunctionType
AX_X = mybir.AxisListType.X

P = 128
D = 1024
SEQ = 256
TT = SEQ // P
KC = D // P
EPS = 1e-6
HEADS = 4
V_DIM = 512
QK_SCALE = (D // HEADS) ** -0.5
GM_HALF = 3072
GM_GROUPS = 4
GROUPS = 4
PER_GROUP = 4
N_EXPERTS = GROUPS * PER_GROUP
D_EXPERT = 512

COLS = 1024
GRAN = 2 * COLS
RING = 6
SPLIT = 3
LEAD = SPLIT - 1
MOE_GRAN = 6 * PER_GROUP
MOE_ORDER = ([(0, "up", j) for j in range(4)] + [(1, "up", j) for j in range(4)] + [(0, "down", j) for j in range(2)]
             + [(2, "up", j) for j in range(4)] + [(1, "down", j) for j in range(2)]
             + [(3, "up", j) for j in range(4)] + [(2, "down", j) for j in range(2)]
             + [(3, "down", j) for j in range(2)])

SMALL = {}
_at = 0
for _name, _n in (("c", KC), ("b_ada", 2 * 6 * KC), ("norm_g", 2 * 2 * KC), ("router_w", KC * N_EXPERTS),
                  ("router_b", N_EXPERTS), ("decay", 2 * HEADS), ("ln_g", GM_HALF // P), ("ln_b", GM_HALF // P)):
    SMALL[_name] = (_at, _n)
    _at += _n
SMALL_N = _at


def stream_plan():
    plan = [("ada", job, kp) for job in (0, 1) for kp in range(4)]
    m = 0

    def dense(n, jobs=()):
        nonlocal m
        parts = [("ada", job, kp) for job in jobs for kp in range(4)]
        for i in range(n):
            if i < len(parts):
                plan.append(parts[i])
            plan.append(("dense", m))
            m += 1
        assert len(parts) <= n

    dense(24, (2, 3, 4, 5, 6, 7))
    dense(8, (8, 9))
    dense(4 * MOE_GRAN)
    dense(4)
    dense(8, (10, 11))
    dense(3 * 8)
    dense(4 * MOE_GRAN)
    dense(LEAD)
    return plan


PLAN = stream_plan()
N_GRAN = len(PLAN)
N_OF = {p[1]: n for n, p in enumerate(PLAN) if p[0] == "dense"}
ADA_OF = {(p[1], p[2]): n for n, p in enumerate(PLAN) if p[0] == "ada"}
ADA_WITH = {p[1]: PLAN[n - 1][1:] for n, p in enumerate(PLAN) if p[0] == "dense" and PLAN[n - 1][0] == "ada" and p[1] > 0}
ADA_WITH[0] = PLAN[N_OF[0] - 1][1:]

M_RET_OUT = 24
M_MOE = (32, 32 + 96 + 36)
M_GM = 32 + 96
assert MOE_GRAN % RING == 0 and MOE_GRAN % SPLIT == 0

SH1, SC1, G1, SH2, SC2, G2 = range(6)
JOBS = [(0, SH1), (0, SC1), (0, G1), (0, SH2), (0, SC2), (0, G2), (1, SH1), (1, SC1), (1, G1), (1, SH2), (1, SC2), (1, G2)]
GATE_ROW = {(0, G1): 0, (0, G2): 1, (1, G1): 2, (1, G2): 0}
FINAL_ROW = 1


def trunk_kernel(nc: bass.Bass, stream: bass.AP, x_in: bass.AP, small_in: bass.AP, const_in: bass.AP, decay_in: bass.AP,
                 gate_bias: bass.AP, final_g: bass.AP, mix_w: bass.AP, mix_b: bass.AP, out: bass.AP):
    with ExitStack() as ctx:
        def sb(name, shape, dt=F32):
            return ctx.enter_context(nc.sbuf_tensor(name, shape, dt))

        def sem(name):
            return ctx.enter_context(nc.semaphore(name))

        ring = sb("ring", [P, RING, 2, COLS])
        w_high = sb("w_high", [P, SPLIT, 2, COLS], F32R)
        w_low = sb("w_low", [P, SPLIT, 2, COLS], F32R)
        ada_acc = sb("ada_acc", [P, 2, COLS])
        x = sb("x", [P, TT, D])
        xn = sb("xn", [P, TT, D])
        h_high = sb("h_high", [P, KC, SEQ], F32R)
        h_low = sb("h_low", [P, KC, SEQ], F32R)
        piece_high = sb("piece_high", [P, 2, 512], F32R)
        piece_low = sb("piece_low", [P, 2, 512], F32R)
        rows = sb("rows", [P, 3, D])
        small = sb("small", [P, SMALL_N])
        const = sb("const", [P, 3 * P + 2 * SEQ])
        scratch = sb("scratch", [P, 2, 512])
        sel = sb("sel", [P, TT, P])
        sel_t = sb("sel_t", [P, SEQ])
        area = sb("area", [P, 8192])
        ones = sb("ones", [P, P])
        mod = sb("mod", [P, 2, 4, KC])
        c_act = sb("c_act", [P, KC])
        eps = sb("eps", [P, 1])
        ssq = sb("ssq", [P, 8])
        std = sb("std", [P, 8])
        rstd = sb("rstd", [P, 8])
        lg = sb("lg", [P, 6, 2 * HEADS])
        bn = sb("bn", [P, TT, 6, 6])
        mean_var = sb("mean_var", [P, TT, 2])
        rt = sb("rt", [P, 16, TT * N_EXPERTS])
        own_gates = sb("own_gates", [P, TT, PER_GROUP])
        slot_of = sb("slot_of", [P, TT, GROUPS + 1])
        slot_gates = sb("slot_gates", [P, PER_GROUP])
        over_f = sb("over_f", [P, 16])
        over_i = sb("over_i", [1, 2], I32)
        done_mark = sb("done_mark", [P, 4])

        ps = ctx.enter_context(nc.psum_tensor("ps", [P, 8, 512], F32))

        ident, upper, iota = (const[:, i * P:(i + 1) * P] for i in range(3))
        cos, sin = (const[:, 3 * P + i * SEQ:3 * P + (i + 1) * SEQ] for i in range(2))

        def small_of(name):
            a, n = SMALL[name]
            return small[:, a:a + n]

        b_ada = small_of("b_ada").rearrange("p (l w k) -> p l w k", l=2, w=6)
        norm_g = small_of("norm_g").rearrange("p (l w k) -> p l w k", l=2, w=2)
        router_w = small_of("router_w").rearrange("p (k e) -> p k e", k=KC)
        router_b = small_of("router_b")
        decay_logit = small_of("decay")
        ln_g, ln_b = small_of("ln_g"), small_of("ln_b")
        qk = area[:, 0:4096].rearrange("p (w h c n) -> p w h c n", w=2, h=HEADS, c=2)
        ret_g = area[:, 0:4096].rearrange("p (t n) -> p t n", t=TT)
        v = area[:, 4096:8192].rearrange("p (t n) -> p t n", t=TT)
        dist = area[:, 4096:5120].rearrange("p (w n) -> p w n", w=2)
        rot = area[:, 5120:7168].rearrange("p (b w n) -> p b w n", b=2, w=2)
        h_ret = area[:, 5120:7168].rearrange("p (k n) -> p k n", k=KC)
        prob = xn[:, :, :].rearrange("p t n -> p (t n)").rearrange("p (h n) -> p h n", h=HEADS)
        h_all = area[:, 0:2048].rearrange("p (k n) -> p k n", k=KC)
        gv = area[:, 0:6144].rearrange("p (t n) -> p t n", t=TT)
        mix_ws = area[:, 6144:6656].rearrange("p (g n) -> p g n", g=GM_GROUPS)
        mix_bs = area[:, 6656:7168].rearrange("p (g n) -> p g n", g=GM_GROUPS)
        mix_rows = area[:, 7168:7680].rearrange("p (g n) -> p g n", g=GM_GROUPS)
        mix_add = area[:, 7680:8192].rearrange("p (b n) -> p b n", b=2)
        u_t = xn[:, :, :].rearrange("p t n -> p (t n)").rearrange("p (k n) -> p k n", k=KC)
        gathered = area[:, 2048:3072].rearrange("p (k n) -> p k n", k=KC)
        y_slots = area[:, 3072:4096]
        hid = area[:, 4096:5120].rearrange("p (b n) -> p b n", b=2)
        over_w = area[:, 6144:8192].rearrange("p (k n) -> p k n", k=2)

        landed = [sem(f"landed{i}") for i in range(RING)]
        x_in_s, small_s, const_s, decay_s = sem("x_landed"), sem("small_landed"), sem("const_landed"), sem("decay_landed")
        row_s = [sem(f"row_landed{i}") for i in range(5)]
        mix_s = sem("mix_landed")
        high_ready, low_ready = sem("high_ready"), sem("low_ready")
        w_used = sem("w_used")
        ada_dve, ada_pool, ada_scaled = sem("ada_dve"), sem("ada_pool"), sem("ada_scaled")
        set_up, c_ready = sem("set_up"), sem("c_ready")
        mod_summed, mod_stored = sem("mod_summed"), sem("mod_stored")
        squares_done, std_ready, rstd_ready, xn_ready = sem("squares_done"), sem("std_ready"), sem("rstd_ready"), sem("xn_ready")
        xn_turned, h_act, h_dve, h_high_s, h_low_s = sem("xn_turned"), sem("h_act"), sem("h_dve"), sem("h_high_s"), sem("h_low_s")
        x_ready = sem("x_ready")
        group_act, group_dve = sem("group_act"), sem("group_dve")
        dve_chain, act_chain, pool_chain = sem("dve_chain"), sem("act_chain"), sem("pool_chain")
        rot_ready, rot_done = sem("rot_ready"), sem("rot_done")
        lg_ready, dist_ready, decay_ready = sem("lg_ready"), sem("dist_ready"), sem("decay_ready")
        scores_done, prob_ready = sem("scores_done"), sem("prob_ready")
        o_done, o_squares, o_std, o_rstd, o_gated = sem("o_done"), sem("o_squares"), sem("o_std"), sem("o_rstd"), sem("o_gated")
        turned, piece_high_s, piece_low_s = sem("turned"), sem("piece_high_s"), sem("piece_low_s")
        ln_std, ln_rstd, gv_ready = sem("ln_std"), sem("ln_rstd"), sem("gv_ready")
        mixed_done, mix_rows_done, mix_rows_s, mix_add_s = sem("mixed_done"), sem("mix_rows_done"), sem("mix_rows_s"), sem("mix_add_s")
        mix_scaled = sem("mix_scaled")
        z_ready = sem("z_ready")
        logits_done, scores_ready, place_done, route_ready = sem("logits_done"), sem("scores_ready"), sem("place_done"), sem("route_ready")
        members_ready, over_counted, over_known = sem("members_ready"), sem("over_counted"), sem("over_known")
        sel_ready, sel_turned, sel_t_s = sem("sel_ready"), sem("sel_turned"), sem("sel_t_s")
        gather_done, gathered_act, gathered_dve, hg_high, hg_low = sem("gather_done"), sem("gathered_act"), sem("gathered_dve"), sem("hg_high"), sem("hg_low")
        silu_done, hid_ready = sem("silu_done"), sem("hid_ready")
        hid_turned, hid_high, hid_low = sem("hid_turned"), sem("hid_high"), sem("hid_low")
        y_act, y_dve = sem("y_act"), sem("y_dve")
        scattered, scatter_term, banks_free = sem("scattered"), sem("scatter_term"), sem("banks_free")
        ov = [{n: sem(f"over{layer}_{n}") for n in ("w", "used", "silu", "hid", "turned", "t_act", "y", "sel_turned",
                                                    "sel_t", "scattered", "term")} for layer in range(2)]
        out_ready, stored = sem("out_ready"), sem("stored")

        block = ctx.enter_context(nc.Block())

        def wait_landed(eng, n, loops=0):
            eng.wait_ge(landed[n % RING], loops * (16 * MOE_GRAN // RING) + 16 * (n // RING + 1))

        def split_high(act, m, loops=0):
            n = N_OF[m]
            wait_landed(act, n, loops)
            if m >= SPLIT:
                act.wait_ge(w_used, loops * MOE_GRAN + m - SPLIT + 1)
            act.copy(w_high[:, m % SPLIT], ring[:, n % RING]).then_inc(high_ready, 1)

        def split_low(dve, m, loops=0):
            n = N_OF[m]
            dve.wait_ge(high_ready, loops * MOE_GRAN + m + 1)
            dve.tensor_tensor(w_low[:, m % SPLIT], ring[:, n % RING], w_high[:, m % SPLIT].bitcast(F32),
                              ALU.subtract).then_inc(low_ready, 1)

        @block.sync
        def _(sp):
            def free_slot(n):
                if n < RING:
                    return
                kind = PLAN[n - RING]
                if kind[0] == "dense":
                    sp.wait_ge(low_ready, kind[1] + 1)
                else:
                    sp.wait_ge(ada_dve, 4 * kind[1] + kind[2] + 1)
                    sp.wait_ge(ada_scaled, 4 * kind[1] + kind[2] + 1)
                    if kind[2]:
                        sp.wait_ge(ada_pool, 3 * kind[1] + kind[2])

            def load(n):
                free_slot(n)
                sp.dma_start(ring[:, n % RING].rearrange("p k n -> p (k n)"), stream[n]).then_inc(landed[n % RING], 16)

            def load_groups(first, m0, groups):
                with sp.Fori(0, groups) as g:
                    for j in range(MOE_GRAN):
                        sp.wait_ge(low_ready, g * MOE_GRAN + (m0 + j + 1))
                        sp.dma_start(ring[:, (first + j) % RING].rearrange("p k n -> p (k n)"),
                                     stream[g * MOE_GRAN + (first + j)]).then_inc(landed[(first + j) % RING], 16)
                return first + MOE_GRAN * groups

            sp.dma_start(small[:, :], small_in).then_inc(small_s, 16)
            load(0)
            sp.dma_start(x[:, :, :], x_in.rearrange("(t p) n -> p t n", p=P)).then_inc(x_in_s, 16)
            for n in range(1, 4):
                load(n)
            sp.dma_start(const[:, :], const_in).then_inc(const_s, 16)
            sp.dma_start(area[:, 4096:5120], decay_in).then_inc(decay_s, 16)
            for i, key in enumerate([(0, G1), (0, G2), (1, G1)]):
                sp.dma_start(rows[:, GATE_ROW[key], :], gate_bias[i:i + 1, :].to_broadcast([P, D])).then_inc(row_s[i], 16)
            n = 4
            while n < N_OF[M_MOE[0]] + RING:
                load(n)
                n += 1
            n = load_groups(n, M_MOE[0], GROUPS)
            sp.wait_ge(x_ready, 1)
            sp.dma_start(rows[:, GATE_ROW[1, G2], :], gate_bias[3:4, :].to_broadcast([P, D])).then_inc(row_s[3], 16)
            while n < N_OF[M_GM + 4]:
                load(n)
                n += 1
            sp.wait_ge(x_ready, 2)
            sp.dma_start(rows[:, FINAL_ROW, :], final_g.to_broadcast([P, D])).then_inc(row_s[4], 16)
            sp.dma_start(area[:, 6144:6656], mix_w).then_inc(mix_s, 16)
            sp.dma_start(area[:, 6656:7168], mix_b).then_inc(mix_s, 16)
            while n < N_OF[M_MOE[1]] + RING:
                load(n)
                n += 1
            n = load_groups(n, M_MOE[1], GROUPS - 1)
            while n < N_GRAN:
                load(n)
                n += 1
            for t in range(TT):
                sp.wait_ge(out_ready, t + 1)
                sp.dma_start(out[t * P:(t + 1) * P, :], xn[:, t, :]).then_inc(stored, 16)
            sp.wait_ge(stored, 16 * TT)

        @block.tensor
        def _(pe):
            def sum_mod(job, bank):
                pe.wait_ge(ada_dve, 4 * job + 4)
                pe.wait_ge(ada_pool, 3 * job + 3)
                if JOBS[job] in GATE_ROW:
                    for h in range(2):
                        for part in range(2):
                            last = pe.matmul(ps[:, bank + h, :], ones[:, :], ada_acc[:, part, h * 512:(h + 1) * 512],
                                             start=(part == 0), stop=(part == 1))
                else:
                    for k in range(KC):
                        for part in range(2):
                            last = pe.matmul(ps[:, bank, k:k + 1], ada_acc[:, part, k * P:(k + 1) * P], ones[:, 0:1],
                                             start=(part == 0), stop=(part == 1))
                last.then_inc(mod_summed, 1)

            def turn_xn(stage):
                pe.wait_ge(xn_ready, 2 * stage + 2)
                for k in range(KC):
                    for t in range(TT):
                        last = pe.transpose(ps[:, k // 2, (k % 2) * SEQ + t * P:(k % 2) * SEQ + (t + 1) * P],
                                            xn[:, t, k * P:(k + 1) * P], ident)
                    if k % 2:
                        last.then_inc(xn_turned, 1)

            def dense_rows(m, act_high, act_low, bank, first, last_one, loops=0):
                tiles = TT if bank < 8 else 1
                pe.wait_ge(low_ready, loops * MOE_GRAN + m + 1)
                for kc in range(2):
                    for t in range(tiles):
                        for a, w in ((act_high(kc, t), w_high), (act_high(kc, t), w_low), (act_low(kc, t), w_high)):
                            for h in range(2):
                                ins = pe.matmul(ps[:, bank + 2 * t + h, :], a, w[:, m % SPLIT, kc, h * 512:(h + 1) * 512],
                                                start=(first and kc == 0 and w is w_high and a is not None and not started[t, h]),
                                                stop=False, skip_group_check=True)
                                started[t, h] = True
                return ins

            started = {}

            def begin():
                for t in range(TT):
                    for h in range(2):
                        started[t, h] = False

            def dense_cols(m, bank, first):
                k0 = 2 * (m % 4)
                pe.wait_ge(low_ready, m + 1)
                for kc in range(2):
                    for cc in range(8):
                        for i, (w, a) in enumerate(((w_high, h_high), (w_high, h_low), (w_low, h_high))):
                            ins = pe.matmul(ps[:, bank + cc // 2, (cc % 2) * SEQ:(cc % 2 + 1) * SEQ],
                                            w[:, m % SPLIT, kc, cc * P:(cc + 1) * P], a[:, k0 + kc, :],
                                            start=(first and kc == 0 and i == 0 and cc % 2 == 0), stop=False,
                                            skip_group_check=True)
                return ins

            def rows_of_h(m):
                k0 = 2 * (m % 4)
                return (lambda kc, t: h_high[:, k0 + kc, t * P:(t + 1) * P]), (lambda kc, t: h_low[:, k0 + kc, t * P:(t + 1) * P])

            def rows_of_piece(b):
                return ((lambda kc, t: piece_high[:, b, kc * SEQ + t * P:kc * SEQ + (t + 1) * P]),
                        (lambda kc, t: piece_low[:, b, kc * SEQ + t * P:kc * SEQ + (t + 1) * P]))

            pe.wait_ge(set_up, 1)
            sum_mod(0, 4)
            sum_mod(1, 5)
            pe.wait_ge(const_s, 16)
            turn_xn(0)

            pe.wait_ge(h_low_s, 1)
            pe.wait_ge(mod_stored, 2)
            for i in range(6):
                bank = 4 * (i % 2)
                if i >= 1:
                    pe.wait_ge(mod_stored, i + 2)
                if i >= 2:
                    pe.wait_ge(group_act, i - 1)
                    pe.wait_ge(group_dve, i - 1)
                if i in (3, 4):
                    pe.wait_ge(prob_ready, 2 * (i - 2))
                begin()
                for j in range(4):
                    m = 4 * i + j
                    if j == 3:
                        if i >= 1:
                            pe.wait_ge(group_act, i)
                            pe.wait_ge(group_dve, i)
                        sum_mod(2 + i, 4 - bank)
                        if i in (2, 3):
                            if i == 2:
                                pe.wait_ge(rot_done, 2 * HEADS)
                            for h in (2 * (i - 2), 2 * (i - 2) + 1):
                                for jt in range(TT):
                                    for c in range(2):
                                        last = pe.matmul(ps[:, 4 - bank + 2 + h % 2, jt * SEQ:(jt + 1) * SEQ],
                                                         qk[:, 1, h, c, jt * P:(jt + 1) * P], qk[:, 0, h, c, :],
                                                         start=(c == 0), stop=(c == 1))
                                last.then_inc(scores_done, 1)
                    if i < 2:
                        last = dense_cols(m, bank, j == 0)
                    else:
                        last = dense_rows(m, *rows_of_h(m), bank, True, j == 3)
                    last.then_inc(w_used, 1)

            for h in range(HEADS):
                pe.wait_ge(prob_ready, h + 1)
                if h == 0:
                    pe.wait_ge(group_act, 5)
                    pe.wait_ge(group_dve, 5)
                    pe.wait_ge(mod_stored, 8)
                if h == 2:
                    pe.wait_ge(group_act, 6)
                    pe.wait_ge(group_dve, 6)
                for t in range(TT):
                    for jt in range(TT):
                        last = pe.matmul(ps[:, 2 * h + t, :], prob[:, h, jt * SEQ + t * P:jt * SEQ + (t + 1) * P],
                                         v[:, jt, h * V_DIM:(h + 1) * V_DIM], start=(jt == 0), stop=(jt == 1))
                last.then_inc(o_done, 1)

            def turn_gated(kp):
                for c in range(2):
                    for t in range(TT):
                        last = pe.transpose(ps[:, 4 + kp % 2, c * SEQ + t * P:c * SEQ + (t + 1) * P],
                                            ret_g[:, t, (2 * kp + c) * P:(2 * kp + c + 1) * P], ident)
                last.then_inc(turned, 1)

            pe.wait_ge(o_gated, 2 * HEADS)
            turn_gated(0)
            turn_gated(1)
            begin()
            for kp in range(8):
                m = M_RET_OUT + kp
                if kp % 4 == 3:
                    if kp == 7:
                        pe.wait_ge(mod_stored, 9)
                    sum_mod(8 + kp // 4, 6)
                pe.wait_ge(piece_low_s, kp + 1)
                dense_rows(m, *rows_of_piece(kp % 2), 0, True, kp == 7).then_inc(w_used, 1)
                if kp + 2 < 8:
                    turn_gated(kp + 2)

            def gather(layer, g, g_next):
                pe.wait_ge(sel_ready, g + (5 * layer + 1))
                for k in range(KC):
                    for t in range(TT):
                        pe.matmul(ps[:, k // 4, (k % 4) * P:(k % 4 + 1) * P], xn[:, t, k * P:(k + 1) * P], sel[:, t, :],
                                  start=(t == 0), stop=(t == 1))
                for t in range(TT):
                    last = pe.matmul(ps[:, 2, 0:PER_GROUP], sel[:, t, :], own_gates[:, t, :], start=(t == 0), stop=(t == 1))
                last.then_inc(gather_done, 1)

            def experts(layer):
                m0 = M_MOE[layer]
                stage = 2 * layer + 1
                turn_xn(stage)
                pe.wait_ge(h_act, stage + 1)
                pe.wait_ge(h_dve, stage + 1)
                for t in range(TT):
                    for k in range(KC):
                        last = pe.matmul(ps[:, 4, t * N_EXPERTS:(t + 1) * N_EXPERTS], h_all[:, k, t * P:(t + 1) * P],
                                         router_w[:, k, :], start=(k == 0), stop=(k == KC - 1))
                last.then_inc(logits_done, 1)
                pe.wait_ge(members_ready, layer + 1)
                members = rt[:, 0, 0:TT * GROUPS]
                pe.matmul(ps[:, 5, 0:GROUPS], upper, members[:, 0:GROUPS], start=True, stop=True)
                pe.matmul(ps[:, 5, GROUPS:2 * GROUPS], upper, members[:, GROUPS:], start=True, stop=False)
                pe.matmul(ps[:, 5, GROUPS:2 * GROUPS], ones[:, :], members[:, 0:GROUPS], start=False, stop=True)\
                    .then_inc(place_done, 1)
                pe.wait_ge(route_ready, layer + 1)
                for t in range(TT):
                    last = pe.matmul(ps[:, 6, 0:GROUPS], ones[:, :], rt[:, 1, t * GROUPS:(t + 1) * GROUPS],
                                     start=(t == 0), stop=(t == 1))
                last.then_inc(over_counted, 1)
                gather(layer, 0, 0)

                with pe.Fori(0, GROUPS) as g:
                    grp = lambda base: g + base
                    began = {}

                    def up(e, j, s):
                        m = m0 + s
                        pe.wait_ge(low_ready, g * MOE_GRAN + (m + 1))
                        for kc in range(2):
                            k = 2 * j + kc
                            for i, (a, w) in enumerate(((h_high, w_high), (h_high, w_low), (h_low, w_high))):
                                for h in range(2):
                                    last = pe.matmul(ps[:, 2 * (e % 2) + h, :], a[:, k, 0:P],
                                                     w[:, m % SPLIT, kc, h * 512:(h + 1) * 512],
                                                     start=(k == 0 and i == 0), stop=(k == KC - 1 and i == 2))
                        last.then_inc(w_used, 1)

                    def turn_hid(e):
                        pe.wait_ge(hid_ready, g * PER_GROUP + (N_EXPERTS * layer + e + 1))
                        for f in range(4):
                            last = pe.transpose(ps[:, 6, f * P:(f + 1) * P], hid[:, e % 2, f * P:(f + 1) * P], ident)
                        last.then_inc(hid_turned, 1)

                    def down(e, j, s):
                        m = m0 + s
                        if j == 0:
                            pe.wait_ge(hid_low, g * PER_GROUP + (N_EXPERTS * layer + e + 1))
                        pe.wait_ge(low_ready, g * MOE_GRAN + (m + 1))
                        for kc in range(2):
                            f = 2 * j + kc
                            for i, (a, w) in enumerate(((piece_high, w_high), (piece_high, w_low), (piece_low, w_high))):
                                for h in range(2):
                                    last = pe.matmul(ps[:, 4 + h, :], a[:, e % 2, f * P:(f + 1) * P],
                                                     w[:, m % SPLIT, kc, h * 512:(h + 1) * 512],
                                                     start=(e == 0 and f == 0 and i == 0), stop=(e == 3 and f == 3 and i == 2))
                        last.then_inc(w_used, 1)

                    for s, (e, kind, j) in enumerate(MOE_ORDER):
                        if kind == "up":
                            if s == 0:
                                pe.wait_ge(hg_low, grp(5 * layer + 1))
                            if s == 4:
                                pe.wait_ge(banks_free, grp(5 * layer + 1))
                            up(e, j, s)
                        else:
                            down(e, j, s)
                        if s == 4:
                            turn_hid(0)
                            for t in range(TT):
                                last = pe.transpose(ps[:, 7, t * P:(t + 1) * P], sel[:, t, :], ident)
                            last.then_inc(sel_turned, 1)
                        elif s in (10, 16, 20):
                            turn_hid({10: 1, 16: 2, 20: 3}[s])
                        if s == 21:
                            gather(layer, g + 1, None)
                    pe.wait_ge(y_act, grp(GROUPS * layer + 1))
                    pe.wait_ge(y_dve, grp(GROUPS * layer + 1))
                    pe.wait_ge(sel_t_s, grp(GROUPS * layer + 1))
                    pe.wait_ge(hg_low, grp(5 * layer + 2))
                    for i, bank in enumerate((6, 7, 2, 3)):
                        pe.matmul(ps[:, bank, :], sel_t[:, (i // 2) * P:(i // 2 + 1) * P], y_slots[:, (i % 2) * 512:(i % 2 + 1) * 512],
                                  start=True, stop=True).then_inc(scattered, 1)

                o = ov[layer]
                pe.wait_ge(over_known, layer + 1)
                flag = pe.value_load(over_i[0:1, 0:1], min_val=0, max_val=1)
                pe.wait_ge(banks_free, 5 * (layer + 1))
                with pe.If(flag > 0):
                    n_w = 0
                    for e in range(PER_GROUP):
                        for j in range(4):
                            n_w += 1
                            pe.wait_ge(o["w"], 16 * n_w)
                            for kc in range(2):
                                k = 2 * j + kc
                                for h in range(2):
                                    last = pe.matmul(ps[:, h, :], gathered[:, k, :], over_w[:, kc, h * 512:(h + 1) * 512],
                                                     start=(k == 0), stop=(k == KC - 1))
                            last.then_inc(o["used"], 1)
                        pe.wait_ge(o["hid"], e + 1)
                        for f in range(4):
                            last = pe.transpose(ps[:, 6, f * P:(f + 1) * P], hid[:, 0, f * P:(f + 1) * P], ident)
                        last.then_inc(o["turned"], 1)
                        pe.wait_ge(o["t_act"], e + 1)
                        for j in range(2):
                            n_w += 1
                            pe.wait_ge(o["w"], 16 * n_w)
                            for kc in range(2):
                                f = 2 * j + kc
                                for h in range(2):
                                    last = pe.matmul(ps[:, 4 + h, :], hid[:, 1, f * P:(f + 1) * P], over_w[:, kc, h * 512:(h + 1) * 512],
                                                     start=(e == 0 and f == 0), stop=(e == 3 and f == 3))
                            last.then_inc(o["used"], 1)
                    for t in range(TT):
                        last = pe.transpose(ps[:, 7, t * P:(t + 1) * P], sel[:, t, :], ident)
                    last.then_inc(o["sel_turned"], 1)
                    pe.wait_ge(o["y"], 2)
                    pe.wait_ge(o["sel_t"], 1)
                    for i, bank in enumerate((6, 7, 2, 3)):
                        pe.matmul(ps[:, bank, :], sel_t[:, (i // 2) * P:(i // 2 + 1) * P], y_slots[:, (i % 2) * 512:(i % 2 + 1) * 512],
                                  start=True, stop=True).then_inc(o["scattered"], 1)

            experts(0)

            turn_xn(2)
            pe.wait_ge(h_low_s, 2)
            for i in range(3):
                bank = 4 * (i % 2)
                if i == 2:
                    pe.wait_ge(group_act, 7)
                    pe.wait_ge(mod_stored, 11)
                begin()
                for j in range(4):
                    m = M_GM + 4 * i + j
                    if j == 3 and i >= 1:
                        pe.wait_ge(group_act, 6 + i)
                        sum_mod(9 + i, 4 - bank)
                    dense_rows(m, *rows_of_h(m), bank, True, j == 3).then_inc(w_used, 1)
            pe.wait_ge(mod_stored, 12)
            pe.wait_ge(mix_s, 32)
            for g in range(GM_GROUPS):
                last = pe.matmul(ps[:, 4, g * P:(g + 1) * P], ones[:, :], mix_ws[:, g, :], start=True, stop=True)
            last.then_inc(mix_rows_done, 1)
            pe.wait_ge(mix_rows_s, 1)
            for i in range(3):
                for j in range(4):
                    m = M_GM + 12 + 8 * i + j
                    if i >= 1 and j == 0:
                        pe.wait_ge(z_ready, 8 * i)
                    dense_cols(m, 4, j == 0).then_inc(w_used, 1)
                pe.wait_ge(gv_ready, 2)
                for b in range(4):
                    pe.wait_ge(group_act, 4 * i + b + 10)
                    for c in (2 * b, 2 * b + 1):
                        ch = 8 * i + c
                        for t in range(TT):
                            last = pe.matmul(ps[:, 4 + b, (c % 2) * SEQ + t * P:(c % 2) * SEQ + (t + 1) * P],
                                             gv[:, t, ch * P:(ch + 1) * P], mix_ws[:, ch * P // (GM_HALF // GM_GROUPS), :],
                                             start=True, stop=True)
                    last.then_inc(mixed_done, 1)
                if i == 0:
                    pe.wait_ge(group_act, 9)
                    begin()
                for kp in range(4):
                    m = M_GM + 12 + 8 * i + 4 + kp
                    pe.wait_ge(piece_low_s, 8 + 4 * i + kp + 1)
                    dense_rows(m, *rows_of_piece(kp % 2), 0, True, False).then_inc(w_used, 1)

            experts(1)

        @block.scalar
        def _(act):
            chain = [0]

            def square_and_root(stage):
                for t in range(TT):
                    act.activation(xn[:, t, :], x[:, t, :], ACT.Square, accum_out=ssq[:, t:t + 1]).then_inc(squares_done, 1)
                act.wait_ge(squares_done, 2 * stage + 2)
                act.activation(std[:, 0:TT], ssq[:, 0:TT], ACT.Sqrt, scale=1.0 / D, bias=eps[:, :]).then_inc(std_ready, 1)

            def h_of(stage, tmp, to_split):
                layer, which = stage // 2, 2 * (stage % 2)
                act.wait_ge(mod_stored, (2, 5, 8, 10)[stage])
                for k in range(4):
                    act.wait_ge(xn_turned, 4 * stage + k // 2 + 1)
                    ins = act.activation(tmp[:, k, :], ps[:, k // 2, (k % 2) * SEQ:(k % 2 + 1) * SEQ], ACT.Identity,
                                         scale=mod[:, layer, which + 1, k:k + 1], bias=mod[:, layer, which, k:k + 1])
                ins.then_inc(h_act, 1)
                if to_split:
                    act.wait_ge(h_act, stage + 1)
                    act.copy(h_high[:, 0:4, :], tmp[:, 0:4, :]).then_inc(h_high_s, 1)
                    act.wait_ge(h_dve, stage + 1)
                    act.copy(h_high[:, 4:8, :], tmp[:, 4:8, :]).then_inc(h_high_s, 1)

            def scale_ada(job, kp):
                n = ADA_OF[job, kp]
                wait_landed(act, n)
                rows_w = ring[:, n % RING, 1, :]
                if kp == 0 and job:
                    act.wait_ge(mod_summed, job)
                act.activation(rows_w if kp else ada_acc[:, 1, :], rows_w, ACT.Copy, scale=c_act[:, 2 * kp + 1:2 * kp + 2])\
                   .then_inc(ada_scaled, 1)

            def step(m):
                split_high(act, m)
                if m in ADA_WITH:
                    scale_ada(*ADA_WITH[m])

            act.wait_ge(small_s, 16)
            act.activation(c_act[:, :], small_of("c"), ACT.Silu).then_inc(c_ready, 1)
            act.wait_ge(c_ready, 1)
            act.wait_ge(x_in_s, 16)
            act.wait_ge(set_up, 1)
            square_and_root(0)
            for kp in range(4):
                scale_ada(0, kp)
            act.wait_ge(lg_ready, 1)
            act.activation(lg[:, 1, :], lg[:, 0, :], ACT.Exp, scale=-1.0).then_inc(act_chain, 1)
            act.wait_ge(lg_ready, 2)
            act.activation(lg[:, 3, :], lg[:, 2, :], ACT.Ln).then_inc(act_chain, 1)
            for kp in range(4):
                scale_ada(1, kp)
            h_of(0, h_ret, True)
            step(0)
            step(1)

            for i in range(6):
                for j in range(4):
                    m = 4 * i + j
                    step(m + LEAD)
                    if i == 0 and j < HEADS:
                        act.wait_ge(dist_ready, j + 1)
                        act.activation(prob[:, j, :], prob[:, j, :], ACT.Exp).then_inc(decay_ready, 1)
                if i < 2:
                    act.sem_inc(group_act, 1)
                    continue
                act.wait_ge(w_used, 4 * i + 4)
                bank = 4 * (i % 2)
                if i >= 4:
                    act.wait_ge(prob_ready, HEADS)
                for t, h in ([(0, 0), (0, 1)] if i < 4 else [(0, 0), (0, 1), (1, 0), (1, 1)]):
                    src = ps[:, bank + 2 * t + h, :]
                    at = (i % 2) * COLS + h * 512
                    if i < 4:
                        ins = act.copy(v[:, t, at:at + 512], src)
                    else:
                        ins = act.activation(ret_g[:, t, at:at + 512], src, ACT.Silu)
                ins.then_inc(group_act, 1)

            for h in range(HEADS):
                act.wait_ge(o_done, h + 1)
                for t in range(TT):
                    n = 2 * h + t
                    if n:
                        act.wait_ge(o_squares, n)
                    act.activation(scratch[:, 0, :], ps[:, n, :], ACT.Square, accum_out=ssq[:, n:n + 1]).then_inc(o_squares, 1)
            act.wait_ge(o_squares, 2 * HEADS)
            act.activation(std[:, :], ssq[:, :], ACT.Sqrt, scale=1.0 / V_DIM, bias=eps[:, :]).then_inc(o_std, 1)

            def piece_up(n, bank):
                act.wait_ge(turned, n + 1)
                act.copy(piece_high[:, n % 2, :], ps[:, bank, :]).then_inc(piece_high_s, 1)

            piece_up(0, 4)
            piece_up(1, 5)
            for kp in range(8):
                step(M_RET_OUT + kp + LEAD)
                if kp + 2 < 8:
                    piece_up(kp + 2, 4 + kp % 2)

            def experts(layer):
                m0 = M_MOE[layer]
                stage = 2 * layer + 1
                act.wait_ge(x_ready, 2 * layer + 1)
                square_and_root(stage)
                h_of(stage, h_all, False)
                act.wait_ge(logits_done, layer + 1)
                act.activation(rt[:, 15, :], ps[:, 4, 0:TT * N_EXPERTS], ACT.Sigmoid).then_inc(scores_ready, 1)

                def gathered_up(g):
                    act.wait_ge(gather_done, g + (5 * layer + 1))
                    for k in range(4):
                        ins = act.activation(gathered[:, k, :], ps[:, 0, k * P:(k + 1) * P], ACT.Identity,
                                             scale=mod[:, layer, 3, k:k + 1], bias=mod[:, layer, 2, k:k + 1])
                    ins.then_inc(gathered_act, 1)
                    act.wait_ge(gathered_act, g + (5 * layer + 1))
                    act.wait_ge(gathered_dve, g + (5 * layer + 1))
                    act.copy(h_high[:, :, 0:P], gathered).then_inc(hg_high, 1)

                gathered_up(0)
                with act.Fori(0, GROUPS) as g:
                    for s in range(MOE_GRAN):
                        split_high(act, m0 + s + LEAD, g)
                        if s in (3, 7, 13, 19):
                            e = {3: 0, 7: 1, 13: 2, 19: 3}[s]
                            act.wait_ge(w_used, g * MOE_GRAN + (m0 + s + 1))
                            act.activation(hid[:, e % 2, :], ps[:, 2 * (e % 2), :], ACT.Silu).then_inc(silu_done, 1)
                        if s in (4, 10, 16, 20):
                            e = {4: 0, 10: 1, 16: 2, 20: 3}[s]
                            act.wait_ge(hid_turned, g * PER_GROUP + (N_EXPERTS * layer + e + 1))
                            act.copy(piece_high[:, e % 2, :], ps[:, 6, :]).then_inc(hid_high, 1)
                        if s == 4:
                            act.wait_ge(sel_turned, g + (GROUPS * layer + 1))
                            act.copy(sel_t[:, :], ps[:, 7, 0:SEQ]).then_inc(sel_t_s, 1)
                        if s == 21:
                            gathered_up(g + 1)
                    act.wait_ge(w_used, (g + 1) * MOE_GRAN + m0)
                    act.copy(y_slots[:, 0:512], ps[:, 4, :]).then_inc(y_act, 1)

                o = ov[layer]
                act.wait_ge(over_known, layer + 1)
                flag = act.value_load(over_i[0:1, 0:1], min_val=0, max_val=1)
                group = act.value_load(over_i[0:1, 1:2], min_val=0, max_val=GROUPS - 1)
                with act.If(flag > 0):
                    n_w = 0

                    def load(e, kind, j):
                        nonlocal n_w
                        if n_w:
                            act.wait_ge(o["used"], n_w)
                        n_w += 1
                        at = N_OF[m0] + MOE_ORDER.index((e, kind, j))
                        act.dma_start(area[:, 6144:8192], stream[group * MOE_GRAN + at]).then_inc(o["w"], 16)

                    for e in range(PER_GROUP):
                        for j in range(4):
                            load(e, "up", j)
                        act.wait_ge(o["used"], n_w)
                        act.activation(hid[:, 0, :], ps[:, 0, :], ACT.Silu).then_inc(o["silu"], 1)
                        act.wait_ge(o["turned"], e + 1)
                        act.copy(hid[:, 1, :], ps[:, 6, :]).then_inc(o["t_act"], 1)
                        for j in range(2):
                            load(e, "down", j)
                    act.wait_ge(o["sel_turned"], 1)
                    act.copy(sel_t[:, :], ps[:, 7, 0:SEQ]).then_inc(o["sel_t"], 1)
                    act.copy(y_slots[:, 0:512], ps[:, 4, :]).then_inc(o["y"], 1)

            experts(0)

            act.wait_ge(x_ready, 2)
            square_and_root(2)
            h_of(2, h_all, True)
            for i in range(3):
                for j in range(4):
                    step(M_GM + 4 * i + j + LEAD)
                act.wait_ge(w_used, M_GM + 4 * i + 4)
                if i == 0:
                    act.wait_ge(h_low_s, 2)
                for t in range(TT):
                    for h in range(2):
                        ins = act.activation(gv[:, t, i * COLS + h * 512:i * COLS + (h + 1) * 512],
                                             ps[:, 4 * (i % 2) + 2 * t + h, :], ACT.Gelu)
                ins.then_inc(group_act, 1)
            for j in range(2):
                step(M_GM + 12 + j + LEAD)
            act.wait_ge(ln_std, 1)
            act.activation(std[:, 0:TT], mean_var[:, :, 1], ACT.Sqrt, bias=eps[:, :]).then_inc(ln_std, 1)
            for i in range(3):
                for j in range(2 if i == 0 else 0, 4):
                    step(M_GM + 12 + 8 * i + j + LEAD)
                act.wait_ge(w_used, M_GM + 12 + 8 * i + 4)
                if i >= 1:
                    act.wait_ge(z_ready, 8 * i)
                for b in range(4):
                    act.activation(u_t[:, 2 * b:2 * b + 2, :], ps[:, 4 + b, :].rearrange("p (k n) -> p k n", k=2),
                                   ACT.Gelu).then_inc(group_act, 1)
                for kp in range(4):
                    act.wait_ge(z_ready, 8 * i + 2 * kp + 2)
                    if kp >= 2 or i:
                        act.wait_ge(w_used, M_GM + 12 + 8 * i + 4 + kp - 2 + 1 if kp >= 2 else M_GM + 12 + 8 * (i - 1) + 8 - 2 + kp + 1)
                    act.copy(piece_high[:, kp % 2, :], u_t[:, 2 * kp:2 * kp + 2, :].rearrange("p k n -> p (k n)"))\
                        .then_inc(piece_high_s, 1)
                    step(M_GM + 12 + 8 * i + 4 + kp + LEAD)

            experts(1)

            act.wait_ge(x_ready, 4)
            square_and_root(4)

        @block.gpsimd
        def _(pool):
            def add_ada(job, kp):
                acc = ada_acc[:, 1, :]
                pool.wait_ge(ada_scaled, 4 * job + kp + 1)
                if kp:
                    if 3 * job + kp > 1:
                        pool.wait_ge(ada_pool, 3 * job + kp - 1)
                    pool.tensor_tensor(acc, acc, ring[:, ADA_OF[job, kp] % RING, 1, :], ALU.add).then_inc(ada_pool, 1)

            for job in range(2):
                for kp in range(4):
                    add_ada(job, kp)
            pool.wait_ge(decay_s, 16)
            pool.wait_ge(lg_ready, 3)
            pool.wait_ge(xn_turned, 4)
            back = scratch[:, 0, :]
            for h in range(HEADS):
                pool.tensor_scalar(prob[:, h, :], dist[:, 0, :], lg[:, 5, h:h + 1], None, ALU.mult).then_inc(pool_chain, 1)
                pool.tensor_scalar(back, dist[:, 1, :], lg[:, 5, HEADS + h:HEADS + h + 1], None, ALU.mult).then_inc(pool_chain, 1)
                pool.wait_ge(pool_chain, 2 * h + 2)
                pool.tensor_tensor(prob[:, h, :], prob[:, h, :], back, ALU.add).then_inc(dist_ready, 1)
                pool.wait_ge(dist_ready, h + 1)
            for job in (2, 3):
                for kp in range(4):
                    add_ada(job, kp)
                for h in range(HEADS):
                    n = HEADS * (job - 2) + h
                    pool.wait_ge(rot_ready, n + 1)
                    pool.tensor_tensor(qk[:, job - 2, h, 0, :], rot[:, h % 2, 0, 0:SEQ], rot[:, h % 2, 1, SEQ:], ALU.subtract)
                    pool.tensor_tensor(qk[:, job - 2, h, 1, :], rot[:, h % 2, 1, 0:SEQ], rot[:, h % 2, 0, SEQ:], ALU.add)\
                        .then_inc(rot_done, 1)
            for job in range(4, 12):
                for kp in range(4):
                    add_ada(job, kp)
                if job == 11:
                    pool.wait_ge(mix_rows_s, 1)
                    pool.wait_ge(mix_s, 32)
                    for ch in range(GM_HALF // P):
                        g = ch * P // (GM_HALF // GM_GROUPS)
                        if ch >= 4:
                            pool.wait_ge(z_ready, ch - 3)
                        to = mix_add[:, (ch // 2) % 2, (ch % 2) * P:(ch % 2 + 1) * P]
                        pool.tensor_scalar(to, mix_rows[:, g, :], ln_b[:, ch:ch + 1], None, ALU.mult).then_inc(mix_scaled, 1)
                        pool.wait_ge(mix_scaled, ch + 1)
                        pool.tensor_tensor(to, to, mix_bs[:, g, :], ALU.add).then_inc(mix_add_s, 1)

        @block.vector
        def _(dve):
            links = [0]

            def link(ins):
                links[0] += 1
                ins.then_inc(dve_chain, 1)
                dve.wait_ge(dve_chain, links[0])

            def add_ada(job, kp):
                n = ADA_OF[job, kp]
                wait_landed(dve, n)
                c = c_act[:, 2 * kp:2 * kp + 1]
                acc = ada_acc[:, 0, :]
                if kp == 0:
                    if job:
                        dve.wait_ge(mod_summed, job)
                    dve.tensor_scalar(acc, ring[:, n % RING, 0, :], c, None, ALU.mult).then_inc(ada_dve, 1)
                else:
                    dve.wait_ge(ada_dve, 4 * job + kp)
                    dve.scalar_tensor_tensor(acc, ring[:, n % RING, 0, :], c, acc, ALU.mult, ALU.add).then_inc(ada_dve, 1)

            def step(m):
                split_low(dve, m)
                if m in ADA_WITH:
                    add_ada(*ADA_WITH[m])

            def store_mod(job, bank):
                layer, which = JOBS[job]
                dve.wait_ge(mod_summed, job + 1)
                if (layer, which) in GATE_ROW:
                    r = GATE_ROW[layer, which]
                    dve.wait_ge(row_s[2 * layer + (which == G2)], 16)
                    for h in range(2):
                        ins = dve.tensor_tensor(rows[:, r, h * 512:(h + 1) * 512], ps[:, bank + h, :],
                                                rows[:, r, h * 512:(h + 1) * 512], ALU.add)
                    ins.then_inc(mod_stored, 1)
                    return
                to = mod[:, layer, {SH1: 0, SC1: 1, SH2: 2, SC2: 3}[which], :]
                if which in (SH1, SH2):
                    dve.tensor_tensor(to, ps[:, bank, 0:KC], b_ada[:, layer, which, :], ALU.add).then_inc(mod_stored, 1)
                else:
                    link(dve.scalar_tensor_tensor(to, ps[:, bank, 0:KC], 1.0, b_ada[:, layer, which, :], ALU.add, ALU.add))
                    dve.tensor_tensor(to, to, norm_g[:, layer, which // 3, :], ALU.mult).then_inc(mod_stored, 1)

            def scale_x(stage):
                dve.wait_ge(std_ready, stage + 1)
                link(dve.reciprocal(rstd[:, 0:TT], std[:, 0:TT]))
                for t in range(TT):
                    dve.tensor_scalar(xn[:, t, :], x[:, t, :], rstd[:, t:t + 1], None, ALU.mult).then_inc(xn_ready, 1)

            def h_of(stage, tmp, to_split):
                layer, which = stage // 2, 2 * (stage % 2)
                dve.wait_ge(mod_stored, (2, 5, 8, 10)[stage])
                for k in range(4, 8):
                    dve.wait_ge(xn_turned, 4 * stage + k // 2 + 1)
                    ins = dve.tensor_scalar(tmp[:, k, :], ps[:, k // 2, (k % 2) * SEQ:(k % 2 + 1) * SEQ],
                                            mod[:, layer, which + 1, k:k + 1], mod[:, layer, which, k:k + 1], ALU.mult, ALU.add)
                ins.then_inc(h_dve, 1)
                if to_split:
                    for half in range(2):
                        dve.wait_ge(h_high_s, stage + half + 1)
                        ks = slice(4 * half, 4 * half + 4)
                        ins = dve.tensor_tensor(h_low[:, ks, :], tmp[:, ks, :], h_high[:, ks, :].bitcast(F32), ALU.subtract)
                    ins.then_inc(h_low_s, 1)

            def add_output(n, row):
                dve.wait_ge(w_used, (M_RET_OUT + 8, M_GM + 36)[n])
                for i in range(4):
                    t, h = i // 2, i % 2
                    cols = slice(h * 512, (h + 1) * 512)
                    link(dve.tensor_tensor(scratch[:, i % 2, :], ps[:, i, :], rows[:, row, cols], ALU.mult))
                    ins = dve.tensor_tensor(x[:, t, cols], x[:, t, cols], scratch[:, i % 2, :], ALU.add)
                ins.then_inc(x_ready, 1)

            dve.memset(ones[:, :], 1.0)
            dve.memset(eps[:, :], EPS).then_inc(set_up, 1)
            dve.wait_ge(small_s, 16)
            link(dve.tensor_scalar(lg[:, 4, :], decay_logit, -1.0, None, ALU.mult))
            dve.tensor_tensor(lg[:, 0, :], decay_logit, lg[:, 4, :], ALU.max).then_inc(lg_ready, 1)
            dve.wait_ge(c_ready, 1)
            for kp in range(4):
                add_ada(0, kp)
            scale_x(0)
            dve.wait_ge(act_chain, 1)
            dve.tensor_scalar(lg[:, 2, :], lg[:, 1, :], 1.0, None, ALU.add).then_inc(lg_ready, 1)
            store_mod(0, 4)
            for kp in range(4):
                add_ada(1, kp)
            dve.wait_ge(act_chain, 2)
            dve.wait_ge(lg_ready, 2)
            link(dve.tensor_scalar(lg[:, 4, :], lg[:, 2, :], -1.0, None, ALU.add))
            link(dve.tensor_scalar(lg[:, 0, :], lg[:, 4, :], 0.0, None, ALU.is_equal))
            link(dve.tensor_tensor(lg[:, 4, :], lg[:, 4, :], lg[:, 0, :], ALU.add))
            link(dve.tensor_tensor(lg[:, 3, :], lg[:, 3, :], lg[:, 0, :], ALU.add))
            link(dve.reciprocal(lg[:, 4, :], lg[:, 4, :]))
            link(dve.tensor_tensor(lg[:, 3, :], lg[:, 3, :], lg[:, 4, :], ALU.mult))
            link(dve.tensor_tensor(lg[:, 3, :], lg[:, 3, :], lg[:, 1, :], ALU.mult))
            link(dve.tensor_scalar(lg[:, 4, :], decay_logit, 0.0, None, ALU.min))
            dve.tensor_tensor(lg[:, 5, :], lg[:, 4, :], lg[:, 3, :], ALU.subtract).then_inc(lg_ready, 1)
            store_mod(1, 5)
            h_of(0, h_ret, True)
            step(0)
            step(1)

            def probs(i):
                for h in (2 * (i - 2), 2 * (i - 2) + 1):
                    dve.wait_ge(scores_done, h + 1)
                    dve.wait_ge(decay_ready, h + 1)
                    dve.scalar_tensor_tensor(prob[:, h, :], ps[:, 4 - 4 * (i % 2) + 2 + h % 2, :], QK_SCALE, prob[:, h, :],
                                             ALU.mult, ALU.mult).then_inc(prob_ready, 1)

            for i in range(6):
                for j in range(4):
                    step(4 * i + j + LEAD)
                    if j == 3:
                        store_mod(2 + i, 4 - 4 * (i % 2))
                        if i in (2, 3):
                            probs(i)
                bank = 4 * (i % 2)
                dve.wait_ge(w_used, 4 * i + 4)
                if i == 0:
                    dve.wait_ge(h_low_s, 1)
                if i < 2:
                    for h in range(HEADS):
                        n = HEADS * i + h
                        if n >= 2:
                            dve.wait_ge(rot_done, n - 1)
                        both = ps[:, bank + h, :].rearrange("p (c n) -> p c n", c=2)
                        for w, table in enumerate((cos, sin)):
                            ins = dve.tensor_tensor(rot[:, h % 2, w, :].rearrange("p (c n) -> p c n", c=2), both,
                                                    table.unsqueeze(1).to_broadcast([P, 2, SEQ]), ALU.mult)
                        ins.then_inc(rot_ready, 1)
                    dve.wait_ge(rot_ready, HEADS * i + HEADS)
                    dve.sem_inc(group_dve, 1)
                elif i < 4:
                    if i == 2:
                        dve.wait_ge(rot_done, 2 * HEADS)
                    for h in range(2):
                        at = (i % 2) * COLS + h * 512
                        ins = dve.tensor_copy(v[:, 1, at:at + 512], ps[:, bank + 2 + h, :])
                    ins.then_inc(group_dve, 1)
                else:
                    dve.sem_inc(group_dve, 1)
            dve.wait_ge(o_std, 1)
            dve.wait_ge(group_act, 6)
            link(dve.reciprocal(rstd[:, :], std[:, :]))
            for h in range(HEADS):
                for t in range(TT):
                    n = 2 * h + t
                    part = ret_g[:, t, h * V_DIM:(h + 1) * V_DIM]
                    dve.scalar_tensor_tensor(part, ps[:, n, :], rstd[:, n:n + 1], part, ALU.mult, ALU.mult).then_inc(o_gated, 1)

            def piece_down(n, bank):
                dve.wait_ge(piece_high_s, n + 1)
                dve.tensor_tensor(piece_low[:, n % 2, :], ps[:, bank, :], piece_high[:, n % 2, :].bitcast(F32), ALU.subtract)\
                   .then_inc(piece_low_s, 1)

            piece_down(0, 4)
            piece_down(1, 5)
            for kp in range(8):
                step(M_RET_OUT + kp + LEAD)
                if kp % 4 == 3:
                    store_mod(8 + kp // 4, 6)
                if kp + 2 < 8:
                    piece_down(kp + 2, 4 + kp % 2)
            add_output(0, GATE_ROW[0, G1])

            def route(layer):
                def r(i, n=TT * N_EXPERTS):
                    return rt[:, i, 0:n]

                def quads(i):
                    return rt[:, i, :].rearrange("p (g e) -> p g e", e=PER_GROUP)

                def by_group(i):
                    return rt[:, i, 0:TT * GROUPS]

                def spread(i):
                    return by_group(i).unsqueeze(2).to_broadcast([P, TT * GROUPS, PER_GROUP])

                def tt(o, a, b, op):
                    link(dve.tensor_tensor(o, a, b, op))

                def ts(o, a, s1, op1, s2=None, op2=None):
                    link(dve.tensor_scalar(o, a, s1, s2, op1, op2) if op2 is not None else dve.tensor_scalar(o, a, s1, None, op1))

                SC, BI = 15, 14
                dve.wait_ge(scores_ready, layer + 1)
                tt(r(BI).rearrange("p (t e) -> p t e", t=TT), r(SC).rearrange("p (t e) -> p t e", t=TT),
                   router_b.unsqueeze(1).to_broadcast([P, TT, N_EXPERTS]), ALU.add)
                b = quads(BI)
                tt(by_group(2), b[:, :, 0], b[:, :, 1], ALU.max)
                tt(by_group(3), b[:, :, 0], b[:, :, 1], ALU.min)
                tt(by_group(4), b[:, :, 2], b[:, :, 3], ALU.max)
                tt(by_group(5), b[:, :, 2], b[:, :, 3], ALU.min)
                tt(by_group(6), by_group(2), by_group(4), ALU.max)
                tt(by_group(7), by_group(2), by_group(4), ALU.min)
                tt(by_group(8), by_group(3), by_group(5), ALU.max)
                tt(by_group(7), by_group(7), by_group(8), ALU.max)
                tt(by_group(6), by_group(6), by_group(7), ALU.add)
                sums = by_group(6).rearrange("p (t g) -> p t g", t=TT)
                link(dve.tensor_reduce(rt[:, 7, 0:TT], sums, AX_X, ALU.max))
                tt(by_group(8).rearrange("p (t g) -> p t g", t=TT), sums,
                   rt[:, 7, 0:TT].unsqueeze(2).to_broadcast([P, TT, GROUPS]), ALU.is_equal)
                members = by_group(0).rearrange("p (t g) -> p t g", t=TT)
                is_max = by_group(8).rearrange("p (t g) -> p t g", t=TT)
                left = rt[:, 7, 0:TT]
                ts(left, left, 0.0, ALU.mult, 1.0, ALU.add)
                for g in range(GROUPS):
                    tt(members[:, :, g], is_max[:, :, g], left, ALU.mult)
                    if g + 1 < GROUPS:
                        tt(left, left, members[:, :, g], ALU.subtract)
                dve.memset(done_mark[:, 0:1], 0.0).then_inc(members_ready, 1)
                rank = quads(10)
                for e in range(PER_GROUP):
                    link(dve.memset(rank[:, :, e], float(PER_GROUP - 1 - e)))
                for d in range(1, PER_GROUP):
                    n = PER_GROUP - d
                    c = quads(11)[:, :, 0:n]
                    tt(c, b[:, :, 0:n], b[:, :, d:], ALU.is_ge)
                    tt(rank[:, :, 0:n], rank[:, :, 0:n], c, ALU.subtract)
                    tt(rank[:, :, d:], rank[:, :, d:], c, ALU.add)
                ts(r(10), r(10), 1.5, ALU.is_lt)
                tt(quads(10), quads(10), spread(0), ALU.mult)
                tt(r(10), r(10), r(SC), ALU.mult)
                by_tile = r(10).rearrange("p (t e) -> p t e", t=TT)
                link(dve.tensor_reduce(rt[:, 11, 0:TT], by_tile, AX_X, ALU.add))
                link(dve.reciprocal(rt[:, 11, 0:TT], rt[:, 11, 0:TT]))
                tt(by_tile, by_tile, rt[:, 11, 0:TT].unsqueeze(2).to_broadcast([P, TT, N_EXPERTS]), ALU.mult)
                gates = r(10).rearrange("p (t g e) -> p t e g", t=TT, g=GROUPS)
                link(dve.tensor_reduce(own_gates[:, :, :], gates, AX_X, ALU.add))
                dve.wait_ge(place_done, layer + 1)
                ts(by_group(12), ps[:, 5, 0:TT * GROUPS], 1.0, ALU.add)
                tt(by_group(12), by_group(12), by_group(0), ALU.mult)
                ts(by_group(1), by_group(12), float(P) + 0.5, ALU.is_gt)
                dve.memset(done_mark[:, 1:2], 0.0).then_inc(route_ready, 1)
                tt(by_group(13), by_group(12), by_group(1), ALU.mult)
                tt(by_group(12), by_group(12), by_group(13), ALU.subtract)
                link(dve.tensor_scalar(slot_of[:, :, 0:GROUPS], by_group(12).rearrange("p (t g) -> p t g", t=TT),
                                       -1.0, None, ALU.add))
                link(dve.tensor_reduce(rt[:, 13, 0:TT], by_group(13).rearrange("p (t g) -> p t g", t=TT), AX_X, ALU.add))
                ts(slot_of[:, :, GROUPS], rt[:, 13, 0:TT], -float(P) - 1.0, ALU.add)
                dve.wait_ge(over_counted, layer + 1)
                ts(over_f[:, 0:GROUPS], ps[:, 6, 0:GROUPS], 1.0, ALU.min)
                link(dve.tensor_reduce(over_f[:, 8:9], over_f[:, 0:GROUPS], AX_X, ALU.add))
                link(dve.scalar_tensor_tensor(over_f[:, 5:6], over_f[:, 3:4], 3.0, over_f[:, 1:2], ALU.mult, ALU.add))
                link(dve.scalar_tensor_tensor(over_f[:, 9:10], over_f[:, 2:3], 2.0, over_f[:, 5:6], ALU.mult, ALU.add))
                link(dve.tensor_copy(over_i[:, :], over_f[0:1, 8:10]))
                dve.memset(done_mark[:, 2:3], 0.0).then_inc(over_known, 1)

            def experts(layer):
                m0 = M_MOE[layer]
                stage = 2 * layer + 1
                row = GATE_ROW[layer, G2]
                scale_x(stage)
                h_of(stage, h_all, False)
                route(layer)
                dve.memset(done_mark[:, 3:4], 0.0).then_inc(banks_free, 1)

                def choose(g, count):
                    for t in range(TT):
                        ins = dve.tensor_scalar(sel[:, t, :], iota, slot_of[:, t, bass.ds(g, 1)], None, ALU.is_equal)
                    ins.then_inc(sel_ready, 1)

                def gathered_down(g):
                    dve.wait_ge(gather_done, g + (5 * layer + 1))
                    dve.tensor_copy(slot_gates[:, :], ps[:, 2, 0:PER_GROUP])
                    for k in range(4, 8):
                        ins = dve.tensor_scalar(gathered[:, k, :], ps[:, 1, (k - 4) * P:(k - 3) * P],
                                                mod[:, layer, 3, k:k + 1], mod[:, layer, 2, k:k + 1], ALU.mult, ALU.add)
                    ins.then_inc(gathered_dve, 1)
                    dve.wait_ge(hg_high, g + (5 * layer + 1))
                    dve.tensor_tensor(h_low[:, :, 0:P], gathered, h_high[:, :, 0:P].bitcast(F32), ALU.subtract)\
                       .then_inc(hg_low, 1)

                choose(0, 0)
                gathered_down(0)
                with dve.Fori(0, GROUPS) as g:
                    for s in range(MOE_GRAN):
                        split_low(dve, m0 + s + LEAD, g)
                        if s in (3, 7, 13, 19):
                            e = {3: 0, 7: 1, 13: 2, 19: 3}[s]
                            dve.wait_ge(silu_done, g * PER_GROUP + (N_EXPERTS * layer + e + 1))
                            dve.scalar_tensor_tensor(hid[:, e % 2, :], hid[:, e % 2, :], slot_gates[:, e:e + 1],
                                                     ps[:, 2 * (e % 2) + 1, :], ALU.mult, ALU.mult).then_inc(hid_ready, 1)
                        if s in (4, 10, 16, 20):
                            e = {4: 0, 10: 1, 16: 2, 20: 3}[s]
                            dve.wait_ge(hid_high, g * PER_GROUP + (N_EXPERTS * layer + e + 1))
                            dve.tensor_tensor(piece_low[:, e % 2, :], ps[:, 6, :], piece_high[:, e % 2, :].bitcast(F32),
                                              ALU.subtract).then_inc(hid_low, 1)
                        if s == 4:
                            dve.wait_ge(sel_turned, g + (GROUPS * layer + 1))
                            choose(g + 1, None)
                        if s == 21:
                            gathered_down(g + 1)
                    dve.wait_ge(w_used, (g + 1) * MOE_GRAN + m0)
                    dve.tensor_copy(y_slots[:, 512:1024], ps[:, 5, :]).then_inc(y_dve, 1)
                    for i, bank in enumerate((6, 7, 2, 3)):
                        t, cols = i // 2, slice((i % 2) * 512, (i % 2 + 1) * 512)
                        dve.wait_ge(scattered, g * 4 + (4 * GROUPS * layer + i + 1))
                        dve.tensor_tensor(scratch[:, i % 2, :], ps[:, bank, :], rows[:, row, cols], ALU.mult)\
                           .then_inc(scatter_term, 1)
                        dve.wait_ge(scatter_term, g * 4 + (4 * GROUPS * layer + i + 1))
                        ins = dve.tensor_tensor(x[:, t, cols], x[:, t, cols], scratch[:, i % 2, :], ALU.add)
                    ins.then_inc(banks_free, 1)

                o = ov[layer]
                flag = dve.value_load(over_i[0:1, 0:1], min_val=0, max_val=1)
                with dve.If(flag > 0):
                    for e in range(PER_GROUP):
                        dve.wait_ge(o["silu"], e + 1)
                        dve.scalar_tensor_tensor(hid[:, 0, :], hid[:, 0, :], slot_gates[:, e:e + 1], ps[:, 1, :],
                                                 ALU.mult, ALU.mult).then_inc(o["hid"], 1)
                    dve.wait_ge(o["sel_turned"], 1)
                    dve.tensor_copy(y_slots[:, 512:1024], ps[:, 5, :]).then_inc(o["y"], 1)
                    for i, bank in enumerate((6, 7, 2, 3)):
                        t, cols = i // 2, slice((i % 2) * 512, (i % 2 + 1) * 512)
                        dve.wait_ge(o["scattered"], i + 1)
                        dve.tensor_tensor(scratch[:, i % 2, :], ps[:, bank, :], rows[:, row, cols], ALU.mult)\
                           .then_inc(o["term"], 1)
                        dve.wait_ge(o["term"], i + 1)
                        dve.tensor_tensor(x[:, t, cols], x[:, t, cols], scratch[:, i % 2, :], ALU.add)
                dve.drain().then_inc(x_ready, 1)

            experts(0)

            scale_x(2)
            h_of(2, h_all, True)
            for i in range(3):
                for j in range(4):
                    step(M_GM + 4 * i + j + LEAD)
                if i >= 1:
                    store_mod(9 + i, 4 - 4 * (i % 2))
                dve.wait_ge(group_act, 7 + i)
                for t in range(TT):
                    for h in range(2):
                        ins = dve.bn_stats(bn[:, t, 2 * i + h, :], gv[:, t, i * COLS + h * 512:i * COLS + (h + 1) * 512])
            link(ins)
            for t in range(TT):
                ins = dve.bn_aggr(mean_var[:, t, :], bn[:, t, :, :])
            ins.then_inc(ln_std, 1)
            dve.wait_ge(mix_rows_done, 1)
            dve.tensor_copy(mix_rows, ps[:, 4, :].rearrange("p (g n) -> p g n", g=GM_GROUPS)).then_inc(mix_rows_s, 1)
            for j in range(2):
                step(M_GM + 12 + j + LEAD)
            dve.wait_ge(ln_std, 2)
            link(dve.reciprocal(rstd[:, 0:TT], std[:, 0:TT]))
            for t in range(TT):
                dve.tensor_scalar(gv[:, t, :], gv[:, t, :], mean_var[:, t, 0:1], rstd[:, t:t + 1], ALU.subtract, ALU.mult)\
                   .then_inc(gv_ready, 1)
            for i in range(3):
                for j in range(2 if i == 0 else 0, 4):
                    step(M_GM + 12 + 8 * i + j + LEAD)
                for kp in range(4):
                    dve.wait_ge(mixed_done, 4 * i + kp + 1)
                    for c in (2 * kp, 2 * kp + 1):
                        ch = 8 * i + c
                        half = slice((c % 2) * SEQ, (c % 2 + 1) * SEQ)
                        tmp = scratch[:, c % 2, 0:SEQ]
                        dve.wait_ge(mix_add_s, ch + 1)
                        added = mix_add[:, (ch // 2) % 2, (ch % 2) * P:(ch % 2 + 1) * P].unsqueeze(1).to_broadcast([P, TT, P])
                        link(dve.scalar_tensor_tensor(tmp.rearrange("p (t n) -> p t n", t=TT),
                                                      ps[:, 4 + kp, half].rearrange("p (t n) -> p t n", t=TT),
                                                      ln_g[:, ch:ch + 1], added, ALU.mult, ALU.add))
                        dve.tensor_tensor(u_t[:, c, :], u_t[:, c, :], tmp, ALU.mult).then_inc(z_ready, 1)
                    dve.wait_ge(piece_high_s, 8 + 4 * i + kp + 1)
                    dve.tensor_tensor(piece_low[:, kp % 2, :], u_t[:, 2 * kp:2 * kp + 2, :].rearrange("p k n -> p (k n)"),
                                      piece_high[:, kp % 2, :].bitcast(F32), ALU.subtract).then_inc(piece_low_s, 1)
                    step(M_GM + 12 + 8 * i + 4 + kp + LEAD)
            add_output(1, GATE_ROW[1, G1])

            experts(1)

            dve.wait_ge(std_ready, 5)
            link(dve.reciprocal(rstd[:, 0:TT], std[:, 0:TT]))
            dve.wait_ge(row_s[4], 16)
            for t in range(TT):
                dve.scalar_tensor_tensor(xn[:, t, :], x[:, t, :], rstd[:, t:t + 1], rows[:, FINAL_ROW, :], ALU.mult, ALU.mult)\
                   .then_inc(out_ready, 1)


def _granules(w):
    k, n = w.shape
    return w.reshape(k // 256, 2, 128, n // COLS, COLS).transpose(3, 0, 2, 1, 4).reshape(n // COLS, k // 256, 128, GRAN)


def _columns(a):
    return a.reshape(-1, 128).T


def kernel(**inputs):
    import numpy as np
    import concourse.bacc as bacc
    from concourse.bass_utils import run_bass_kernel_spmd as run

    inp = {k: np.asarray(a) for k, a in inputs.items()}
    ada = [_granules(inp["w_ada"][layer]) for layer in range(2)]
    ret_in, ret_out = _granules(inp["ret_w_in"][0]), _granules(inp["ret_w_out"][0])
    gm_in, gm_out = _granules(inp["gm_w_in"][0]), _granules(inp["gm_w_out"][0])
    dense = [ret_in[i, j] for i in range(6) for j in range(4)] + [ret_out[0, j] for j in range(8)]

    def expert_granules(layer):
        out = []
        for g in range(GROUPS):
            for e, kind, j in MOE_ORDER:
                w = inp["moe_w_gate_up" if kind == "up" else "moe_w_down"][layer, g * PER_GROUP + e]
                out.append(w[j * 256:(j + 1) * 256].reshape(2, 128, COLS).transpose(1, 0, 2).reshape(128, GRAN))
        return out

    dense += expert_granules(0)
    dense += [gm_in[3 + i, j] for i in range(3) for j in range(4)]
    for i in range(3):
        dense += [gm_in[i, j] for j in range(4)] + [gm_out[0, 4 * i + j] for j in range(4)]
    dense += expert_granules(1)
    dense += [dense[0]] * LEAD
    stream = np.empty((N_GRAN, 128, GRAN), np.float32)
    for n, p in enumerate(PLAN):
        stream[n] = dense[p[1]] if p[0] == "dense" else ada[JOBS[p[1]][0]][JOBS[p[1]][1], p[2]]

    def over_partitions(a):
        return np.broadcast_to(a.reshape(1, -1), (128, a.size))

    small = np.concatenate([
        _columns(inp["c"]), _columns(inp["b_ada"]), _columns(inp["norm_g"]),
        inp["router_w"].reshape(KC, 128, N_EXPERTS).transpose(1, 0, 2).reshape(128, -1),
        over_partitions(inp["router_b"]), over_partitions(inp["ret_decay_logit"][0]),
        _columns(inp["gm_ln_g"]), _columns(inp["gm_ln_b"])], axis=1)
    at = np.arange(128)
    half = D // HEADS // 2
    freq = (np.float32(10000.0) ** (-np.arange(half, dtype=np.float32) / np.float32(half))).astype(np.float32)
    angle = freq[:, None] * np.arange(SEQ, dtype=np.float32)[None, :]
    const = np.concatenate([np.eye(128), at[:, None] < at[None, :], np.broadcast_to(at, (128, 128)),
                            np.cos(angle), np.sin(angle)], axis=1).astype(np.float32)
    j_at = (np.arange(TT)[None, :, None] * 128 + at[:, None, None])
    dist = np.arange(SEQ)[None, None, :] - j_at
    decay = np.stack([np.maximum(dist, 0), np.maximum(-dist, 0)], axis=1).reshape(128, -1).astype(np.float32)
    b_ada = inp["b_ada"]
    gate_bias = np.stack([b_ada[0, 2 * D:3 * D], b_ada[0, 5 * D:], b_ada[1, 2 * D:3 * D], b_ada[1, 5 * D:]])
    mix_w = inp["gm_w_s"][0].transpose(2, 0, 1).reshape(128, -1)
    arrays = {
        "stream": stream, "x": inp["x"].reshape(SEQ, D), "small": small, "const": const, "decay_dist": decay,
        "gate_bias": gate_bias, "final_g": inp["final_g"].reshape(1, D), "mix_w": mix_w, "mix_b": over_partitions(inp["gm_b_s"][0]),
    }
    arrays = {k: np.ascontiguousarray(a) for k, a in arrays.items()}
    nc = bacc.Bacc("TRN2", target_bir_lowering=False, num_devices=1)
    aps = [nc.dram_tensor(f"{k}_dram", a.shape, mybir.dt.from_np(a.dtype), kind="ExternalInput").ap() for k, a in arrays.items()]
    out = nc.dram_tensor("out_dram", (SEQ, D), F32, kind="ExternalOutput").ap()
    trunk_kernel(nc, *aps, out)
    r = run(nc, [{f"{k}_dram": a for k, a in arrays.items()}], core_ids=[0])
    return r.results[0]["out_dram"].reshape(1, SEQ, D)
```

```python
from contextlib import ExitStack

import concourse.bass as bass
from concourse import mybir

F32 = mybir.dt.float32
F32R = mybir.dt.float32r
I32 = mybir.dt.int32
ALU = mybir.AluOpType
ACT = mybir.ActivationFunctionType
AX_X = mybir.AxisListType.X

P = 128
D = 1024
SEQ = 256
TT = SEQ // P
KC = D // P
EPS = 1e-6
HEADS = 4
V_DIM = 512
QK_SCALE = (D // HEADS) ** -0.5
GM_HALF = 3072
GM_GROUPS = 4
GROUPS = 4
PER_GROUP = 4
N_EXPERTS = GROUPS * PER_GROUP
D_EXPERT = 512

COLS = 1024
GRAN = 2 * COLS
RING = 6
SPLIT = 3
LEAD = SPLIT - 1
MOE_GRAN = 6 * PER_GROUP
MOE_ORDER = ([(0, "up", j) for j in range(4)] + [(1, "up", j) for j in range(4)] + [(0, "down", j) for j in range(2)]
             + [(2, "up", j) for j in range(4)] + [(1, "down", j) for j in range(2)]
             + [(3, "up", j) for j in range(4)] + [(2, "down", j) for j in range(2)]
             + [(3, "down", j) for j in range(2)])

SMALL = {}
_at = 0
for _name, _n in (("c", KC), ("b_ada", 2 * 6 * KC), ("norm_g", 2 * 2 * KC), ("router_w", KC * N_EXPERTS),
                  ("router_b", N_EXPERTS), ("decay", 2 * HEADS), ("ln_g", GM_HALF // P), ("ln_b", GM_HALF // P)):
    SMALL[_name] = (_at, _n)
    _at += _n
SMALL_N = _at


def stream_plan():
    plan = []
    m = 0

    def ada(jobs):
        return [("ada", job, kp) for job in jobs for kp in range(4)]

    def dense(n, parts=(), before=()):
        nonlocal m
        parts = list(parts)
        for i in range(n):
            for _ in range(list(before).count(i)):
                plan.append(parts.pop(0))
            plan.append(("dense", m))
            m += 1
        assert not parts

    plan += ada((0, 1))
    dense(24 + 8, ada(range(2, 8)), (3, 4, 5, 7, 8, 9, 11, 12, 13, 14, 15, 16, 18, 20, 21, 23) + 4 * (26,) + (27, 28, 29, 30))
    dense(4 * MOE_GRAN)
    dense(12 + 3 * 8, ada(range(8, 12)), range(4, 36, 2))
    dense(4 * MOE_GRAN)
    dense(LEAD)
    return plan


PLAN = stream_plan()
N_GRAN = len(PLAN)
N_OF = {p[1]: n for n, p in enumerate(PLAN) if p[0] == "dense"}
ADA_OF = {(p[1], p[2]): n for n, p in enumerate(PLAN) if p[0] == "ada"}
ADA_WITH = {p[1]: PLAN[n - 1][1:] for n, p in enumerate(PLAN) 
            if p[0] == "dense" and n and PLAN[n - 1][0] == "ada" and PLAN[n - 1][1] not in (1, 6)}

M_RET_OUT = 24
M_MOE = (32, 32 + 96 + 36)
M_GM = 32 + 96
assert MOE_GRAN % RING == 0 and MOE_GRAN % SPLIT == 0

SH1, SC1, G1, SH2, SC2, G2 = range(6)
JOBS = [(layer, which) for layer in range(2) for which in (SH1, SC1, G1, SH2, SC2, G2)]
RET_SUMS = {1: 2, 2: 3, 3: 4, 5: 5}
GATE_ROW = {(0, G1): 0, (0, G2): 1, (1, G1): 2, (1, G2): 0}
FINAL_ROW = 1


def trunk_kernel(nc: bass.Bass, stream: bass.AP, x_in: bass.AP, small_in: bass.AP, const_in: bass.AP, decay_in: bass.AP,
                 gate_bias: bass.AP, final_g: bass.AP, mix_w: bass.AP, mix_b: bass.AP, out: bass.AP):
    with ExitStack() as ctx:
        def sb(name, shape, dt=F32):
            return ctx.enter_context(nc.sbuf_tensor(name, shape, dt))

        def sem(name):
            return ctx.enter_context(nc.semaphore(name))

        ring = sb("ring", [P, RING, 2, COLS])
        w_high = sb("w_high", [P, SPLIT, 2, COLS], F32R)
        w_low = sb("w_low", [P, SPLIT, 2, COLS], F32R)
        ada_acc = sb("ada_acc", [P, COLS])
        x = sb("x", [P, TT, D])
        xn = sb("xn", [P, TT, D])
        h_high = sb("h_high", [P, KC, SEQ], F32R)
        h_low = sb("h_low", [P, KC, SEQ], F32R)
        piece_high = sb("piece_high", [P, 2, 512], F32R)
        piece_low = sb("piece_low", [P, 2, 512], F32R)
        rows = sb("rows", [P, 3, D])
        small = sb("small", [P, SMALL_N])
        const = sb("const", [P, 3 * P + 2 * SEQ])
        scratch = sb("scratch", [P, 2, 512])
        sel = sb("sel", [P, TT, P])
        sel_t = sb("sel_t", [P, SEQ], F32R)
        area = sb("area", [P, 8192])
        ones = sb("ones", [P, P])
        mod = sb("mod", [P, 2, 4, KC])
        c_act = sb("c_act", [P, KC])
        eps = sb("eps", [P, 1])
        warm = sb("warm", [P, 6])
        ssq = sb("ssq", [P, 8])
        std = sb("std", [P, 8])
        rstd = sb("rstd", [P, 8])
        lg = sb("lg", [P, 6, 2 * HEADS])
        bn = sb("bn", [P, TT, 6, 6])
        mean_var = sb("mean_var", [P, TT, 2])
        rt = sb("rt", [P, 16, TT * N_EXPERTS])
        own_gates = sb("own_gates", [P, TT, PER_GROUP])
        slot_of = sb("slot_of", [P, TT, GROUPS + 1])
        slot_gates = sb("slot_gates", [P, PER_GROUP])
        over_f = sb("over_f", [P, 16])
        over_i = sb("over_i", [1, 2], I32)
        done_mark = sb("done_mark", [P, 4])

        ps = ctx.enter_context(nc.psum_tensor("ps", [P, 8, 512], F32))

        ident, upper, iota = (const[:, i * P:(i + 1) * P] for i in range(3))
        cos, sin = (const[:, 3 * P + i * SEQ:3 * P + (i + 1) * SEQ] for i in range(2))

        def acc_of(job):
            return area[:, 0:COLS] if job == 1 else ada_acc[:, :]

        def small_of(name):
            a, n = SMALL[name]
            return small[:, a:a + n]

        b_ada = small_of("b_ada").rearrange("p (l w k) -> p l w k", l=2, w=6)
        norm_g = small_of("norm_g").rearrange("p (l w k) -> p l w k", l=2, w=2)
        router_w = small_of("router_w").rearrange("p (k e) -> p k e", k=KC)
        router_b = small_of("router_b")
        decay_logit = small_of("decay")
        ln_g, ln_b = small_of("ln_g"), small_of("ln_b")
        qk = area[:, 0:4096].rearrange("p (w h c n) -> p w h c n", w=2, h=HEADS, c=2)
        ret_g = area[:, 0:4096].rearrange("p (t n) -> p t n", t=TT)
        v = area[:, 4096:8192].rearrange("p (t n) -> p t n", t=TT)
        dist = area[:, 4096:5120].rearrange("p (w n) -> p w n", w=2)
        rot = area[:, 5120:7168].rearrange("p (b w n) -> p b w n", b=2, w=2)
        h_ret = area[:, 5120:7168].rearrange("p (k n) -> p k n", k=KC)
        prob = xn[:, :, :].rearrange("p t n -> p (t n)").rearrange("p (h n) -> p h n", h=HEADS)
        h_all = area[:, 0:2048].rearrange("p (k n) -> p k n", k=KC)
        gv = area[:, 0:6144].rearrange("p (t n) -> p t n", t=TT)
        mix_ws = area[:, 6144:6656].rearrange("p (g n) -> p g n", g=GM_GROUPS)
        mix_bs = area[:, 6656:7168].rearrange("p (g n) -> p g n", g=GM_GROUPS)
        mix_rows = area[:, 7168:7680].rearrange("p (g n) -> p g n", g=GM_GROUPS)
        mix_add = area[:, 7680:8192].rearrange("p (b n) -> p b n", b=2)
        u_t = xn[:, :, :].rearrange("p t n -> p (t n)").rearrange("p (k n) -> p k n", k=KC)
        gathered = area[:, 2048:3072].rearrange("p (k n) -> p k n", k=KC)
        y_high, y_low = h_high[:, :, P:SEQ], h_low[:, :, P:SEQ]
        hid = area[:, 4096:5120].rearrange("p (b n) -> p b n", b=2)
        more_terms = area[:, 5120:6144].rearrange("p (b n) -> p b n", b=2)

        def bank_of(bank):
            return ps[:, bank, :].rearrange("p (k n) -> p k n", k=4)

        def term(i):
            return scratch[:, i, :] if i < 2 else more_terms[:, i - 2, :]
        over_w = area[:, 6144:8192].rearrange("p (k n) -> p k n", k=2)

        landed = [sem(f"landed{i}") for i in range(RING)]
        x_in_s, small_s, const_s, decay_s = sem("x_landed"), sem("small_landed"), sem("const_landed"), sem("decay_landed")
        row_s = [sem(f"row_landed{i}") for i in range(5)]
        mix_s = sem("mix_landed")
        high_ready, low_ready = sem("high_ready"), sem("low_ready")
        w_used = sem("w_used")
        ada_dve, ada_pool, ada_scaled = sem("ada_dve"), sem("ada_pool"), sem("ada_scaled")
        set_up, c_ready = sem("set_up"), sem("c_ready")
        mod_summed, mod_stored = sem("mod_summed"), sem("mod_stored")
        squares_done, std_ready, rstd_ready, xn_ready = sem("squares_done"), sem("std_ready"), sem("rstd_ready"), sem("xn_ready")
        xn_turned, h_act, h_dve, h_high_s, h_low_s = sem("xn_turned"), sem("h_act"), sem("h_dve"), sem("h_high_s"), sem("h_low_s")
        x_ready, tile_done = sem("x_ready"), sem("tile_done")
        group_act, group_dve = sem("group_act"), sem("group_dve")
        dve_chain, act_chain, pool_chain = sem("dve_chain"), sem("act_chain"), sem("pool_chain")
        rot_ready, rot_done = sem("rot_ready"), sem("rot_done")
        lg_ready, dist_ready, decay_ready = sem("lg_ready"), sem("dist_ready"), sem("decay_ready")
        scores_done, prob_ready = sem("scores_done"), sem("prob_ready")
        o_done, o_squares, o_std, o_rstd, o_gated = sem("o_done"), sem("o_squares"), sem("o_std"), sem("o_rstd"), sem("o_gated")
        turned, piece_high_s, piece_low_s = sem("turned"), sem("piece_high_s"), sem("piece_low_s")
        ln_std, ln_rstd, gv_ready = sem("ln_std"), sem("ln_rstd"), sem("gv_ready")
        mixed_done, mix_rows_done, mix_rows_s, mix_add_s = sem("mixed_done"), sem("mix_rows_done"), sem("mix_rows_s"), sem("mix_add_s")
        mix_scaled = sem("mix_scaled")
        z_ready = sem("z_ready")
        logits_done, scores_ready, place_done, route_ready = sem("logits_done"), sem("scores_ready"), sem("place_done"), sem("route_ready")
        members_ready, over_counted, over_known = sem("members_ready"), sem("over_counted"), sem("over_known")
        sel_ready, sel_turned, sel_t_s = sem("sel_ready"), sem("sel_turned"), sem("sel_t_s")
        gates_done = sem("gates_done")
        gather_done, gathered_act, gathered_dve, hg_high, hg_low = sem("gather_done"), sem("gathered_act"), sem("gathered_dve"), sem("hg_high"), sem("hg_low")
        silu_done, hid_ready = sem("silu_done"), sem("hid_ready")
        hid_turned, hid_high, hid_low = sem("hid_turned"), sem("hid_high"), sem("hid_low")
        y_high_s, y_ready = sem("y_high_s"), sem("y_ready")
        scattered, scatter_term, x_added, banks_free = sem("scattered"), sem("scatter_term"), sem("x_added"), sem("banks_free")
        ov = [{n: sem(f"over{layer}_{n}") for n in ("w", "used", "silu", "hid", "turned", "t_act", "y_high", "y_low", "sel_turned",
                                                    "sel_t", "scattered", "term", "term_added")} for layer in range(2)]
        out_ready, stored = sem("out_ready"), sem("stored")

        block = ctx.enter_context(nc.Block())

        def turns(job, kp):
            return 4 * (job - 2) + kp + 1

        def wait_landed(eng, n, loops=0):
            eng.wait_ge(landed[n % RING], loops * (16 * MOE_GRAN // RING) + 16 * (n // RING + 1))

        def split_high(act, m, loops=0):
            n = N_OF[m]
            wait_landed(act, n, loops)
            if m >= SPLIT:
                act.wait_ge(w_used, loops * MOE_GRAN + m - SPLIT + 1)
            act.copy(w_high[:, m % SPLIT], ring[:, n % RING]).then_inc(high_ready, 1)

        def split_low(dve, m, loops=0):
            n = N_OF[m]
            dve.wait_ge(high_ready, loops * MOE_GRAN + m + 1)
            dve.tensor_tensor(w_low[:, m % SPLIT], ring[:, n % RING], w_high[:, m % SPLIT].bitcast(F32),
                              ALU.subtract).then_inc(low_ready, 1)

        @block.sync
        def _(sp):
            def free_slot(n):
                if n < RING:
                    return
                kind = PLAN[n - RING]
                if kind[0] == "dense":
                    sp.wait_ge(low_ready, kind[1] + 1)
                else:
                    sp.wait_ge(ada_dve, 4 * kind[1] + kind[2] + 1)
                    if kind[1] >= 2:
                        sp.wait_ge(ada_pool, turns(kind[1], kind[2]))

            def load(n):
                free_slot(n)
                sp.dma_start(ring[:, n % RING].rearrange("p k n -> p (k n)"), stream[n]).then_inc(landed[n % RING], 16)

            def load_groups(first, m0, groups):
                with sp.Fori(0, groups) as g:
                    for j in range(MOE_GRAN):
                        sp.wait_ge(low_ready, g * MOE_GRAN + (m0 + j + 1))
                        sp.dma_start(ring[:, (first + j) % RING].rearrange("p k n -> p (k n)"),
                                     stream[g * MOE_GRAN + (first + j)]).then_inc(landed[(first + j) % RING], 16)
                return first + MOE_GRAN * groups

            def load_row(i, key):
                sp.dma_start(rows[:, GATE_ROW[key], :], gate_bias[i:i + 1, :].to_broadcast([P, D])).then_inc(row_s[i], 16)

            sp.dma_start(small[:, :], small_in).then_inc(small_s, 16)
            load(0)
            sp.dma_start(x[:, :, :], x_in.rearrange("(t p) n -> p t n", p=P)).then_inc(x_in_s, 16)
            for n in range(1, N_OF[M_MOE[0]] + RING):
                load(n)
                if n == 4:
                    sp.dma_start(const[:, :], const_in).then_inc(const_s, 16)
                elif n == 8:
                    sp.dma_start(area[:, 4096:5120], decay_in).then_inc(decay_s, 16)
                elif n == 10:
                    load_row(0, (0, G1))
                elif n == 20:
                    load_row(1, (0, G2))
                elif n == 30:
                    load_row(2, (1, G1))
            n = N_OF[M_MOE[0]] + RING
            n = load_groups(n, M_MOE[0], GROUPS)
            sp.wait_ge(x_ready, TT)
            sp.dma_start(rows[:, GATE_ROW[1, G2], :], gate_bias[3:4, :].to_broadcast([P, D])).then_inc(row_s[3], 16)
            while n < N_OF[M_GM + 4]:
                load(n)
                n += 1
            sp.wait_ge(x_ready, 2 * TT)
            sp.dma_start(rows[:, FINAL_ROW, :], final_g.to_broadcast([P, D])).then_inc(row_s[4], 16)
            sp.dma_start(area[:, 6144:6656], mix_w).then_inc(mix_s, 16)
            sp.dma_start(area[:, 6656:7168], mix_b).then_inc(mix_s, 16)
            while n < N_OF[M_MOE[1]] + RING:
                load(n)
                n += 1
            n = load_groups(n, M_MOE[1], GROUPS - 1)
            while n < N_GRAN:
                load(n)
                n += 1
            for t in range(TT):
                sp.wait_ge(out_ready, t + 1)
                sp.dma_start(out[t * P:(t + 1) * P, :], xn[:, t, :]).then_inc(stored, 16)
            sp.wait_ge(stored, 16 * TT)

        @block.tensor
        def _(pe):
            def sum_mod(job, bank):
                pe.wait_ge(ada_dve, 4 * job + 4)
                if job >= 2:
                    pe.wait_ge(ada_pool, turns(job, 3))
                if JOBS[job] in GATE_ROW:
                    for h in range(2):
                        last = pe.matmul(ps[:, bank + h, :], ones[:, :], acc_of(job)[:, h * 512:(h + 1) * 512], start=True, stop=True)
                else:
                    for k in range(KC):
                        last = pe.matmul(ps[:, bank, k:k + 1], acc_of(job)[:, k * P:(k + 1) * P], ones[:, 0:1], start=True, stop=True)
                last.then_inc(mod_summed, 1)

            def turn_xn(stage):
                for t in range(TT):
                    pe.wait_ge(xn_ready, 2 * stage + t + 1)
                    for k in range(KC):
                        last = pe.transpose(ps[:, k // 2, (k % 2) * SEQ + t * P:(k % 2) * SEQ + (t + 1) * P],
                                            xn[:, t, k * P:(k + 1) * P], ident)
                        if t == TT - 1 and k % 2:
                            last.then_inc(xn_turned, 1)

            def dense_rows(m, act_high, act_low, bank, last_one=False):
                pe.wait_ge(low_ready, m + 1)
                for kc, t in ([(0, 0), (1, 0), (0, 1), (1, 1)] if last_one else [(0, 0), (0, 1), (1, 0), (1, 1)]):
                    for a, w in ((act_high(kc, t), w_high), (act_high(kc, t), w_low), (act_low(kc, t), w_high)):
                        for h in range(2):
                            ins = pe.matmul(ps[:, bank + 2 * t + h, :], a, w[:, m % SPLIT, kc, h * 512:(h + 1) * 512],
                                            start=not started[t, h], stop=False, skip_group_check=True)
                            started[t, h] = True
                    if last_one and (kc, t) == (1, 0):
                        ins.then_inc(tile_done, 1)
                return ins

            started = {}

            def begin():
                for t in range(TT):
                    for h in range(2):
                        started[t, h] = False

            def dense_cols(m, bank, first):
                k0 = 2 * (m % 4)
                pe.wait_ge(low_ready, m + 1)
                for kc in range(2):
                    for cc in range(8):
                        for i, (w, a) in enumerate(((w_high, h_high), (w_high, h_low), (w_low, h_high))):
                            ins = pe.matmul(ps[:, bank + cc // 2, (cc % 2) * SEQ:(cc % 2 + 1) * SEQ],
                                            w[:, m % SPLIT, kc, cc * P:(cc + 1) * P], a[:, k0 + kc, :],
                                            start=(first and kc == 0 and i == 0 and cc % 2 == 0), stop=False,
                                            skip_group_check=True)
                return ins

            def rows_of_h(m):
                k0 = 2 * (m % 4)
                return (lambda kc, t: h_high[:, k0 + kc, t * P:(t + 1) * P]), (lambda kc, t: h_low[:, k0 + kc, t * P:(t + 1) * P])

            def rows_of_piece(b):
                return ((lambda kc, t: piece_high[:, b, kc * SEQ + t * P:kc * SEQ + (t + 1) * P]),
                        (lambda kc, t: piece_low[:, b, kc * SEQ + t * P:kc * SEQ + (t + 1) * P]))

            pe.wait_ge(set_up, 1)
            pe.wait_ge(const_s, 16)
            turn_xn(0)
            sum_mod(0, 4)
            sum_mod(1, 5)

            pe.wait_ge(h_low_s, 1)
            pe.wait_ge(mod_stored, 2)
            for i in range(6):
                bank = 4 * (i % 2)
                if i and i - 1 in RET_SUMS:
                    pe.wait_ge(mod_stored, RET_SUMS[i - 1] + 1)
                if i >= 2:
                    pe.wait_ge(group_act, i - 1)
                    pe.wait_ge(group_dve, i - 1)
                if i in (3, 4):
                    pe.wait_ge(prob_ready, 2 * (i - 2))
                begin()
                for j in range(4):
                    m = 4 * i + j
                    if j == 3:
                        if i:
                            pe.wait_ge(group_act, i)
                            pe.wait_ge(group_dve, i)
                        if i in RET_SUMS:
                            sum_mod(RET_SUMS[i], 4 - bank)
                        if i in (2, 3):
                            if i == 2:
                                pe.wait_ge(rot_done, 2 * HEADS)
                            for h in (2 * (i - 2), 2 * (i - 2) + 1):
                                for jt in range(TT):
                                    for c in range(2):
                                        last = pe.matmul(ps[:, 4 - bank + 2 + h % 2, jt * SEQ:(jt + 1) * SEQ],
                                                         qk[:, 1, h, c, jt * P:(jt + 1) * P], qk[:, 0, h, c, :],
                                                         start=(c == 0), stop=(c == 1))
                                last.then_inc(scores_done, 1)
                    if i < 2:
                        last = dense_cols(m, bank, j == 0)
                    else:
                        last = dense_rows(m, *rows_of_h(m), bank)
                    last.then_inc(w_used, 1)

            for h in range(HEADS):
                pe.wait_ge(prob_ready, h + 1)
                if h == 0:
                    pe.wait_ge(group_act, 5)
                    pe.wait_ge(group_dve, 5)
                    pe.wait_ge(mod_stored, 6)
                if h == 2:
                    pe.wait_ge(group_act, 6)
                    pe.wait_ge(group_dve, 6)
                for t in range(TT):
                    for jt in range(TT):
                        last = pe.matmul(ps[:, 2 * h + t, :], prob[:, h, jt * SEQ + t * P:jt * SEQ + (t + 1) * P],
                                         v[:, jt, h * V_DIM:(h + 1) * V_DIM], start=(jt == 0), stop=(jt == 1))
                last.then_inc(o_done, 1)

            def turn_gated(kp):
                for c in range(2):
                    for t in range(TT):
                        last = pe.transpose(ps[:, 4 + kp % 2, c * SEQ + t * P:c * SEQ + (t + 1) * P],
                                            ret_g[:, t, (2 * kp + c) * P:(2 * kp + c + 1) * P], ident)
                last.then_inc(turned, 1)

            pe.wait_ge(o_gated, 6)
            turn_gated(0)
            turn_gated(1)
            pe.wait_ge(o_gated, 2 * HEADS)
            sum_mod(6, 7)
            begin()
            for kp in range(8):
                m = M_RET_OUT + kp
                if kp == 7:
                    sum_mod(7, 6)
                pe.wait_ge(piece_low_s, kp + 1)
                dense_rows(m, *rows_of_piece(kp % 2), 0, kp == 7).then_inc(w_used, 1)
                if kp + 2 < 8:
                    turn_gated(kp + 2)

            def gather(layer, g):
                pe.wait_ge(sel_ready, g + (5 * layer + 1))
                for k in range(KC):
                    for t in range(TT):
                        last = pe.matmul(ps[:, k // 4, (k % 4) * P:(k % 4 + 1) * P], xn[:, t, k * P:(k + 1) * P], sel[:, t, :],
                                         start=(t == 0), stop=(t == 1))
                    if k % 4 == 3:
                        last.then_inc(gather_done, 1)

            def gather_gates(layer, g):
                for t in range(TT):
                    last = pe.matmul(ps[:, 7, SEQ:SEQ + PER_GROUP], sel[:, t, :], own_gates[:, t, :], start=(t == 0), stop=(t == 1))
                last.then_inc(gates_done, 1)

            def experts(layer):
                m0 = M_MOE[layer]
                stage = 2 * layer + 1
                turn_xn(stage)
                for k in range(KC):
                    pe.wait_ge(h_act if k < 4 else h_dve, 4 * stage + k % 4 + 1)
                    for t in range(TT):
                        last = pe.matmul(ps[:, 4, t * N_EXPERTS:(t + 1) * N_EXPERTS], h_all[:, k, t * P:(t + 1) * P],
                                         router_w[:, k, :], start=(k == 0 and t == 0), stop=False, skip_group_check=True)
                last.then_inc(logits_done, 1)
                pe.wait_ge(members_ready, layer + 1)
                members = rt[:, 0, 0:TT * GROUPS]
                pe.matmul(ps[:, 5, 0:GROUPS], upper, members[:, 0:GROUPS], start=True, stop=True)
                pe.matmul(ps[:, 5, GROUPS:2 * GROUPS], upper, members[:, GROUPS:], start=True, stop=False)
                pe.matmul(ps[:, 5, GROUPS:2 * GROUPS], ones[:, :], members[:, 0:GROUPS], start=False, stop=True)\
                    .then_inc(place_done, 1)
                gather(layer, 0)
                pe.wait_ge(route_ready, layer + 1)
                gather_gates(layer, 0)
                for t in range(TT):
                    last = pe.matmul(ps[:, 6, 0:GROUPS], ones[:, :], rt[:, 1, t * GROUPS:(t + 1) * GROUPS],
                                     start=(t == 0), stop=(t == 1))
                last.then_inc(over_counted, 1)

                def scatter_products(done):
                    for i, bank in enumerate((6, 7, 2, 3)):
                        for y in (y_high, y_low):
                            last = pe.matmul(bank_of(bank), sel_t[:, (i // 2) * P:(i // 2 + 1) * P],
                                             y[:, 4 * (i % 2):4 * (i % 2) + 4, :], start=(y is y_high), stop=(y is y_low))
                        last.then_inc(done, 1)

                def scatter(g):
                    pe.wait_ge(y_ready, g * 2 + (2 * GROUPS * layer + 2))
                    pe.wait_ge(sel_t_s, g + (GROUPS * layer + 1))
                    scatter_products(scattered)

                def group(g, first):
                    def up(e, j, s):
                        m = m0 + s
                        pe.wait_ge(low_ready, g * MOE_GRAN + (m + 1))
                        for kc in range(2):
                            k = 2 * j + kc
                            for i, (a, w) in enumerate(((h_high, w_high), (h_high, w_low), (h_low, w_high))):
                                for h in range(2):
                                    last = pe.matmul(ps[:, 2 * (e % 2) + h, :], a[:, k, 0:P],
                                                     w[:, m % SPLIT, kc, h * 512:(h + 1) * 512],
                                                     start=(k == 0 and i == 0), stop=(k == KC - 1 and i == 2))
                        last.then_inc(w_used, 1)

                    def turn_hid(e):
                        pe.wait_ge(hid_ready, g * PER_GROUP + (N_EXPERTS * layer + e + 1))
                        for f in range(4):
                            last = pe.transpose(ps[:, 6, f * P:(f + 1) * P], hid[:, e % 2, f * P:(f + 1) * P], ident)
                        last.then_inc(hid_turned, 1)

                    def down(e, j, s):
                        m = m0 + s
                        if j == 0:
                            pe.wait_ge(hid_low, g * PER_GROUP + (N_EXPERTS * layer + e + 1))
                        pe.wait_ge(low_ready, g * MOE_GRAN + (m + 1))
                        for kc in range(2):
                            f = 2 * j + kc
                            for i, (a, w) in enumerate(((piece_high, w_high), (piece_high, w_low), (piece_low, w_high))):
                                for h in range(2):
                                    last = pe.matmul(ps[:, 4 + h, :], a[:, e % 2, f * P:(f + 1) * P],
                                                     w[:, m % SPLIT, kc, h * 512:(h + 1) * 512],
                                                     start=(e == 0 and f == 0 and i == 0), stop=(e == 3 and f == 3 and i == 2))
                        last.then_inc(w_used, 1)

                    for s, (e, kind, j) in enumerate(MOE_ORDER):
                        if kind == "up":
                            if s == 0:
                                pe.wait_ge(hg_low, g * 2 + (10 * layer + 1))
                            if s == 2:
                                pe.wait_ge(hg_low, g * 2 + (10 * layer + 2))
                            if s == 4:
                                pe.wait_ge(banks_free, g + (5 * layer + 1))
                            up(e, j, s)
                        else:
                            down(e, j, s)
                        if s == 0 and not first:
                            scatter(g - 1)
                        if s == 4:
                            turn_hid(0)
                            for t in range(TT):
                                last = pe.transpose(ps[:, 7, t * P:(t + 1) * P], sel[:, t, :], ident)
                            last.then_inc(sel_turned, 1)
                        elif s in (10, 16, 20):
                            turn_hid({10: 1, 16: 2, 20: 3}[s])
                        if s == 16:
                            gather(layer, g + 1)
                            gather_gates(layer, g + 1)

                group(0, True)
                with pe.Fori(1, GROUPS) as g:
                    group(g, False)
                scatter(GROUPS - 1)

                o = ov[layer]
                pe.wait_ge(over_known, layer + 1)
                flag = pe.value_load(over_i[0:1, 0:1], min_val=0, max_val=1)
                pe.wait_ge(banks_free, 5 * (layer + 1))
                with pe.If(flag > 0):
                    n_w = 0
                    for e in range(PER_GROUP):
                        for j in range(4):
                            n_w += 1
                            pe.wait_ge(o["w"], 16 * n_w)
                            for kc in range(2):
                                k = 2 * j + kc
                                for h in range(2):
                                    last = pe.matmul(ps[:, h, :], gathered[:, k, :], over_w[:, kc, h * 512:(h + 1) * 512],
                                                     start=(k == 0), stop=(k == KC - 1))
                            last.then_inc(o["used"], 1)
                        pe.wait_ge(o["hid"], e + 1)
                        for f in range(4):
                            last = pe.transpose(ps[:, 6, f * P:(f + 1) * P], hid[:, 0, f * P:(f + 1) * P], ident)
                        last.then_inc(o["turned"], 1)
                        pe.wait_ge(o["t_act"], e + 1)
                        for j in range(2):
                            n_w += 1
                            pe.wait_ge(o["w"], 16 * n_w)
                            for kc in range(2):
                                f = 2 * j + kc
                                for h in range(2):
                                    last = pe.matmul(ps[:, 4 + h, :], hid[:, 1, f * P:(f + 1) * P], over_w[:, kc, h * 512:(h + 1) * 512],
                                                     start=(e == 0 and f == 0), stop=(e == 3 and f == 3))
                            last.then_inc(o["used"], 1)
                    for t in range(TT):
                        last = pe.transpose(ps[:, 7, t * P:(t + 1) * P], sel[:, t, :], ident)
                    last.then_inc(o["sel_turned"], 1)
                    pe.wait_ge(o["y_low"], 2)
                    pe.wait_ge(o["sel_t"], 1)
                    scatter_products(o["scattered"])

            experts(0)

            turn_xn(2)
            pe.wait_ge(h_low_s, 2)
            for i in range(3):
                bank = 4 * (i % 2)
                if i == 2:
                    pe.wait_ge(group_act, 7)
                begin()
                for j in range(4):
                    m = M_GM + 4 * i + j
                    if j == 3 and i == 2:
                        pe.wait_ge(group_act, 8)
                        sum_mod(8, 4)
                    dense_rows(m, *rows_of_h(m), bank).then_inc(w_used, 1)
            pe.wait_ge(mod_stored, 9)
            pe.wait_ge(mix_s, 32)
            for g in range(GM_GROUPS):
                last = pe.matmul(ps[:, 4, g * P:(g + 1) * P], ones[:, :], mix_ws[:, g, :], start=True, stop=True)
            last.then_inc(mix_rows_done, 1)
            pe.wait_ge(mix_rows_s, 1)
            for i in range(3):
                for j in range(4):
                    m = M_GM + 12 + 8 * i + j
                    if i >= 1 and j == 0:
                        pe.wait_ge(z_ready, 8 * i)
                        pe.wait_ge(mod_stored, 9 + i)
                    dense_cols(m, 4, j == 0).then_inc(w_used, 1)
                pe.wait_ge(gv_ready, 2)
                for b in range(4):
                    pe.wait_ge(group_act, 4 * i + b + 10)
                    for c in (2 * b, 2 * b + 1):
                        ch = 8 * i + c
                        for t in range(TT):
                            last = pe.matmul(ps[:, 4 + b, (c % 2) * SEQ + t * P:(c % 2) * SEQ + (t + 1) * P],
                                             gv[:, t, ch * P:(ch + 1) * P], mix_ws[:, ch * P // (GM_HALF // GM_GROUPS), :],
                                             start=True, stop=True)
                    last.then_inc(mixed_done, 1)
                if i == 0:
                    pe.wait_ge(group_act, 9)
                    begin()
                for kp in range(4):
                    m = M_GM + 12 + 8 * i + 4 + kp
                    if kp == 3:
                        sum_mod(9 + i, 4)
                    pe.wait_ge(piece_low_s, 8 + 4 * i + kp + 1)
                    dense_rows(m, *rows_of_piece(kp % 2), 0, (i, kp) == (2, 3)).then_inc(w_used, 1)

            experts(1)

        @block.scalar
        def _(act):
            chain = [0]

            def square_and_root(stage):
                act.activation(warm[:, stage:stage + 1], eps[:, :], ACT.Sqrt)
                for t in range(TT):
                    if stage:
                        act.wait_ge(x_ready, TT * (stage - 1) + t + 1)
                    act.activation(xn[:, t, :], x[:, t, :], ACT.Square, accum_out=ssq[:, t:t + 1]).then_inc(squares_done, 1)
                    act.wait_ge(squares_done, 2 * stage + t + 1)
                    act.activation(std[:, t:t + 1], ssq[:, t:t + 1], ACT.Sqrt, scale=1.0 / D, bias=eps[:, :]).then_inc(std_ready, 1)

            def h_of(stage, tmp, to_split):
                layer, which = stage // 2, 2 * (stage % 2)
                act.wait_ge(mod_stored, (2, 5, 8, 11)[stage])
                for k in range(4):
                    act.wait_ge(xn_turned, 4 * stage + k // 2 + 1)
                    act.activation(tmp[:, k, :], ps[:, k // 2, (k % 2) * SEQ:(k % 2 + 1) * SEQ], ACT.Identity,
                                   scale=mod[:, layer, which + 1, k:k + 1], bias=mod[:, layer, which, k:k + 1])\
                       .then_inc(h_act, 1)
                if to_split:
                    act.wait_ge(h_act, 4 * stage + 4)
                    act.copy(h_high[:, 0:4, :], tmp[:, 0:4, :]).then_inc(h_high_s, 1)
                    act.wait_ge(h_dve, 4 * stage + 4)
                    act.copy(h_high[:, 4:8, :], tmp[:, 4:8, :]).then_inc(h_high_s, 1)

            def scale_ada(job, kp):
                n = ADA_OF[job, kp]
                wait_landed(act, n)
                rows_w = ring[:, n % RING, 1, :]
                act.activation(rows_w, rows_w, ACT.Copy, scale=c_act[:, 2 * kp + 1:2 * kp + 2]).then_inc(ada_scaled, 1)

            def step(m):
                split_high(act, m)
                if m in ADA_WITH:
                    scale_ada(*ADA_WITH[m])

            act.wait_ge(small_s, 16)
            act.activation(c_act[:, :], small_of("c"), ACT.Silu).then_inc(c_ready, 1)
            act.wait_ge(c_ready, 1)
            act.wait_ge(x_in_s, 16)
            act.wait_ge(set_up, 1)
            square_and_root(0)
            act.wait_ge(lg_ready, 1)
            act.activation(lg[:, 1, :], lg[:, 0, :], ACT.Exp, scale=-1.0).then_inc(act_chain, 1)
            act.wait_ge(lg_ready, 2)
            act.activation(lg[:, 3, :], lg[:, 2, :], ACT.Ln).then_inc(act_chain, 1)
            h_of(0, h_ret, True)
            step(0)
            step(1)

            for i in range(6):
                for j in range(4):
                    m = 4 * i + j
                    step(m + LEAD)
                    if i == 0 and j < HEADS:
                        act.wait_ge(dist_ready, j + 1)
                        act.activation(prob[:, j, :], prob[:, j, :], ACT.Exp).then_inc(decay_ready, 1)
                if i < 2:
                    act.sem_inc(group_act, 1)
                    continue
                act.wait_ge(w_used, 4 * i + 4)
                bank = 4 * (i % 2)
                if i >= 4:
                    act.wait_ge(prob_ready, HEADS)
                for t, h in ([(0, 0), (0, 1)] if i < 4 else [(0, 0), (0, 1), (1, 0), (1, 1)]):
                    src = ps[:, bank + 2 * t + h, :]
                    at = (i % 2) * COLS + h * 512
                    if i < 4:
                        ins = act.copy(v[:, t, at:at + 512], src)
                    else:
                        ins = act.activation(ret_g[:, t, at:at + 512], src, ACT.Silu)
                ins.then_inc(group_act, 1)

            for kp in range(4):
                scale_ada(6, kp)
            act.activation(warm[:, 5:6], eps[:, :], ACT.Sqrt)
            for h in range(HEADS):
                act.wait_ge(o_done, h + 1)
                for t in range(TT):
                    n = 2 * h + t
                    if n:
                        act.wait_ge(o_squares, n)
                    act.activation(scratch[:, 0, :], ps[:, n, :], ACT.Square, accum_out=ssq[:, n:n + 1]).then_inc(o_squares, 1)
                if h % 2:
                    act.wait_ge(o_squares, 2 * h + 2)
                    two = slice(2 * h - 2, 2 * h + 2)
                    act.activation(std[:, two], ssq[:, two], ACT.Sqrt, scale=1.0 / V_DIM, bias=eps[:, :]).then_inc(o_std, 1)

            def piece_up(n, bank):
                act.wait_ge(turned, n + 1)
                act.copy(piece_high[:, n % 2, :], ps[:, bank, :]).then_inc(piece_high_s, 1)

            piece_up(0, 4)
            piece_up(1, 5)
            for kp in range(8):
                step(M_RET_OUT + kp + LEAD)
                if kp + 2 < 8:
                    piece_up(kp + 2, 4 + kp % 2)

            def experts(layer):
                m0 = M_MOE[layer]
                stage = 2 * layer + 1
                square_and_root(stage)
                h_of(stage, h_all, False)
                act.wait_ge(logits_done, layer + 1)
                act.activation(rt[:, 15, :], ps[:, 4, 0:TT * N_EXPERTS], ACT.Sigmoid).then_inc(scores_ready, 1)

                def gathered_up(g):
                    act.wait_ge(gather_done, g * 2 + (10 * layer + 1))
                    for k in range(4):
                        ins = act.activation(gathered[:, k, :], ps[:, 0, k * P:(k + 1) * P], ACT.Identity,
                                             scale=mod[:, layer, 3, k:k + 1], bias=mod[:, layer, 2, k:k + 1])
                    ins.then_inc(gathered_act, 1)

                def gathered_high(g):
                    act.wait_ge(gathered_act, g + (5 * layer + 1))
                    act.copy(h_high[:, 0:4, 0:P], gathered[:, 0:4, :]).then_inc(hg_high, 1)
                    act.wait_ge(gathered_dve, g + (5 * layer + 1))
                    act.copy(h_high[:, 4:8, 0:P], gathered[:, 4:8, :]).then_inc(hg_high, 1)

                def take_output(g):
                    act.wait_ge(w_used, g * MOE_GRAN + (m0 + MOE_GRAN))
                    for h in range(2):
                        act.copy(y_high[:, 4 * h:4 * h + 4, :], bank_of(4 + h)).then_inc(y_high_s, 1)

                def group(g, first):
                    for s in range(MOE_GRAN):
                        if s == 0 and not first:
                            take_output(g - 1)
                        split_high(act, m0 + s + LEAD, g)
                        if s in (3, 7, 13, 19):
                            e = {3: 0, 7: 1, 13: 2, 19: 3}[s]
                            act.wait_ge(w_used, g * MOE_GRAN + (m0 + s + 1))
                            act.activation(hid[:, e % 2, :], ps[:, 2 * (e % 2), :], ACT.Silu).then_inc(silu_done, 1)
                        if s in (4, 10, 16, 20):
                            e = {4: 0, 10: 1, 16: 2, 20: 3}[s]
                            act.wait_ge(hid_turned, g * PER_GROUP + (N_EXPERTS * layer + e + 1))
                            act.copy(piece_high[:, e % 2, :], ps[:, 6, :]).then_inc(hid_high, 1)
                        if s == 4:
                            act.wait_ge(sel_turned, g + (GROUPS * layer + 1))
                            act.copy(sel_t[:, :], ps[:, 7, 0:SEQ]).then_inc(sel_t_s, 1)
                        if s == 16:
                            gathered_up(g + 1)
                        if s == 20:
                            gathered_high(g + 1)

                gathered_up(0)
                gathered_high(0)
                group(0, True)
                with act.Fori(1, GROUPS) as g:
                    group(g, False)
                take_output(GROUPS - 1)

                o = ov[layer]
                act.wait_ge(over_known, layer + 1)
                flag = act.value_load(over_i[0:1, 0:1], min_val=0, max_val=1)
                group = act.value_load(over_i[0:1, 1:2], min_val=0, max_val=GROUPS - 1)
                with act.If(flag > 0):
                    n_w = 0

                    def load(e, kind, j):
                        nonlocal n_w
                        if n_w:
                            act.wait_ge(o["used"], n_w)
                        n_w += 1
                        at = N_OF[m0] + MOE_ORDER.index((e, kind, j))
                        act.dma_start(area[:, 6144:8192], stream[group * MOE_GRAN + at]).then_inc(o["w"], 16)

                    for e in range(PER_GROUP):
                        for j in range(4):
                            load(e, "up", j)
                        act.wait_ge(o["used"], n_w)
                        act.activation(hid[:, 0, :], ps[:, 0, :], ACT.Silu).then_inc(o["silu"], 1)
                        act.wait_ge(o["turned"], e + 1)
                        act.copy(hid[:, 1, :], ps[:, 6, :]).then_inc(o["t_act"], 1)
                        for j in range(2):
                            load(e, "down", j)
                    act.wait_ge(o["sel_turned"], 1)
                    act.copy(sel_t[:, :], ps[:, 7, 0:SEQ]).then_inc(o["sel_t"], 1)
                    for h in range(2):
                        act.copy(y_high[:, 4 * h:4 * h + 4, :], bank_of(4 + h)).then_inc(o["y_high"], 1)

            experts(0)

            square_and_root(2)
            h_of(2, h_all, True)
            for i in range(3):
                for j in range(4):
                    step(M_GM + 4 * i + j + LEAD)
                act.wait_ge(w_used, M_GM + 4 * i + 4)
                if i == 0:
                    act.wait_ge(h_low_s, 2)
                for t in range(TT):
                    for h in range(2):
                        ins = act.activation(gv[:, t, i * COLS + h * 512:i * COLS + (h + 1) * 512],
                                             ps[:, 4 * (i % 2) + 2 * t + h, :], ACT.Gelu)
                ins.then_inc(group_act, 1)
            for j in range(2):
                step(M_GM + 12 + j + LEAD)
            act.wait_ge(ln_std, 1)
            act.activation(std[:, 0:TT], mean_var[:, :, 1], ACT.Sqrt, bias=eps[:, :]).then_inc(ln_std, 1)
            for i in range(3):
                for j in range(2 if i == 0 else 0, 4):
                    step(M_GM + 12 + 8 * i + j + LEAD)
                act.wait_ge(w_used, M_GM + 12 + 8 * i + 4)
                if i >= 1:
                    act.wait_ge(z_ready, 8 * i)
                for b in range(4):
                    act.activation(u_t[:, 2 * b:2 * b + 2, :], ps[:, 4 + b, :].rearrange("p (k n) -> p k n", k=2),
                                   ACT.Gelu).then_inc(group_act, 1)
                for kp in range(4):
                    act.wait_ge(z_ready, 8 * i + 2 * kp + 2)
                    if kp >= 2 or i:
                        act.wait_ge(w_used, M_GM + 12 + 8 * i + 4 + kp - 2 + 1 if kp >= 2 else M_GM + 12 + 8 * (i - 1) + 8 - 2 + kp + 1)
                    act.copy(piece_high[:, kp % 2, :], u_t[:, 2 * kp:2 * kp + 2, :].rearrange("p k n -> p (k n)"))\
                        .then_inc(piece_high_s, 1)
                    step(M_GM + 12 + 8 * i + 4 + kp + LEAD)

            experts(1)

            square_and_root(4)

        @block.gpsimd
        def _(pool):
            def add_ada(job, kp):
                acc = acc_of(job)
                pool.wait_ge(ada_scaled, turns(job, kp))
                pool.wait_ge(ada_dve, 4 * job + kp + 1)
                pool.tensor_tensor(acc, acc, ring[:, ADA_OF[job, kp] % RING, 1, :], ALU.add).then_inc(ada_pool, 1)

            def mix_rows_plus_bias(first, last):
                pool.wait_ge(mix_rows_s, 1)
                pool.wait_ge(mix_s, 32)
                for ch in range(first, last):
                    g = ch * P // (GM_HALF // GM_GROUPS)
                    if ch >= 4:
                        pool.wait_ge(z_ready, ch - 3)
                    to = mix_add[:, (ch // 2) % 2, (ch % 2) * P:(ch % 2 + 1) * P]
                    pool.tensor_scalar(to, mix_rows[:, g, :], ln_b[:, ch:ch + 1], None, ALU.mult).then_inc(mix_scaled, 1)
                    pool.wait_ge(mix_scaled, ch + 1)
                    pool.tensor_tensor(to, to, mix_bs[:, g, :], ALU.add).then_inc(mix_add_s, 1)

            pool.sem_inc(x_added, 1)
            pool.wait_ge(decay_s, 16)
            pool.wait_ge(lg_ready, 3)
            pool.wait_ge(xn_turned, 4)
            back = scratch[:, 0, :]
            for h in range(HEADS):
                pool.tensor_scalar(prob[:, h, :], dist[:, 0, :], lg[:, 5, h:h + 1], None, ALU.mult).then_inc(pool_chain, 1)
                pool.tensor_scalar(back, dist[:, 1, :], lg[:, 5, HEADS + h:HEADS + h + 1], None, ALU.mult).then_inc(pool_chain, 1)
                pool.wait_ge(pool_chain, 2 * h + 2)
                pool.tensor_tensor(prob[:, h, :], prob[:, h, :], back, ALU.add).then_inc(dist_ready, 1)
                pool.wait_ge(dist_ready, h + 1)
            ada_parts = [(job, kp) for job in range(2, 12) for kp in range(4)]
            for w in range(2):
                while ADA_OF[ada_parts[0]] < N_OF[4 * (w + 1) + LEAD - 1]:
                    add_ada(*ada_parts.pop(0))
                for h in range(HEADS):
                    n = HEADS * w + h
                    pool.wait_ge(rot_ready, n + 1)
                    pool.tensor_tensor(qk[:, w, h, 0, :], rot[:, h % 2, 0, 0:SEQ], rot[:, h % 2, 1, SEQ:], ALU.subtract)
                    pool.tensor_tensor(qk[:, w, h, 1, :], rot[:, h % 2, 1, 0:SEQ], rot[:, h % 2, 0, SEQ:], ALU.add)\
                        .then_inc(rot_done, 1)
            def add_outputs(layer):
                base = 4 * (GROUPS - 1) * layer
                with pool.Fori(0, GROUPS - 1) as g:
                    for i in range(4):
                        t, cols = i // 2, slice((i % 2) * 512, (i % 2 + 1) * 512)
                        pool.wait_ge(scatter_term, g * 4 + (base + i + 1))
                        pool.tensor_tensor(x[:, t, cols], x[:, t, cols], term(i), ALU.add).then_inc(x_added, 1)

            for job, kp in ada_parts:
                if (job, kp) == (8, 0):
                    add_outputs(0)
                add_ada(job, kp)
                if job >= 9 and kp % 2:
                    first = 8 * (job - 9) + 4 * (kp // 2)
                    mix_rows_plus_bias(first, first + 4)
            add_outputs(1)

        @block.vector
        def _(dve):
            links = [0]

            def link(ins):
                links[0] += 1
                ins.then_inc(dve_chain, 1)
                dve.wait_ge(dve_chain, links[0])

            def add_ada(job, kp):
                n = ADA_OF[job, kp]
                wait_landed(dve, n)
                acc = acc_of(job)
                for part in range(2 if job < 2 else 1):
                    rows_w = ring[:, n % RING, part, :]
                    c = c_act[:, 2 * kp + part:2 * kp + part + 1]
                    if kp == 0 and part == 0:
                        if job >= 2:
                            dve.wait_ge(mod_summed, job)
                        ins = dve.tensor_scalar(acc, rows_w, c, None, ALU.mult)
                    else:
                        if part == 0 and job >= 2:
                            dve.wait_ge(ada_pool, turns(job, kp - 1))
                        elif part == 0:
                            dve.wait_ge(ada_dve, 4 * job + kp)
                        ins = dve.scalar_tensor_tensor(acc, rows_w, c, acc, ALU.mult, ALU.add)
                    if job < 2 and part == 0:
                        link(ins)
                    else:
                        ins.then_inc(ada_dve, 1)

            def step(m):
                split_low(dve, m)
                if m in ADA_WITH:
                    add_ada(*ADA_WITH[m])

            def store_mod(job, bank):
                layer, which = JOBS[job]
                dve.wait_ge(mod_summed, job + 1)
                if (layer, which) in GATE_ROW:
                    r = GATE_ROW[layer, which]
                    dve.wait_ge(row_s[2 * layer + (which == G2)], 16)
                    for h in range(2):
                        ins = dve.tensor_tensor(rows[:, r, h * 512:(h + 1) * 512], ps[:, bank + h, :],
                                                rows[:, r, h * 512:(h + 1) * 512], ALU.add)
                    ins.then_inc(mod_stored, 1)
                    return
                to = mod[:, layer, {SH1: 0, SC1: 1, SH2: 2, SC2: 3}[which], :]
                if which in (SH1, SH2):
                    dve.tensor_tensor(to, ps[:, bank, 0:KC], b_ada[:, layer, which, :], ALU.add).then_inc(mod_stored, 1)
                else:
                    link(dve.scalar_tensor_tensor(to, ps[:, bank, 0:KC], 1.0, b_ada[:, layer, which, :], ALU.add, ALU.add))
                    dve.tensor_tensor(to, to, norm_g[:, layer, which // 3, :], ALU.mult).then_inc(mod_stored, 1)

            def scale_x(stage):
                for t in range(TT):
                    dve.wait_ge(std_ready, TT * stage + t + 1)
                    link(dve.reciprocal(rstd[:, t:t + 1], std[:, t:t + 1]))
                    dve.tensor_scalar(xn[:, t, :], x[:, t, :], rstd[:, t:t + 1], None, ALU.mult).then_inc(xn_ready, 1)

            def h_of(stage, tmp, to_split):
                layer, which = stage // 2, 2 * (stage % 2)
                dve.wait_ge(mod_stored, (2, 5, 8, 11)[stage])
                for k in range(4, 8):
                    dve.wait_ge(xn_turned, 4 * stage + k // 2 + 1)
                    dve.tensor_scalar(tmp[:, k, :], ps[:, k // 2, (k % 2) * SEQ:(k % 2 + 1) * SEQ],
                                      mod[:, layer, which + 1, k:k + 1], mod[:, layer, which, k:k + 1], ALU.mult, ALU.add)\
                       .then_inc(h_dve, 1)
                if to_split:
                    for half in range(2):
                        dve.wait_ge(h_high_s, stage + half + 1)
                        ks = slice(4 * half, 4 * half + 4)
                        ins = dve.tensor_tensor(h_low[:, ks, :], tmp[:, ks, :], h_high[:, ks, :].bitcast(F32), ALU.subtract)
                    ins.then_inc(h_low_s, 1)

            def add_output(n, row):
                for i in range(4):
                    t, h = i // 2, i % 2
                    if i == 0:
                        dve.wait_ge(tile_done, n + 1)
                    if i == 2:
                        dve.wait_ge(w_used, (M_RET_OUT + 8, M_GM + 36)[n])
                    cols = slice(h * 512, (h + 1) * 512)
                    link(dve.tensor_tensor(scratch[:, i % 2, :], ps[:, i, :], rows[:, row, cols], ALU.mult))
                    ins = dve.tensor_tensor(x[:, t, cols], x[:, t, cols], scratch[:, i % 2, :], ALU.add)
                    if h:
                        ins.then_inc(x_ready, 1)

            dve.memset(ones[:, :], 1.0)
            dve.memset(eps[:, :], EPS).then_inc(set_up, 1)
            dve.wait_ge(small_s, 16)
            link(dve.tensor_scalar(lg[:, 4, :], decay_logit, -1.0, None, ALU.mult))
            dve.tensor_tensor(lg[:, 0, :], decay_logit, lg[:, 4, :], ALU.max).then_inc(lg_ready, 1)
            dve.wait_ge(c_ready, 1)
            for kp in range(4):
                add_ada(0, kp)
            scale_x(0)
            dve.wait_ge(act_chain, 1)
            dve.tensor_scalar(lg[:, 2, :], lg[:, 1, :], 1.0, None, ALU.add).then_inc(lg_ready, 1)
            for kp in range(4):
                add_ada(1, kp)
            store_mod(0, 4)
            dve.wait_ge(act_chain, 2)
            dve.wait_ge(lg_ready, 2)
            link(dve.tensor_scalar(lg[:, 4, :], lg[:, 2, :], -1.0, None, ALU.add))
            link(dve.tensor_scalar(lg[:, 0, :], lg[:, 4, :], 0.0, None, ALU.is_equal))
            link(dve.tensor_tensor(lg[:, 4, :], lg[:, 4, :], lg[:, 0, :], ALU.add))
            link(dve.tensor_tensor(lg[:, 3, :], lg[:, 3, :], lg[:, 0, :], ALU.add))
            link(dve.reciprocal(lg[:, 4, :], lg[:, 4, :]))
            link(dve.tensor_tensor(lg[:, 3, :], lg[:, 3, :], lg[:, 4, :], ALU.mult))
            link(dve.tensor_tensor(lg[:, 3, :], lg[:, 3, :], lg[:, 1, :], ALU.mult))
            link(dve.tensor_scalar(lg[:, 4, :], decay_logit, 0.0, None, ALU.min))
            dve.tensor_tensor(lg[:, 5, :], lg[:, 4, :], lg[:, 3, :], ALU.subtract).then_inc(lg_ready, 1)
            store_mod(1, 5)
            h_of(0, h_ret, True)
            step(0)
            step(1)

            def probs(i):
                for h in (2 * (i - 2), 2 * (i - 2) + 1):
                    dve.wait_ge(scores_done, h + 1)
                    dve.wait_ge(decay_ready, h + 1)
                    dve.scalar_tensor_tensor(prob[:, h, :], ps[:, 4 - 4 * (i % 2) + 2 + h % 2, :], QK_SCALE, prob[:, h, :],
                                             ALU.mult, ALU.mult).then_inc(prob_ready, 1)

            for i in range(6):
                for j in range(4):
                    step(4 * i + j + LEAD)
                    if j == 3:
                        if i in RET_SUMS:
                            store_mod(RET_SUMS[i], 4 - 4 * (i % 2))
                        if i in (2, 3):
                            probs(i)
                bank = 4 * (i % 2)
                dve.wait_ge(w_used, 4 * i + 4)
                if i == 0:
                    dve.wait_ge(h_low_s, 1)
                if i < 2:
                    for h in range(HEADS):
                        n = HEADS * i + h
                        if n >= 2:
                            dve.wait_ge(rot_done, n - 1)
                        both = ps[:, bank + h, :].rearrange("p (c n) -> p c n", c=2)
                        for w, table in enumerate((cos, sin)):
                            ins = dve.tensor_tensor(rot[:, h % 2, w, :].rearrange("p (c n) -> p c n", c=2), both,
                                                    table.unsqueeze(1).to_broadcast([P, 2, SEQ]), ALU.mult)
                        ins.then_inc(rot_ready, 1)
                    dve.wait_ge(rot_ready, HEADS * i + HEADS)
                    dve.sem_inc(group_dve, 1)
                elif i < 4:
                    if i == 2:
                        dve.wait_ge(rot_done, 2 * HEADS)
                    for h in range(2):
                        at = (i % 2) * COLS + h * 512
                        ins = dve.tensor_copy(v[:, 1, at:at + 512], ps[:, bank + 2 + h, :])
                    ins.then_inc(group_dve, 1)
                else:
                    dve.sem_inc(group_dve, 1)
            for kp in range(4):
                add_ada(6, kp)
            dve.wait_ge(group_act, 6)
            for h in range(HEADS):
                if h % 2 == 0:
                    dve.wait_ge(o_std, h // 2 + 1)
                    two = slice(2 * h, 2 * h + 4)
                    link(dve.reciprocal(rstd[:, two], std[:, two]))
                for t in range(TT):
                    n = 2 * h + t
                    part = ret_g[:, t, h * V_DIM:(h + 1) * V_DIM]
                    dve.scalar_tensor_tensor(part, ps[:, n, :], rstd[:, n:n + 1], part, ALU.mult, ALU.mult).then_inc(o_gated, 1)

            def piece_down(n, bank):
                dve.wait_ge(piece_high_s, n + 1)
                dve.tensor_tensor(piece_low[:, n % 2, :], ps[:, bank, :], piece_high[:, n % 2, :].bitcast(F32), ALU.subtract)\
                   .then_inc(piece_low_s, 1)

            piece_down(0, 4)
            piece_down(1, 5)
            for kp in range(8):
                step(M_RET_OUT + kp + LEAD)
                if kp == 0:
                    store_mod(6, 7)
                if kp == 7:
                    store_mod(7, 6)
                if kp + 2 < 8:
                    piece_down(kp + 2, 4 + kp % 2)
            add_output(0, GATE_ROW[0, G1])

            SC, BI = 15, 14

            def r(i, n=TT * N_EXPERTS):
                return rt[:, i, 0:n]

            def quads(i):
                return rt[:, i, :].rearrange("p (g e) -> p g e", e=PER_GROUP)

            def by_group(i):
                return rt[:, i, 0:TT * GROUPS]

            def spread(i):
                return by_group(i).unsqueeze(2).to_broadcast([P, TT * GROUPS, PER_GROUP])

            def tt(o, a, b, op):
                link(dve.tensor_tensor(o, a, b, op))

            def ts(o, a, s1, op1, s2=None, op2=None):
                link(dve.tensor_scalar(o, a, s1, s2, op1, op2) if op2 is not None else dve.tensor_scalar(o, a, s1, None, op1))

            def find_slots(layer):
                b = quads(BI)
                dve.wait_ge(scores_ready, layer + 1)
                tt(r(BI).rearrange("p (t e) -> p t e", t=TT), r(SC).rearrange("p (t e) -> p t e", t=TT),
                   router_b.unsqueeze(1).to_broadcast([P, TT, N_EXPERTS]), ALU.add)
                tt(by_group(2), b[:, :, 0], b[:, :, 1], ALU.max)
                tt(by_group(3), b[:, :, 0], b[:, :, 1], ALU.min)
                tt(by_group(4), b[:, :, 2], b[:, :, 3], ALU.max)
                tt(by_group(5), b[:, :, 2], b[:, :, 3], ALU.min)
                tt(by_group(6), by_group(2), by_group(4), ALU.max)
                tt(by_group(7), by_group(2), by_group(4), ALU.min)
                tt(by_group(8), by_group(3), by_group(5), ALU.max)
                tt(by_group(7), by_group(7), by_group(8), ALU.max)
                tt(by_group(6), by_group(6), by_group(7), ALU.add)
                sums = by_group(6).rearrange("p (t g) -> p t g", t=TT)
                link(dve.tensor_reduce(rt[:, 7, 0:TT], sums, AX_X, ALU.max))
                tt(by_group(8).rearrange("p (t g) -> p t g", t=TT), sums,
                   rt[:, 7, 0:TT].unsqueeze(2).to_broadcast([P, TT, GROUPS]), ALU.is_equal)
                members = by_group(0).rearrange("p (t g) -> p t g", t=TT)
                is_max = by_group(8).rearrange("p (t g) -> p t g", t=TT)
                left = rt[:, 7, 0:TT]
                ts(left, left, 0.0, ALU.mult, 1.0, ALU.add)
                for g in range(GROUPS):
                    tt(members[:, :, g], is_max[:, :, g], left, ALU.mult)
                    if g + 1 < GROUPS:
                        tt(left, left, members[:, :, g], ALU.subtract)
                dve.memset(done_mark[:, 0:1], 0.0).then_inc(members_ready, 1)
                dve.wait_ge(place_done, layer + 1)
                ts(by_group(12), ps[:, 5, 0:TT * GROUPS], 1.0, ALU.add)
                tt(by_group(12), by_group(12), by_group(0), ALU.mult)
                ts(by_group(1), by_group(12), float(P) + 0.5, ALU.is_gt)
                tt(by_group(13), by_group(12), by_group(1), ALU.mult)
                tt(by_group(12), by_group(12), by_group(13), ALU.subtract)
                link(dve.tensor_scalar(slot_of[:, :, 0:GROUPS], by_group(12).rearrange("p (t g) -> p t g", t=TT),
                                       -1.0, None, ALU.add))

            def find_gates(layer):
                b = quads(BI)
                rank = quads(10)
                for e in range(PER_GROUP):
                    link(dve.memset(rank[:, :, e], float(PER_GROUP - 1 - e)))
                for d in range(1, PER_GROUP):
                    n = PER_GROUP - d
                    c = quads(11)[:, :, 0:n]
                    tt(c, b[:, :, 0:n], b[:, :, d:], ALU.is_ge)
                    tt(rank[:, :, 0:n], rank[:, :, 0:n], c, ALU.subtract)
                    tt(rank[:, :, d:], rank[:, :, d:], c, ALU.add)
                ts(r(10), r(10), 1.5, ALU.is_lt)
                tt(quads(10), quads(10), spread(0), ALU.mult)
                tt(r(10), r(10), r(SC), ALU.mult)
                by_tile = r(10).rearrange("p (t e) -> p t e", t=TT)
                link(dve.tensor_reduce(rt[:, 11, 0:TT], by_tile, AX_X, ALU.add))
                link(dve.reciprocal(rt[:, 11, 0:TT], rt[:, 11, 0:TT]))
                tt(by_tile, by_tile, rt[:, 11, 0:TT].unsqueeze(2).to_broadcast([P, TT, N_EXPERTS]), ALU.mult)
                gates = r(10).rearrange("p (t g e) -> p t e g", t=TT, g=GROUPS)
                link(dve.tensor_reduce(own_gates[:, :, :], gates, AX_X, ALU.add))
                dve.memset(done_mark[:, 1:2], 0.0).then_inc(route_ready, 1)
                link(dve.tensor_reduce(rt[:, 13, 0:TT], by_group(13).rearrange("p (t g) -> p t g", t=TT), AX_X, ALU.add))
                ts(slot_of[:, :, GROUPS], rt[:, 13, 0:TT], -float(P) - 1.0, ALU.add)
                dve.wait_ge(over_counted, layer + 1)
                ts(over_f[:, 0:GROUPS], ps[:, 6, 0:GROUPS], 1.0, ALU.min)
                link(dve.tensor_reduce(over_f[:, 8:9], over_f[:, 0:GROUPS], AX_X, ALU.add))
                link(dve.scalar_tensor_tensor(over_f[:, 5:6], over_f[:, 3:4], 3.0, over_f[:, 1:2], ALU.mult, ALU.add))
                link(dve.scalar_tensor_tensor(over_f[:, 9:10], over_f[:, 2:3], 2.0, over_f[:, 5:6], ALU.mult, ALU.add))
                link(dve.tensor_copy(over_i[:, :], over_f[0:1, 8:10]))
                dve.memset(done_mark[:, 2:3], 0.0).then_inc(over_known, 1)

            def experts(layer):
                m0 = M_MOE[layer]
                stage = 2 * layer + 1
                row = GATE_ROW[layer, G2]
                def choose(g):
                    for t in range(TT):
                        ins = dve.tensor_scalar(sel[:, t, :], iota, slot_of[:, t, bass.ds(g, 1)], None, ALU.is_equal)
                    ins.then_inc(sel_ready, 1)

                scale_x(stage)
                h_of(stage, h_all, False)
                find_slots(layer)
                choose(0)
                find_gates(layer)
                dve.memset(done_mark[:, 3:4], 0.0).then_inc(banks_free, 1)

                def gathered_down(g):
                    dve.wait_ge(gather_done, g * 2 + (10 * layer + 2))
                    for k in range(4, 8):
                        ins = dve.tensor_scalar(gathered[:, k, :], ps[:, 1, (k - 4) * P:(k - 3) * P],
                                                mod[:, layer, 3, k:k + 1], mod[:, layer, 2, k:k + 1], ALU.mult, ALU.add)
                    ins.then_inc(gathered_dve, 1)

                def gathered_low(g):
                    for half in range(2):
                        dve.wait_ge(hg_high, g * 2 + (10 * layer + half + 1))
                        ks = slice(4 * half, 4 * half + 4)
                        dve.tensor_tensor(h_low[:, ks, 0:P], gathered[:, ks, :], h_high[:, ks, 0:P].bitcast(F32), ALU.subtract)\
                           .then_inc(hg_low, 1)
                    dve.wait_ge(gates_done, g + (5 * layer + 1))
                    dve.tensor_copy(slot_gates[:, :], ps[:, 7, SEQ:SEQ + PER_GROUP])

                def rest_of_output(h):
                    ks = slice(4 * h, 4 * h + 4)
                    return dve.tensor_tensor(y_low[:, ks, :], bank_of(4 + h), y_high[:, ks, :].bitcast(F32), ALU.subtract)

                def take_output(g):
                    for h in range(2):
                        dve.wait_ge(y_high_s, g * 2 + (2 * GROUPS * layer + h + 1))
                        rest_of_output(h).then_inc(y_ready, 1)

                def scale_scattered(g):
                    dve.wait_ge(x_added, g * 4 + (4 * (GROUPS - 1) * layer + 1))
                    for i, bank in enumerate((6, 7, 2, 3)):
                        dve.wait_ge(scattered, g * 4 + (4 * GROUPS * layer + i + 1))
                        ins = dve.tensor_tensor(term(i), ps[:, bank, :], rows[:, row, (i % 2) * 512:(i % 2 + 1) * 512], ALU.mult)
                        ins.then_inc(scatter_term, 1)
                    dve.wait_ge(scatter_term, g * 4 + (4 * (GROUPS - 1) * layer + 4))
                    dve.sem_inc(banks_free, 1)

                def group(g, first):
                    for s in range(MOE_GRAN):
                        if s == 0 and not first:
                            take_output(g - 1)
                        split_low(dve, m0 + s + LEAD, g)
                        if s == 1 and not first:
                            scale_scattered(g - 1)
                        if s in (3, 7, 13, 19):
                            e = {3: 0, 7: 1, 13: 2, 19: 3}[s]
                            dve.wait_ge(silu_done, g * PER_GROUP + (N_EXPERTS * layer + e + 1))
                            dve.scalar_tensor_tensor(hid[:, e % 2, :], hid[:, e % 2, :], slot_gates[:, e:e + 1],
                                                     ps[:, 2 * (e % 2) + 1, :], ALU.mult, ALU.mult).then_inc(hid_ready, 1)
                        if s in (4, 10, 16, 20):
                            e = {4: 0, 10: 1, 16: 2, 20: 3}[s]
                            dve.wait_ge(hid_high, g * PER_GROUP + (N_EXPERTS * layer + e + 1))
                            dve.tensor_tensor(piece_low[:, e % 2, :], ps[:, 6, :], piece_high[:, e % 2, :].bitcast(F32),
                                              ALU.subtract).then_inc(hid_low, 1)
                        if s == 4:
                            dve.wait_ge(sel_turned, g + (GROUPS * layer + 1))
                            choose(g + 1)
                        if s == 16:
                            gathered_down(g + 1)
                        if s == 20:
                            gathered_low(g + 1)

                gathered_down(0)
                gathered_low(0)
                group(0, True)
                with dve.Fori(1, GROUPS) as g:
                    group(g, False)
                take_output(GROUPS - 1)
                dve.wait_ge(x_added, 4 * (GROUPS - 1) * (layer + 1) + 1)

                o = ov[layer]
                flag = dve.value_load(over_i[0:1, 0:1], min_val=0, max_val=1)
                for i, bank in enumerate((6, 7, 2, 3)):
                    t, cols = i // 2, slice((i % 2) * 512, (i % 2 + 1) * 512)
                    dve.wait_ge(scattered, 4 * GROUPS * (layer + 1) - 3 + i)
                    link(dve.tensor_tensor(term(i), ps[:, bank, :], rows[:, row, cols], ALU.mult))
                    link(dve.tensor_tensor(x[:, t, cols], x[:, t, cols], term(i), ALU.add))
                    if i % 2:
                        with dve.If(flag < 1):
                            dve.sem_inc(x_ready, 1)
                dve.sem_inc(banks_free, 1)
                with dve.If(flag > 0):
                    for e in range(PER_GROUP):
                        dve.wait_ge(o["silu"], e + 1)
                        dve.scalar_tensor_tensor(hid[:, 0, :], hid[:, 0, :], slot_gates[:, e:e + 1], ps[:, 1, :],
                                                 ALU.mult, ALU.mult).then_inc(o["hid"], 1)
                    dve.wait_ge(o["sel_turned"], 1)
                    for h in range(2):
                        dve.wait_ge(o["y_high"], h + 1)
                        rest_of_output(h).then_inc(o["y_low"], 1)
                    for i, bank in enumerate((6, 7, 2, 3)):
                        t, cols = i // 2, slice((i % 2) * 512, (i % 2 + 1) * 512)
                        dve.wait_ge(o["scattered"], i + 1)
                        dve.tensor_tensor(term(i), ps[:, bank, :], rows[:, row, cols], ALU.mult).then_inc(o["term"], 1)
                        dve.wait_ge(o["term"], i + 1)
                        dve.tensor_tensor(x[:, t, cols], x[:, t, cols], term(i), ALU.add).then_inc(o["term_added"], 1)
                    dve.wait_ge(o["term_added"], 4)
                    dve.sem_inc(x_ready, TT)

            experts(0)

            scale_x(2)
            h_of(2, h_all, True)
            for i in range(3):
                for j in range(4):
                    step(M_GM + 4 * i + j + LEAD)
                if i == 2:
                    store_mod(8, 4)
                dve.wait_ge(group_act, 7 + i)
                for t in range(TT):
                    for h in range(2):
                        ins = dve.bn_stats(bn[:, t, 2 * i + h, :], gv[:, t, i * COLS + h * 512:i * COLS + (h + 1) * 512])
            link(ins)
            for t in range(TT):
                ins = dve.bn_aggr(mean_var[:, t, :], bn[:, t, :, :])
            ins.then_inc(ln_std, 1)
            dve.wait_ge(mix_rows_done, 1)
            dve.tensor_copy(mix_rows, ps[:, 4, :].rearrange("p (g n) -> p g n", g=GM_GROUPS)).then_inc(mix_rows_s, 1)
            for j in range(2):
                step(M_GM + 12 + j + LEAD)
            dve.wait_ge(ln_std, 2)
            link(dve.reciprocal(rstd[:, 0:TT], std[:, 0:TT]))
            for t in range(TT):
                dve.tensor_scalar(gv[:, t, :], gv[:, t, :], mean_var[:, t, 0:1], rstd[:, t:t + 1], ALU.subtract, ALU.mult)\
                   .then_inc(gv_ready, 1)
            for i in range(3):
                for j in range(2 if i == 0 else 0, 4):
                    step(M_GM + 12 + 8 * i + j + LEAD)
                for kp in range(4):
                    dve.wait_ge(mixed_done, 4 * i + kp + 1)
                    for c in (2 * kp, 2 * kp + 1):
                        ch = 8 * i + c
                        half = slice((c % 2) * SEQ, (c % 2 + 1) * SEQ)
                        tmp = scratch[:, c % 2, 0:SEQ]
                        dve.wait_ge(mix_add_s, ch + 1)
                        added = mix_add[:, (ch // 2) % 2, (ch % 2) * P:(ch % 2 + 1) * P].unsqueeze(1).to_broadcast([P, TT, P])
                        link(dve.scalar_tensor_tensor(tmp.rearrange("p (t n) -> p t n", t=TT),
                                                      ps[:, 4 + kp, half].rearrange("p (t n) -> p t n", t=TT),
                                                      ln_g[:, ch:ch + 1], added, ALU.mult, ALU.add))
                        dve.tensor_tensor(u_t[:, c, :], u_t[:, c, :], tmp, ALU.mult).then_inc(z_ready, 1)
                    dve.wait_ge(piece_high_s, 8 + 4 * i + kp + 1)
                    dve.tensor_tensor(piece_low[:, kp % 2, :], u_t[:, 2 * kp:2 * kp + 2, :].rearrange("p k n -> p (k n)"),
                                      piece_high[:, kp % 2, :].bitcast(F32), ALU.subtract).then_inc(piece_low_s, 1)
                    step(M_GM + 12 + 8 * i + 4 + kp + LEAD)
                store_mod(9 + i, 4)
            add_output(1, GATE_ROW[1, G1])

            experts(1)

            dve.wait_ge(row_s[4], 16)
            for t in range(TT):
                dve.wait_ge(std_ready, 4 * TT + t + 1)
                link(dve.reciprocal(rstd[:, t:t + 1], std[:, t:t + 1]))
                dve.scalar_tensor_tensor(xn[:, t, :], x[:, t, :], rstd[:, t:t + 1], rows[:, FINAL_ROW, :], ALU.mult, ALU.mult)\
                   .then_inc(out_ready, 1)


def _granules(w):
    k, n = w.shape
    return w.reshape(k // 256, 2, 128, n // COLS, COLS).transpose(3, 0, 2, 1, 4).reshape(n // COLS, k // 256, 128, GRAN)


def _columns(a):
    return a.reshape(-1, 128).T


def kernel(**inputs):
    import numpy as np
    import concourse.bacc as bacc
    from concourse.bass_utils import run_bass_kernel_spmd as run

    inp = {k: np.asarray(a) for k, a in inputs.items()}
    ada = [_granules(inp["w_ada"][layer]) for layer in range(2)]
    ret_in, ret_out = _granules(inp["ret_w_in"][0]), _granules(inp["ret_w_out"][0])
    gm_in, gm_out = _granules(inp["gm_w_in"][0]), _granules(inp["gm_w_out"][0])
    dense = [ret_in[i, j] for i in range(6) for j in range(4)] + [ret_out[0, j] for j in range(8)]

    def expert_granules(layer):
        out = []
        for g in range(GROUPS):
            for e, kind, j in MOE_ORDER:
                w = inp["moe_w_gate_up" if kind == "up" else "moe_w_down"][layer, g * PER_GROUP + e]
                out.append(w[j * 256:(j + 1) * 256].reshape(2, 128, COLS).transpose(1, 0, 2).reshape(128, GRAN))
        return out

    dense += expert_granules(0)
    dense += [gm_in[3 + i, j] for i in range(3) for j in range(4)]
    for i in range(3):
        dense += [gm_in[i, j] for j in range(4)] + [gm_out[0, 4 * i + j] for j in range(4)]
    dense += expert_granules(1)
    dense += [dense[0]] * LEAD
    stream = np.empty((N_GRAN, 128, GRAN), np.float32)
    for n, p in enumerate(PLAN):
        stream[n] = dense[p[1]] if p[0] == "dense" else ada[JOBS[p[1]][0]][JOBS[p[1]][1], p[2]]

    def over_partitions(a):
        return np.broadcast_to(a.reshape(1, -1), (128, a.size))

    small = np.concatenate([
        _columns(inp["c"]), _columns(inp["b_ada"]), _columns(inp["norm_g"]),
        inp["router_w"].reshape(KC, 128, N_EXPERTS).transpose(1, 0, 2).reshape(128, -1),
        over_partitions(inp["router_b"]), over_partitions(inp["ret_decay_logit"][0]),
        _columns(inp["gm_ln_g"]), _columns(inp["gm_ln_b"])], axis=1)
    at = np.arange(128)
    half = D // HEADS // 2
    freq = (np.float32(10000.0) ** (-np.arange(half, dtype=np.float32) / np.float32(half))).astype(np.float32)
    angle = freq[:, None] * np.arange(SEQ, dtype=np.float32)[None, :]
    const = np.concatenate([np.eye(128), at[:, None] < at[None, :], np.broadcast_to(at, (128, 128)),
                            np.cos(angle), np.sin(angle)], axis=1).astype(np.float32)
    j_at = (np.arange(TT)[None, :, None] * 128 + at[:, None, None])
    dist = np.arange(SEQ)[None, None, :] - j_at
    decay = np.stack([np.maximum(dist, 0), np.maximum(-dist, 0)], axis=1).reshape(128, -1).astype(np.float32)
    b_ada = inp["b_ada"]
    gate_bias = np.stack([b_ada[0, 2 * D:3 * D], b_ada[0, 5 * D:], b_ada[1, 2 * D:3 * D], b_ada[1, 5 * D:]])
    mix_w = inp["gm_w_s"][0].transpose(2, 0, 1).reshape(128, -1)
    arrays = {
        "stream": stream, "x": inp["x"].reshape(SEQ, D), "small": small, "const": const, "decay_dist": decay,
        "gate_bias": gate_bias, "final_g": inp["final_g"].reshape(1, D), "mix_w": mix_w, "mix_b": over_partitions(inp["gm_b_s"][0]),
    }
    arrays = {k: np.ascontiguousarray(a) for k, a in arrays.items()}
    nc = bacc.Bacc("TRN2", target_bir_lowering=False, num_devices=1)
    aps = [nc.dram_tensor(f"{k}_dram", a.shape, mybir.dt.from_np(a.dtype), kind="ExternalInput").ap() for k, a in arrays.items()]
    out = nc.dram_tensor("out_dram", (SEQ, D), F32, kind="ExternalOutput").ap()
    trunk_kernel(nc, *aps, out)
    r = run(nc, [{f"{k}_dram": a for k, a in arrays.items()}], core_ids=[0])
    return r.results[0]["out_dram"].reshape(1, SEQ, D)
```

```python
from contextlib import ExitStack

import concourse.bass as bass
from concourse import mybir

F32 = mybir.dt.float32
F32R = mybir.dt.float32r
I32 = mybir.dt.int32
ALU = mybir.AluOpType
ACT = mybir.ActivationFunctionType
AX_X = mybir.AxisListType.X

P = 128
D = 1024
SEQ = 256
TT = SEQ // P
KC = D // P
EPS = 1e-6
HEADS = 4
V_DIM = 512
QK_SCALE = (D // HEADS) ** -0.5
GM_HALF = 3072
GM_GROUPS = 4
GROUPS = 4
PER_GROUP = 4
N_EXPERTS = GROUPS * PER_GROUP

COLS = 1024
GRAN = 2 * COLS
RING = 6
SPLIT = 3
LEAD = SPLIT - 1
MOE_GRAN = 6 * PER_GROUP
MOE_ORDER = ([(0, "up", j) for j in range(4)] + [(1, "up", j) for j in range(4)] + [(0, "down", j) for j in range(2)]
             + [(2, "up", j) for j in range(4)] + [(1, "down", j) for j in range(2)]
             + [(3, "up", j) for j in range(4)] + [(2, "down", j) for j in range(2)]
             + [(3, "down", j) for j in range(2)])

SMALL = {}
_at = 0
for _name, _n in (("c", KC), ("b_ada", 2 * 6 * KC), ("norm_g", 2 * 2 * KC), ("router_w", KC * N_EXPERTS),
                  ("router_b", N_EXPERTS), ("decay", 2 * HEADS), ("ln_g", GM_HALF // P), ("ln_b", GM_HALF // P)):
    SMALL[_name] = (_at, _n)
    _at += _n
SMALL_N = _at


def stream_plan():
    plan = []
    m = 0

    def ada(jobs):
        return [("ada", job, kp) for job in jobs for kp in range(4)]

    def dense(n, parts=(), before=()):
        nonlocal m
        parts = list(parts)
        for i in range(n):
            for _ in range(list(before).count(i)):
                plan.append(parts.pop(0))
            plan.append(("dense", m))
            m += 1
        assert not parts

    plan += ada((0, 1))
    dense(24 + 8, ada(range(2, 8)), (4, 6, 8, 10, 12, 13, 14, 15, 16, 17, 18, 19, 20, 21, 22, 23) + 4 * (26,) + (27, 28, 29, 30))
    dense(4 * MOE_GRAN)
    dense(12 + 3 * 8, ada(range(8, 12)), range(4, 36, 2))
    dense(4 * MOE_GRAN)
    dense(LEAD)
    return plan


PLAN = stream_plan()
N_GRAN = len(PLAN)
N_OF = {p[1]: n for n, p in enumerate(PLAN) if p[0] == "dense"}
ADA_OF = {(p[1], p[2]): n for n, p in enumerate(PLAN) if p[0] == "ada"}
ADA_WITH = {p[1]: PLAN[n - 1][1:] for n, p in enumerate(PLAN)
            if p[0] == "dense" and n and PLAN[n - 1][0] == "ada" and PLAN[n - 1][1] not in (1, 6)}

M_RET_OUT = 24
M_MOE = (32, 32 + 96 + 36)
M_GM = 32 + 96
assert MOE_GRAN % RING == 0 and MOE_GRAN % SPLIT == 0

SH1, SC1, G1, SH2, SC2, G2 = range(6)
JOBS = [(layer, which) for layer in range(2) for which in (SH1, SC1, G1, SH2, SC2, G2)]
RET_SUMS = {2: 2, 3: 3, 4: 4, 5: 5}
GATE_ROW = {(0, G1): 0, (0, G2): 1, (1, G1): 2, (1, G2): 0}
FINAL_ROW = 1


def trunk_kernel(nc: bass.Bass, stream: bass.AP, x_in: bass.AP, small_in: bass.AP, const_in: bass.AP, decay_in: bass.AP,
                 gate_bias: bass.AP, final_g: bass.AP, mix_w: bass.AP, mix_b: bass.AP, out: bass.AP):
    with ExitStack() as ctx:
        def sb(name, shape, dt=F32):
            return ctx.enter_context(nc.sbuf_tensor(name, shape, dt))

        def sem(name):
            return ctx.enter_context(nc.semaphore(name))

        ring = sb("ring", [P, RING, 2, COLS])
        w_high = sb("w_high", [P, SPLIT, 2, COLS], F32R)
        w_low = sb("w_low", [P, SPLIT, 2, COLS], F32R)
        ada_acc = sb("ada_acc", [P, COLS])
        x = sb("x", [P, TT, D])
        xn = sb("xn", [P, TT, D])
        h_high = sb("h_high", [P, KC, SEQ], F32R)
        h_low = sb("h_low", [P, KC, SEQ], F32R)
        piece_high = sb("piece_high", [P, 2, 512], F32R)
        piece_low = sb("piece_low", [P, 2, 512], F32R)
        rows = sb("rows", [P, 3, D])
        small = sb("small", [P, SMALL_N])
        const = sb("const", [P, 3 * P + 2 * SEQ])
        scratch = sb("scratch", [P, 2, 512])
        mixture = sb("mixture", [P, 2, 512])
        sel = sb("sel", [P, TT, P])
        sel_t = sb("sel_t", [P, SEQ], F32R)
        area = sb("area", [P, 8192])
        ones = sb("ones", [P, P])
        mod = sb("mod", [P, 2, 4, KC])
        c_act = sb("c_act", [P, KC])
        eps = sb("eps", [P, 1])
        warm = sb("warm", [P, 6])
        ssq = sb("ssq", [P, 8])
        std = sb("std", [P, 8])
        rstd = sb("rstd", [P, 8])
        lg = sb("lg", [P, 6, 2 * HEADS])
        bn = sb("bn", [P, TT, 6, 6])
        mean_var = sb("mean_var", [P, TT, 2])
        rt = sb("rt", [P, 16, TT * N_EXPERTS])
        own_gates = sb("own_gates", [P, TT, PER_GROUP])
        slot_of = sb("slot_of", [P, TT, GROUPS + 1])
        slot_gates = sb("slot_gates", [P, PER_GROUP])
        over_f = sb("over_f", [P, 16])
        over_i = sb("over_i", [1, 2], I32)
        done_mark = sb("done_mark", [P, 4])

        ps = ctx.enter_context(nc.psum_tensor("ps", [P, 8, 512], F32))

        ident, upper, iota = (const[:, i * P:(i + 1) * P] for i in range(3))
        cos, sin = (const[:, 3 * P + i * SEQ:3 * P + (i + 1) * SEQ] for i in range(2))

        def acc_of(job):
            return area[:, 0:COLS] if job == 1 else ada_acc[:, :]

        def small_of(name):
            a, n = SMALL[name]
            return small[:, a:a + n]

        b_ada = small_of("b_ada").rearrange("p (l w k) -> p l w k", l=2, w=6)
        norm_g = small_of("norm_g").rearrange("p (l w k) -> p l w k", l=2, w=2)
        router_w = small_of("router_w").rearrange("p (k e) -> p k e", k=KC)
        router_b = small_of("router_b")
        decay_logit = small_of("decay")
        ln_g, ln_b = small_of("ln_g"), small_of("ln_b")
        qk = area[:, 0:4096].rearrange("p (w h c n) -> p w h c n", w=2, h=HEADS, c=2)
        ret_g = area[:, 0:4096].rearrange("p (t n) -> p t n", t=TT)
        v = area[:, 4096:8192].rearrange("p (t n) -> p t n", t=TT)
        dist = area[:, 4096:5120].rearrange("p (w n) -> p w n", w=2)
        rot = area[:, 5120:7168].rearrange("p (b w n) -> p b w n", b=2, w=2)
        h_ret = area[:, 5120:7168].rearrange("p (k n) -> p k n", k=KC)
        prob = xn[:, :, :].rearrange("p t n -> p (t n)").rearrange("p (h n) -> p h n", h=HEADS)
        h_all = area[:, 0:2048].rearrange("p (k n) -> p k n", k=KC)
        gv = area[:, 0:6144].rearrange("p (t n) -> p t n", t=TT)
        mix_ws = area[:, 6144:6656].rearrange("p (g n) -> p g n", g=GM_GROUPS)
        mix_bs = area[:, 6656:7168].rearrange("p (g n) -> p g n", g=GM_GROUPS)
        mix_rows = area[:, 7168:7680].rearrange("p (g n) -> p g n", g=GM_GROUPS)
        mix_add = area[:, 7680:8192].rearrange("p (b n) -> p b n", b=2)
        def mixed(c):
            place = scratch if c < 4 else mixture
            return place[:, (c % 4) // 2, (c % 2) * SEQ:(c % 2 + 1) * SEQ]

        u_t = xn[:, :, :].rearrange("p t n -> p (t n)").rearrange("p (k n) -> p k n", k=KC)
        gathered = area[:, 2048:3072].rearrange("p (k n) -> p k n", k=KC)
        y_high, y_low = h_high[:, :, P:SEQ], h_low[:, :, P:SEQ]
        hid = area[:, 4096:5120].rearrange("p (b n) -> p b n", b=2)
        more_terms = area[:, 5120:6144].rearrange("p (b n) -> p b n", b=2)

        def bank_of(bank):
            return ps[:, bank, :].rearrange("p (k n) -> p k n", k=4)

        def term(i):
            return scratch[:, i, :] if i < 2 else more_terms[:, i - 2, :]
        over_w = area[:, 6144:8192].rearrange("p (k n) -> p k n", k=2)

        landed = [sem(f"landed{i}") for i in range(RING)]
        x_in_s, small_s, const_s, decay_s = sem("x_landed"), sem("small_landed"), sem("const_landed"), sem("decay_landed")
        tables_s = sem("tables_landed")
        row_s = [sem(f"row_landed{i}") for i in range(5)]
        mix_s = sem("mix_landed")
        high_ready, low_ready = sem("high_ready"), sem("low_ready")
        w_used = sem("w_used")
        ada_dve, ada_pool, ada_scaled = sem("ada_dve"), sem("ada_pool"), sem("ada_scaled")
        set_up, c_ready = sem("set_up"), sem("c_ready")
        mod_summed, mod_stored = sem("mod_summed"), sem("mod_stored")
        squares_done, std_ready, rstd_ready, xn_ready = sem("squares_done"), sem("std_ready"), sem("rstd_ready"), sem("xn_ready")
        xn_turned, h_act, h_dve, h_high_s, h_low_s = sem("xn_turned"), sem("h_act"), sem("h_dve"), sem("h_high_s"), sem("h_low_s")
        x_ready, tile_done = sem("x_ready"), sem("tile_done")
        group_act, group_dve = sem("group_act"), sem("group_dve")
        dve_chain, act_chain, pool_chain = sem("dve_chain"), sem("act_chain"), sem("pool_chain")
        rot_ready, rot_done = sem("rot_ready"), sem("rot_done")
        lg_ready, dist_ready, decay_ready = sem("lg_ready"), sem("dist_ready"), sem("decay_ready")
        scores_done, prob_ready = sem("scores_done"), sem("prob_ready")
        o_done, o_squares, o_std, o_rstd, o_gated = sem("o_done"), sem("o_squares"), sem("o_std"), sem("o_rstd"), sem("o_gated")
        turned, piece_high_s, piece_low_s = sem("turned"), sem("piece_high_s"), sem("piece_low_s")
        ln_std, ln_rstd, gv_ready = sem("ln_std"), sem("ln_rstd"), sem("gv_ready")
        mix_taken = sem("mix_taken")
        mixed_done, mix_rows_done, mix_rows_s, mix_add_s = sem("mixed_done"), sem("mix_rows_done"), sem("mix_rows_s"), sem("mix_add_s")
        mix_scaled = sem("mix_scaled")
        z_ready = sem("z_ready")
        logits_done, scores_ready, place_done, route_ready = sem("logits_done"), sem("scores_ready"), sem("place_done"), sem("route_ready")
        members_ready, over_counted, over_known = sem("members_ready"), sem("over_counted"), sem("over_known")
        sel_ready, sel_turned, sel_t_s = sem("sel_ready"), sem("sel_turned"), sem("sel_t_s")
        gates_done, scores_by_expert = sem("gates_done"), sem("scores_by_expert")
        gather_done, gathered_act, gathered_dve, hg_high, hg_low = sem("gather_done"), sem("gathered_act"), sem("gathered_dve"), sem("hg_high"), sem("hg_low")
        silu_done, hid_ready = sem("silu_done"), sem("hid_ready")
        hid_turned, hid_high, hid_low = sem("hid_turned"), sem("hid_high"), sem("hid_low")
        y_high_s, y_ready = sem("y_high_s"), sem("y_ready")
        scattered, scatter_term, x_added, banks_free = sem("scattered"), sem("scatter_term"), sem("x_added"), sem("banks_free")
        ov = [{n: sem(f"over{layer}_{n}") for n in ("w", "used", "silu", "hid", "turned", "t_act", "y_high", "y_low", "sel_turned",
                                                    "sel_t", "scattered", "term", "term_added")} for layer in range(2)]
        out_ready, stored = sem("out_ready"), sem("stored")

        block = ctx.enter_context(nc.Block())

        def turns(job, kp):
            return 4 * (job - 2) + kp + 1

        def wait_landed(eng, n, loops=0):
            eng.wait_ge(landed[n % RING], loops * (16 * MOE_GRAN // RING) + 16 * (n // RING + 1))

        def split_high(act, m, loops=0):
            n = N_OF[m]
            wait_landed(act, n, loops)
            if m >= SPLIT:
                act.wait_ge(w_used, loops * MOE_GRAN + m - SPLIT + 1)
            act.copy(w_high[:, m % SPLIT], ring[:, n % RING]).then_inc(high_ready, 1)

        def split_low(dve, m, loops=0):
            n = N_OF[m]
            dve.wait_ge(high_ready, loops * MOE_GRAN + m + 1)
            dve.tensor_tensor(w_low[:, m % SPLIT], ring[:, n % RING], w_high[:, m % SPLIT].bitcast(F32),
                              ALU.subtract).then_inc(low_ready, 1)

        @block.sync
        def _(sp):
            def free_slot(n):
                if n < RING:
                    return
                kind = PLAN[n - RING]
                if kind[0] == "dense":
                    sp.wait_ge(low_ready, kind[1] + 1)
                else:
                    sp.wait_ge(ada_dve, 4 * kind[1] + kind[2] + 1)
                    if kind[1] >= 2:
                        sp.wait_ge(ada_pool, turns(kind[1], kind[2]))

            def load(n):
                free_slot(n)
                sp.dma_start(ring[:, n % RING].rearrange("p k n -> p (k n)"), stream[n]).then_inc(landed[n % RING], 16)

            def load_groups(first, m0, groups):
                with sp.Fori(0, groups) as g:
                    for j in range(MOE_GRAN):
                        sp.wait_ge(low_ready, g * MOE_GRAN + (m0 + j + 1))
                        sp.dma_start(ring[:, (first + j) % RING].rearrange("p k n -> p (k n)"),
                                     stream[g * MOE_GRAN + (first + j)]).then_inc(landed[(first + j) % RING], 16)
                return first + MOE_GRAN * groups

            def load_row(i, key):
                sp.dma_start(rows[:, GATE_ROW[key], :], gate_bias[i:i + 1, :].to_broadcast([P, D])).then_inc(row_s[i], 16)

            sp.dma_start(small[:, :], small_in).then_inc(small_s, 16)
            load(0)
            sp.dma_start(x[:, :, :], x_in.rearrange("(t p) n -> p t n", p=P)).then_inc(x_in_s, 16)
            for n in range(1, N_OF[M_MOE[0]] + RING):
                load(n)
                if n == 4:
                    sp.dma_start(const[:, 0:P], const_in[:, 0:P]).then_inc(const_s, 16)
                elif n == 9:
                    sp.dma_start(const[:, P:], const_in[:, P:]).then_inc(tables_s, 16)
                    sp.dma_start(area[:, 4096:5120], decay_in).then_inc(decay_s, 16)
                elif n == 10:
                    load_row(0, (0, G1))
                elif n == 20:
                    load_row(1, (0, G2))
                elif n == 30:
                    load_row(2, (1, G1))
            n = N_OF[M_MOE[0]] + RING
            n = load_groups(n, M_MOE[0], GROUPS)
            sp.wait_ge(x_ready, TT)
            sp.dma_start(rows[:, GATE_ROW[1, G2], :], gate_bias[3:4, :].to_broadcast([P, D])).then_inc(row_s[3], 16)
            while n < N_OF[M_GM + 4]:
                load(n)
                n += 1
            sp.wait_ge(x_ready, 2 * TT)
            sp.dma_start(rows[:, FINAL_ROW, :], final_g.to_broadcast([P, D])).then_inc(row_s[4], 16)
            sp.dma_start(area[:, 6144:6656], mix_w).then_inc(mix_s, 16)
            sp.dma_start(area[:, 6656:7168], mix_b).then_inc(mix_s, 16)
            while n < N_OF[M_MOE[1]] + RING:
                load(n)
                n += 1
            n = load_groups(n, M_MOE[1], GROUPS - 1)
            while n < N_GRAN:
                load(n)
                n += 1
            for t in range(TT):
                sp.wait_ge(out_ready, t + 1)
                sp.dma_start(out[t * P:(t + 1) * P, :], xn[:, t, :]).then_inc(stored, 16)
            sp.wait_ge(stored, 16 * TT)

        @block.tensor
        def _(pe):
            def sum_mod(job, bank):
                pe.wait_ge(ada_dve, 4 * job + 4)
                if job >= 2:
                    pe.wait_ge(ada_pool, turns(job, 3))
                if JOBS[job] in GATE_ROW:
                    for h in range(2):
                        last = pe.matmul(ps[:, bank + h, :], ones[:, :], acc_of(job)[:, h * 512:(h + 1) * 512], start=True, stop=True)
                else:
                    for k in range(KC):
                        last = pe.matmul(ps[:, bank, k:k + 1], acc_of(job)[:, k * P:(k + 1) * P], ones[:, 0:1], start=True, stop=True)
                last.then_inc(mod_summed, 1)

            def turn_xn(stage):
                for t in range(TT):
                    pe.wait_ge(xn_ready, 2 * stage + t + 1)
                    for k in range(KC):
                        last = pe.transpose(ps[:, k // 2, (k % 2) * SEQ + t * P:(k % 2) * SEQ + (t + 1) * P],
                                            xn[:, t, k * P:(k + 1) * P], ident)
                        if t == TT - 1 and k % 2:
                            last.then_inc(xn_turned, 1)

            def dense_rows(m, act_high, act_low, bank, last_one=False):
                pe.wait_ge(low_ready, m + 1)
                for kc, t in ([(0, 0), (1, 0), (0, 1), (1, 1)] if last_one else [(0, 0), (0, 1), (1, 0), (1, 1)]):
                    for a, w in ((act_high(kc, t), w_high), (act_high(kc, t), w_low), (act_low(kc, t), w_high)):
                        for h in range(2):
                            ins = pe.matmul(ps[:, bank + 2 * t + h, :], a, w[:, m % SPLIT, kc, h * 512:(h + 1) * 512],
                                            start=not started[t, h], stop=False, skip_group_check=True)
                            started[t, h] = True
                    if last_one and (kc, t) == (1, 0):
                        ins.then_inc(tile_done, 1)
                return ins

            started = {}

            def begin():
                for t in range(TT):
                    for h in range(2):
                        started[t, h] = False

            def dense_cols(m, bank, first):
                k0 = 2 * (m % 4)
                pe.wait_ge(low_ready, m + 1)
                for kc in range(2):
                    for cc in range(8):
                        for i, (w, a) in enumerate(((w_high, h_high), (w_high, h_low), (w_low, h_high))):
                            ins = pe.matmul(ps[:, bank + cc // 2, (cc % 2) * SEQ:(cc % 2 + 1) * SEQ],
                                            w[:, m % SPLIT, kc, cc * P:(cc + 1) * P], a[:, k0 + kc, :],
                                            start=(first and kc == 0 and i == 0 and cc % 2 == 0), stop=False,
                                            skip_group_check=True)
                return ins

            def rows_of_h(m):
                k0 = 2 * (m % 4)
                return (lambda kc, t: h_high[:, k0 + kc, t * P:(t + 1) * P]), (lambda kc, t: h_low[:, k0 + kc, t * P:(t + 1) * P])

            def rows_of_piece(b):
                return ((lambda kc, t: piece_high[:, b, kc * SEQ + t * P:kc * SEQ + (t + 1) * P]),
                        (lambda kc, t: piece_low[:, b, kc * SEQ + t * P:kc * SEQ + (t + 1) * P]))

            pe.wait_ge(set_up, 1)
            pe.wait_ge(const_s, 16)
            turn_xn(0)
            sum_mod(0, 4)
            sum_mod(1, 5)

            pe.wait_ge(h_act, 4)
            pe.wait_ge(h_dve, 4)
            pe.wait_ge(mod_stored, 2)
            for i in range(6):
                bank = 4 * (i % 2)
                if i and i - 1 in RET_SUMS:
                    pe.wait_ge(mod_stored, RET_SUMS[i - 1] + 1)
                if i >= 2:
                    pe.wait_ge(group_act, i - 1)
                    pe.wait_ge(group_dve, i - 1)
                if i in (3, 4):
                    pe.wait_ge(prob_ready, 2 * (i - 2))
                begin()
                for j in range(4):
                    m = 4 * i + j
                    if i == 0:
                        pe.wait_ge(h_low_s, j + 1)
                    if j == 3:
                        if i:
                            pe.wait_ge(group_act, i)
                            pe.wait_ge(group_dve, i)
                        if i in RET_SUMS:
                            sum_mod(RET_SUMS[i], 4 - bank)
                        if i in (2, 3):
                            if i == 2:
                                pe.wait_ge(rot_done, 2 * HEADS)
                            for h in (2 * (i - 2), 2 * (i - 2) + 1):
                                for jt in range(TT):
                                    for c in range(2):
                                        last = pe.matmul(ps[:, 4 - bank + 2 + h % 2, jt * SEQ:(jt + 1) * SEQ],
                                                         qk[:, 1, h, c, jt * P:(jt + 1) * P], qk[:, 0, h, c, :],
                                                         start=(c == 0), stop=(c == 1))
                                last.then_inc(scores_done, 1)
                    if i < 2:
                        last = dense_cols(m, bank, j == 0)
                    else:
                        last = dense_rows(m, *rows_of_h(m), bank)
                    last.then_inc(w_used, 1)

            for h in range(HEADS):
                pe.wait_ge(prob_ready, h + 1)
                if h == 0:
                    pe.wait_ge(group_act, 5)
                    pe.wait_ge(group_dve, 5)
                    pe.wait_ge(mod_stored, 6)
                if h == 2:
                    pe.wait_ge(group_act, 6)
                    pe.wait_ge(group_dve, 6)
                for t in range(TT):
                    for jt in range(TT):
                        last = pe.matmul(ps[:, 2 * h + t, :], prob[:, h, jt * SEQ + t * P:jt * SEQ + (t + 1) * P],
                                         v[:, jt, h * V_DIM:(h + 1) * V_DIM], start=(jt == 0), stop=(jt == 1))
                last.then_inc(o_done, 1)

            def turn_gated(kp):
                for c in range(2):
                    for t in range(TT):
                        last = pe.transpose(ps[:, 4 + kp % 2, c * SEQ + t * P:c * SEQ + (t + 1) * P],
                                            ret_g[:, t, (2 * kp + c) * P:(2 * kp + c + 1) * P], ident)
                last.then_inc(turned, 1)

            pe.wait_ge(o_gated, 6)
            turn_gated(0)
            turn_gated(1)
            pe.wait_ge(o_gated, 2 * HEADS)
            begin()
            for kp in range(8):
                m = M_RET_OUT + kp
                if kp == 1:
                    sum_mod(6, 6)
                pe.wait_ge(piece_low_s, kp + 1)
                dense_rows(m, *rows_of_piece(kp % 2), 0, kp == 7).then_inc(w_used, 1)
                if kp + 2 < 8:
                    turn_gated(kp + 2)
            pe.wait_ge(mod_stored, 7)
            sum_mod(7, 6)

            def gather(layer, g, bank):
                pe.wait_ge(sel_ready, g + (5 * layer + 1))
                for k in range(KC):
                    for t in range(TT):
                        last = pe.matmul(ps[:, bank if k // 4 else 0, (k % 4) * P:(k % 4 + 1) * P], xn[:, t, k * P:(k + 1) * P], sel[:, t, :],
                                         start=(t == 0), stop=(t == 1))
                    if k % 4 == 3:
                        last.then_inc(gather_done, 1)

            def gather_gates(layer, g):
                for t in range(TT):
                    last = pe.matmul(ps[:, 7, SEQ:SEQ + PER_GROUP], sel[:, t, :], own_gates[:, t, :], start=(t == 0), stop=(t == 1))
                last.then_inc(gates_done, 1)

            def experts(layer):
                m0 = M_MOE[layer]
                stage = 2 * layer + 1
                turn_xn(stage)
                pe.wait_ge(mod_stored, (8, 12)[layer])
                for k in range(KC):
                    pe.wait_ge(h_act if k < 4 else h_dve, 4 * stage + k % 4 + 1)
                    last = pe.matmul(ps[0:N_EXPERTS, 4, 0:SEQ], router_w[:, k, :], h_all[:, k, :], start=(k == 0), stop=(k == KC - 1))
                last.then_inc(logits_done, 1)
                pe.wait_ge(scores_by_expert, layer + 1)
                for t in range(TT):
                    last = pe.transpose(ps[:, 5, (t + 1) * N_EXPERTS:(t + 2) * N_EXPERTS], scratch[0:N_EXPERTS, 0, t * P:(t + 1) * P],
                                        ident[0:N_EXPERTS, 0:N_EXPERTS])
                last.then_inc(scores_ready, 1)
                pe.wait_ge(members_ready, layer + 1)
                members = rt[:, 0, 0:TT * GROUPS]
                pe.matmul(ps[:, 5, 0:GROUPS], upper, members[:, 0:GROUPS], start=True, stop=True)
                pe.matmul(ps[:, 5, GROUPS:2 * GROUPS], upper, members[:, GROUPS:], start=True, stop=False)
                pe.matmul(ps[:, 5, GROUPS:2 * GROUPS], ones[:, :], members[:, 0:GROUPS], start=False, stop=True)\
                    .then_inc(place_done, 1)
                gather(layer, 0, 3)

                def gates_and_count():
                    pe.wait_ge(route_ready, layer + 1)
                    gather_gates(layer, 0)
                    for t in range(TT):
                        last = pe.matmul(ps[:, 6, 0:GROUPS], ones[:, :], rt[:, 1, t * GROUPS:(t + 1) * GROUPS],
                                         start=(t == 0), stop=(t == 1))
                    last.then_inc(over_counted, 1)

                def scatter_products(done):
                    for i, bank in enumerate((6, 7, 2, 3)):
                        for y in (y_high, y_low):
                            last = pe.matmul(bank_of(bank), sel_t[:, (i // 2) * P:(i // 2 + 1) * P],
                                             y[:, 4 * (i % 2):4 * (i % 2) + 4, :], start=(y is y_high), stop=(y is y_low))
                        last.then_inc(done, 1)

                def scatter(g):
                    pe.wait_ge(y_ready, g * 2 + (2 * GROUPS * layer + 2))
                    pe.wait_ge(sel_t_s, g + (GROUPS * layer + 1))
                    scatter_products(scattered)

                def group(g, first):
                    def up(e, j, s):
                        m = m0 + s
                        pe.wait_ge(low_ready, g * MOE_GRAN + (m + 1))
                        for kc in range(2):
                            k = 2 * j + kc
                            for i, (a, w) in enumerate(((h_high, w_high), (h_high, w_low), (h_low, w_high))):
                                for h in range(2):
                                    last = pe.matmul(ps[:, 2 * (e % 2) + h, :], a[:, k, 0:P],
                                                     w[:, m % SPLIT, kc, h * 512:(h + 1) * 512],
                                                     start=(k == 0 and i == 0), stop=(k == KC - 1 and i == 2))
                        last.then_inc(w_used, 1)

                    def turn_hid(e):
                        pe.wait_ge(hid_ready, g * PER_GROUP + (N_EXPERTS * layer + e + 1))
                        for f in range(4):
                            last = pe.transpose(ps[:, 6, f * P:(f + 1) * P], hid[:, e % 2, f * P:(f + 1) * P], ident)
                        last.then_inc(hid_turned, 1)

                    def down(e, j, s):
                        m = m0 + s
                        if j == 0:
                            pe.wait_ge(hid_low, g * PER_GROUP + (N_EXPERTS * layer + e + 1))
                        pe.wait_ge(low_ready, g * MOE_GRAN + (m + 1))
                        for kc in range(2):
                            f = 2 * j + kc
                            for i, (a, w) in enumerate(((piece_high, w_high), (piece_high, w_low), (piece_low, w_high))):
                                for h in range(2):
                                    last = pe.matmul(ps[:, 4 + h, :], a[:, e % 2, f * P:(f + 1) * P],
                                                     w[:, m % SPLIT, kc, h * 512:(h + 1) * 512],
                                                     start=(e == 0 and f == 0 and i == 0), stop=(e == 3 and f == 3 and i == 2))
                        last.then_inc(w_used, 1)

                    for s, (e, kind, j) in enumerate(MOE_ORDER):
                        if kind == "up":
                            if s == 0:
                                pe.wait_ge(hg_low, g * 2 + (10 * layer + 1))
                            if s == 2:
                                pe.wait_ge(hg_low, g * 2 + (10 * layer + 2))
                            if s == 4:
                                pe.wait_ge(banks_free, g + (5 * layer + 1))
                            up(e, j, s)
                        else:
                            down(e, j, s)
                        if s == 0 and not first:
                            scatter(g - 1)
                        if s == 1 and first:
                            gates_and_count()
                        if s == 4:
                            turn_hid(0)
                            for t in range(TT):
                                last = pe.transpose(ps[:, 7, t * P:(t + 1) * P], sel[:, t, :], ident)
                            last.then_inc(sel_turned, 1)
                        elif s in (10, 16, 20):
                            turn_hid({10: 1, 16: 2, 20: 3}[s])
                        if s == 16:
                            gather(layer, g + 1, 1)
                            gather_gates(layer, g + 1)

                group(0, True)
                with pe.Fori(1, GROUPS) as g:
                    group(g, False)
                scatter(GROUPS - 1)

                o = ov[layer]
                pe.wait_ge(over_known, layer + 1)
                flag = pe.value_load(over_i[0:1, 0:1], min_val=0, max_val=1)
                pe.wait_ge(banks_free, 5 * (layer + 1))
                with pe.If(flag > 0):
                    n_w = 0
                    for e in range(PER_GROUP):
                        for j in range(4):
                            n_w += 1
                            pe.wait_ge(o["w"], 16 * n_w)
                            for kc in range(2):
                                k = 2 * j + kc
                                for h in range(2):
                                    last = pe.matmul(ps[:, h, :], gathered[:, k, :], over_w[:, kc, h * 512:(h + 1) * 512],
                                                     start=(k == 0), stop=(k == KC - 1))
                            last.then_inc(o["used"], 1)
                        pe.wait_ge(o["hid"], e + 1)
                        for f in range(4):
                            last = pe.transpose(ps[:, 6, f * P:(f + 1) * P], hid[:, 0, f * P:(f + 1) * P], ident)
                        last.then_inc(o["turned"], 1)
                        pe.wait_ge(o["t_act"], e + 1)
                        for j in range(2):
                            n_w += 1
                            pe.wait_ge(o["w"], 16 * n_w)
                            for kc in range(2):
                                f = 2 * j + kc
                                for h in range(2):
                                    last = pe.matmul(ps[:, 4 + h, :], hid[:, 1, f * P:(f + 1) * P], over_w[:, kc, h * 512:(h + 1) * 512],
                                                     start=(e == 0 and f == 0), stop=(e == 3 and f == 3))
                            last.then_inc(o["used"], 1)
                    for t in range(TT):
                        last = pe.transpose(ps[:, 7, t * P:(t + 1) * P], sel[:, t, :], ident)
                    last.then_inc(o["sel_turned"], 1)
                    pe.wait_ge(o["y_low"], 2)
                    pe.wait_ge(o["sel_t"], 1)
                    scatter_products(o["scattered"])

            experts(0)

            turn_xn(2)
            pe.wait_ge(h_act, 12)
            pe.wait_ge(h_dve, 12)
            for i in range(3):
                bank = 4 * (i % 2)
                if i == 2:
                    pe.wait_ge(group_act, 7)
                begin()
                for j in range(4):
                    m = M_GM + 4 * i + j
                    if i == 0:
                        pe.wait_ge(h_low_s, 4 + j + 1)
                    if i == 2 and j == 2:
                        pe.wait_ge(group_act, 8)
                        pe.wait_ge(mix_s, 32)
                        for g in range(GM_GROUPS):
                            last = pe.matmul(ps[:, 6, g * P:(g + 1) * P], ones[:, :], mix_ws[:, g, :], start=True, stop=True)
                        last.then_inc(mix_rows_done, 1)
                    if i == 2 and j == 3:
                        sum_mod(8, 4)
                    dense_rows(m, *rows_of_h(m), bank).then_inc(w_used, 1)
            pe.wait_ge(mod_stored, 9)
            pe.wait_ge(mix_rows_s, 1)
            def mix(i):
                for b in range(4):
                    if i != 1:
                        pe.wait_ge(group_act, 4 * (i // 2) + b + 10)
                    for c in (2 * b, 2 * b + 1):
                        ch = 8 * i + c
                        for t in range(TT):
                            last = pe.matmul(ps[:, 4 + b, (c % 2) * SEQ + t * P:(c % 2) * SEQ + (t + 1) * P],
                                             gv[:, t, ch * P:(ch + 1) * P], mix_ws[:, ch * P // (GM_HALF // GM_GROUPS), :],
                                             start=True, stop=True)
                    last.then_inc(mixed_done, 1)

            for i in range(3):
                for j in range(4):
                    m = M_GM + 12 + 8 * i + j
                    if i >= 1 and j == 0:
                        pe.wait_ge(mix_taken, 8 * (i + 1))
                        pe.wait_ge(mod_stored, 9 + i)
                    dense_cols(m, 4, j == 0).then_inc(w_used, 1)
                if i == 0:
                    pe.wait_ge(gv_ready, 2)
                    mix(0)
                    pe.wait_ge(group_act, 9)
                    begin()
                if i == 1:
                    mix(2)
                for kp in range(4):
                    m = M_GM + 12 + 8 * i + 4 + kp
                    if i == 0 and kp == 3:
                        pe.wait_ge(mod_stored, 10)
                        mix(1)
                    if kp == 2 and i < 2:
                        pe.wait_ge(mix_taken, (8, 20)[i])
                        sum_mod(9 + i, 4)
                    pe.wait_ge(piece_low_s, 8 + 4 * i + kp + 1)
                    dense_rows(m, *rows_of_piece(kp % 2), 0, (i, kp) == (2, 3)).then_inc(w_used, 1)
            sum_mod(11, 4)

            experts(1)

        @block.scalar
        def _(act):
            chain = [0]

            def square_and_root(stage):
                act.activation(warm[:, stage:stage + 1], eps[:, :], ACT.Sqrt)
                for t in range(TT):
                    if stage:
                        act.wait_ge(x_ready, TT * (stage - 1) + t + 1)
                    act.activation(xn[:, t, :], x[:, t, :], ACT.Square, accum_out=ssq[:, t:t + 1]).then_inc(squares_done, 1)
                    act.wait_ge(squares_done, 2 * stage + t + 1)
                    act.activation(std[:, t:t + 1], ssq[:, t:t + 1], ACT.Sqrt, scale=1.0 / D, bias=eps[:, :]).then_inc(std_ready, 1)

            def h_of(stage, tmp, to_split):
                layer, which = stage // 2, 2 * (stage % 2)
                act.wait_ge(mod_stored, (2, 5, 8, 11)[stage])
                for pair in range(4):
                    two = slice(2 * pair, 2 * pair + 2)
                    if pair < 2:
                        act.wait_ge(xn_turned, 4 * stage + pair + 1)
                        for k in (2 * pair, 2 * pair + 1):
                            act.activation(tmp[:, k, :], ps[:, k // 2, (k % 2) * SEQ:(k % 2 + 1) * SEQ], ACT.Identity,
                                           scale=mod[:, layer, which + 1, k:k + 1], bias=mod[:, layer, which, k:k + 1])\
                               .then_inc(h_act, 1)
                    if to_split:
                        done = 4 * stage + 2 * (pair % 2) + 2
                        act.wait_ge(h_act if pair < 2 else h_dve, done)
                        act.copy(h_high[:, two, :], tmp[:, two, :]).then_inc(h_high_s, 1)

            def scale_ada(job, kp):
                n = ADA_OF[job, kp]
                wait_landed(act, n)
                rows_w = ring[:, n % RING, 1, :]
                act.activation(rows_w, rows_w, ACT.Copy, scale=c_act[:, 2 * kp + 1:2 * kp + 2]).then_inc(ada_scaled, 1)

            def step(m):
                split_high(act, m)
                if m in ADA_WITH:
                    scale_ada(*ADA_WITH[m])

            act.wait_ge(small_s, 16)
            act.activation(c_act[:, :], small_of("c"), ACT.Silu).then_inc(c_ready, 1)
            act.wait_ge(c_ready, 1)
            act.wait_ge(x_in_s, 16)
            act.wait_ge(set_up, 1)
            square_and_root(0)
            act.wait_ge(lg_ready, 1)
            act.activation(lg[:, 1, :], lg[:, 0, :], ACT.Exp, scale=-1.0).then_inc(act_chain, 1)
            act.wait_ge(lg_ready, 2)
            act.activation(lg[:, 3, :], lg[:, 2, :], ACT.Ln).then_inc(act_chain, 1)
            step(0)
            h_of(0, h_ret, True)
            step(1)

            for i in range(6):
                for j in range(4):
                    m = 4 * i + j
                    step(m + LEAD)
                    if i == 0 and j < HEADS:
                        act.wait_ge(dist_ready, j + 1)
                        act.activation(prob[:, j, :], prob[:, j, :], ACT.Exp).then_inc(decay_ready, 1)
                if i < 2:
                    act.sem_inc(group_act, 1)
                    continue
                act.wait_ge(w_used, 4 * i + 4)
                bank = 4 * (i % 2)
                if i >= 4:
                    act.wait_ge(prob_ready, HEADS)
                for t, h in ([(0, 0), (0, 1)] if i < 4 else [(0, 0), (0, 1), (1, 0), (1, 1)]):
                    src = ps[:, bank + 2 * t + h, :]
                    at = (i % 2) * COLS + h * 512
                    if i < 4:
                        ins = act.copy(v[:, t, at:at + 512], src)
                    else:
                        ins = act.activation(ret_g[:, t, at:at + 512], src, ACT.Silu)
                ins.then_inc(group_act, 1)

            for kp in range(4):
                scale_ada(6, kp)
            act.activation(warm[:, 5:6], eps[:, :], ACT.Sqrt)
            for h in range(HEADS):
                act.wait_ge(o_done, h + 1)
                for t in range(TT):
                    n = 2 * h + t
                    if n:
                        act.wait_ge(o_squares, n)
                    act.activation(scratch[:, 0, :], ps[:, n, :], ACT.Square, accum_out=ssq[:, n:n + 1]).then_inc(o_squares, 1)
                if h % 2:
                    act.wait_ge(o_squares, 2 * h + 2)
                    two = slice(2 * h - 2, 2 * h + 2)
                    act.activation(std[:, two], ssq[:, two], ACT.Sqrt, scale=1.0 / V_DIM, bias=eps[:, :]).then_inc(o_std, 1)

            def piece_up(n, bank):
                act.wait_ge(turned, n + 1)
                act.copy(piece_high[:, n % 2, :], ps[:, bank, :]).then_inc(piece_high_s, 1)

            piece_up(0, 4)
            piece_up(1, 5)
            for kp in range(8):
                step(M_RET_OUT + kp + LEAD)
                if kp + 2 < 8:
                    piece_up(kp + 2, 4 + kp % 2)

            def experts(layer):
                m0 = M_MOE[layer]
                stage = 2 * layer + 1
                square_and_root(stage)
                h_of(stage, h_all, False)
                act.wait_ge(logits_done, layer + 1)
                act.activation(scratch[0:N_EXPERTS, 0, 0:SEQ], ps[0:N_EXPERTS, 4, 0:SEQ], ACT.Sigmoid).then_inc(scores_by_expert, 1)

                def gathered_up(g):
                    act.wait_ge(gather_done, g * 2 + (10 * layer + 1))
                    for k in range(4):
                        ins = act.activation(gathered[:, k, :], ps[:, 0, k * P:(k + 1) * P], ACT.Identity,
                                             scale=mod[:, layer, 3, k:k + 1], bias=mod[:, layer, 2, k:k + 1])
                    ins.then_inc(gathered_act, 1)

                def gathered_high(g):
                    act.wait_ge(gathered_act, g + (5 * layer + 1))
                    act.copy(h_high[:, 0:4, 0:P], gathered[:, 0:4, :]).then_inc(hg_high, 1)
                    act.wait_ge(gathered_dve, g + (5 * layer + 1))
                    act.copy(h_high[:, 4:8, 0:P], gathered[:, 4:8, :]).then_inc(hg_high, 1)

                def take_output(g):
                    act.wait_ge(w_used, g * MOE_GRAN + (m0 + MOE_GRAN))
                    for h in range(2):
                        act.copy(y_high[:, 4 * h:4 * h + 4, :], bank_of(4 + h)).then_inc(y_high_s, 1)

                def group(g, first):
                    for s in range(MOE_GRAN):
                        if s == 0 and not first:
                            take_output(g - 1)
                        split_high(act, m0 + s + LEAD, g)
                        if s in (3, 7, 13, 19):
                            e = {3: 0, 7: 1, 13: 2, 19: 3}[s]
                            act.wait_ge(w_used, g * MOE_GRAN + (m0 + s + 1))
                            act.activation(hid[:, e % 2, :], ps[:, 2 * (e % 2), :], ACT.Silu).then_inc(silu_done, 1)
                        if s in (4, 10, 16, 20):
                            e = {4: 0, 10: 1, 16: 2, 20: 3}[s]
                            act.wait_ge(hid_turned, g * PER_GROUP + (N_EXPERTS * layer + e + 1))
                            act.copy(piece_high[:, e % 2, :], ps[:, 6, :]).then_inc(hid_high, 1)
                        if s == 4:
                            act.wait_ge(sel_turned, g + (GROUPS * layer + 1))
                            act.copy(sel_t[:, :], ps[:, 7, 0:SEQ]).then_inc(sel_t_s, 1)
                        if s == 16:
                            gathered_up(g + 1)
                        if s == 20:
                            gathered_high(g + 1)

                gathered_up(0)
                gathered_high(0)
                group(0, True)
                with act.Fori(1, GROUPS) as g:
                    group(g, False)
                take_output(GROUPS - 1)

                o = ov[layer]
                act.wait_ge(over_known, layer + 1)
                flag = act.value_load(over_i[0:1, 0:1], min_val=0, max_val=1)
                group = act.value_load(over_i[0:1, 1:2], min_val=0, max_val=GROUPS - 1)
                with act.If(flag > 0):
                    n_w = 0

                    def load(e, kind, j):
                        nonlocal n_w
                        if n_w:
                            act.wait_ge(o["used"], n_w)
                        n_w += 1
                        at = N_OF[m0] + MOE_ORDER.index((e, kind, j))
                        act.dma_start(area[:, 6144:8192], stream[group * MOE_GRAN + at]).then_inc(o["w"], 16)

                    for e in range(PER_GROUP):
                        for j in range(4):
                            load(e, "up", j)
                        act.wait_ge(o["used"], n_w)
                        act.activation(hid[:, 0, :], ps[:, 0, :], ACT.Silu).then_inc(o["silu"], 1)
                        act.wait_ge(o["turned"], e + 1)
                        act.copy(hid[:, 1, :], ps[:, 6, :]).then_inc(o["t_act"], 1)
                        for j in range(2):
                            load(e, "down", j)
                    act.wait_ge(o["sel_turned"], 1)
                    act.copy(sel_t[:, :], ps[:, 7, 0:SEQ]).then_inc(o["sel_t"], 1)
                    for h in range(2):
                        act.copy(y_high[:, 4 * h:4 * h + 4, :], bank_of(4 + h)).then_inc(o["y_high"], 1)

            experts(0)

            square_and_root(2)
            h_of(2, h_all, True)
            for i in range(3):
                for j in range(4):
                    step(M_GM + 4 * i + j + LEAD)
                act.wait_ge(w_used, M_GM + 4 * i + 4)
                if i == 0:
                    act.wait_ge(h_low_s, 8)
                for t in range(TT):
                    for h in range(2):
                        ins = act.activation(gv[:, t, i * COLS + h * 512:i * COLS + (h + 1) * 512],
                                             ps[:, 4 * (i % 2) + 2 * t + h, :], ACT.Gelu)
                ins.then_inc(group_act, 1)
            for j in range(2):
                step(M_GM + 12 + j + LEAD)
            act.wait_ge(ln_std, 1)
            act.activation(std[:, 0:TT], mean_var[:, :, 1], ACT.Sqrt, bias=eps[:, :]).then_inc(ln_std, 1)
            for i in range(3):
                for j in range(2 if i == 0 else 0, 4):
                    step(M_GM + 12 + 8 * i + j + LEAD)
                act.wait_ge(w_used, M_GM + 12 + 8 * i + 4)
                if i >= 1:
                    act.wait_ge(z_ready, 8 * i)
                def u_gelu(b):
                    act.activation(u_t[:, 2 * b:2 * b + 2, :], ps[:, 4 + b, :].rearrange("p (k n) -> p k n", k=2),
                                   ACT.Gelu).then_inc(group_act, 1)

                def piece(kp):
                    act.wait_ge(z_ready, 8 * i + 2 * kp + 2)
                    if kp >= 2 or i:
                        act.wait_ge(w_used, M_GM + 12 + 8 * i + 4 + kp - 2 + 1 if kp >= 2 else M_GM + 12 + 8 * (i - 1) + 8 - 2 + kp + 1)
                    act.copy(piece_high[:, kp % 2, :], u_t[:, 2 * kp:2 * kp + 2, :].rearrange("p k n -> p (k n)"))\
                        .then_inc(piece_high_s, 1)

                u_gelu(0)
                u_gelu(1)
                if i == 2:
                    piece(0)
                u_gelu(2)
                u_gelu(3)
                if i < 2:
                    piece(0)
                for kp in range(4):
                    if kp < 3:
                        piece(kp + 1)
                    step(M_GM + 12 + 8 * i + 4 + kp + LEAD)

            experts(1)

            square_and_root(4)

        @block.gpsimd
        def _(pool):
            def add_ada(job, kp):
                acc = acc_of(job)
                pool.wait_ge(ada_scaled, turns(job, kp))
                pool.wait_ge(ada_dve, 4 * job + kp + 1)
                pool.tensor_tensor(acc, acc, ring[:, ADA_OF[job, kp] % RING, 1, :], ALU.add).then_inc(ada_pool, 1)

            def mix_rows_plus_bias(first, last):
                pool.wait_ge(mix_rows_s, 1)
                pool.wait_ge(mix_s, 32)
                for ch in range(first, last):
                    g = ch * P // (GM_HALF // GM_GROUPS)
                    if ch >= 4:
                        pool.wait_ge(mix_taken, ch - 3)
                    to = mix_add[:, (ch // 2) % 2, (ch % 2) * P:(ch % 2 + 1) * P]
                    pool.tensor_scalar(to, mix_rows[:, g, :], ln_b[:, ch:ch + 1], None, ALU.mult).then_inc(mix_scaled, 1)
                    pool.wait_ge(mix_scaled, ch + 1)
                    pool.tensor_tensor(to, to, mix_bs[:, g, :], ALU.add).then_inc(mix_add_s, 1)

            pool.sem_inc(x_added, 1)
            pool.wait_ge(decay_s, 16)
            pool.wait_ge(lg_ready, 3)
            pool.wait_ge(xn_turned, 4)
            back = scratch[:, 0, :]
            for h in range(HEADS):
                pool.tensor_scalar(prob[:, h, :], dist[:, 0, :], lg[:, 5, h:h + 1], None, ALU.mult).then_inc(pool_chain, 1)
                pool.tensor_scalar(back, dist[:, 1, :], lg[:, 5, HEADS + h:HEADS + h + 1], None, ALU.mult).then_inc(pool_chain, 1)
                pool.wait_ge(pool_chain, 2 * h + 2)
                pool.tensor_tensor(prob[:, h, :], prob[:, h, :], back, ALU.add).then_inc(dist_ready, 1)
                pool.wait_ge(dist_ready, h + 1)
            ada_parts = [(job, kp) for job in range(2, 12) for kp in range(4)]
            for w in range(2):
                while ADA_OF[ada_parts[0]] < N_OF[4 * (w + 1) + LEAD - 1]:
                    add_ada(*ada_parts.pop(0))
                for h in range(HEADS):
                    n = HEADS * w + h
                    pool.wait_ge(rot_ready, n + 1)
                    pool.tensor_tensor(qk[:, w, h, 0, :], rot[:, h % 2, 0, 0:SEQ], rot[:, h % 2, 1, SEQ:], ALU.subtract)
                    pool.tensor_tensor(qk[:, w, h, 1, :], rot[:, h % 2, 1, 0:SEQ], rot[:, h % 2, 0, SEQ:], ALU.add)\
                        .then_inc(rot_done, 1)
            def add_outputs(layer):
                base = 4 * (GROUPS - 1) * layer
                with pool.Fori(0, GROUPS - 1) as g:
                    for i in range(4):
                        t, cols = i // 2, slice((i % 2) * 512, (i % 2 + 1) * 512)
                        pool.wait_ge(scatter_term, g * 4 + (base + i + 1))
                        pool.tensor_tensor(x[:, t, cols], x[:, t, cols], term(i), ALU.add).then_inc(x_added, 1)

            for job, kp in ada_parts:
                if (job, kp) == (8, 0):
                    add_outputs(0)
                add_ada(job, kp)
                for first, last in {(9, 1): [(0, 4)], (9, 2): [(4, 8)], (9, 3): [(8, 12)], (10, 0): [(12, 20)], (10, 3): [(20, 24)]}.get((job, kp), ()):
                    mix_rows_plus_bias(first, last)
            add_outputs(1)

        @block.vector
        def _(dve):
            links = [0]

            def link(ins):
                links[0] += 1
                ins.then_inc(dve_chain, 1)
                dve.wait_ge(dve_chain, links[0])

            def add_ada(job, kp):
                n = ADA_OF[job, kp]
                wait_landed(dve, n)
                acc = acc_of(job)
                for part in range(2 if job < 2 else 1):
                    rows_w = ring[:, n % RING, part, :]
                    c = c_act[:, 2 * kp + part:2 * kp + part + 1]
                    if kp == 0 and part == 0:
                        if job >= 2:
                            dve.wait_ge(mod_summed, job)
                        ins = dve.tensor_scalar(acc, rows_w, c, None, ALU.mult)
                    else:
                        if part == 0 and job >= 2:
                            dve.wait_ge(ada_pool, turns(job, kp - 1))
                        elif part == 0:
                            dve.wait_ge(ada_dve, 4 * job + kp)
                        ins = dve.scalar_tensor_tensor(acc, rows_w, c, acc, ALU.mult, ALU.add)
                    if job < 2 and part == 0:
                        link(ins)
                    else:
                        ins.then_inc(ada_dve, 1)

            def step(m, job=None, bank=None):
                split_low(dve, m)
                if job is not None:
                    store_mod(job, bank)
                if m in ADA_WITH:
                    add_ada(*ADA_WITH[m])

            def store_mod(job, bank):
                layer, which = JOBS[job]
                dve.wait_ge(mod_summed, job + 1)
                if (layer, which) in GATE_ROW:
                    r = GATE_ROW[layer, which]
                    dve.wait_ge(row_s[2 * layer + (which == G2)], 16)
                    for h in range(2):
                        ins = dve.tensor_tensor(rows[:, r, h * 512:(h + 1) * 512], ps[:, bank + h, :],
                                                rows[:, r, h * 512:(h + 1) * 512], ALU.add)
                    ins.then_inc(mod_stored, 1)
                    return
                to = mod[:, layer, {SH1: 0, SC1: 1, SH2: 2, SC2: 3}[which], :]
                if which in (SH1, SH2):
                    dve.tensor_tensor(to, ps[:, bank, 0:KC], b_ada[:, layer, which, :], ALU.add).then_inc(mod_stored, 1)
                else:
                    link(dve.scalar_tensor_tensor(to, ps[:, bank, 0:KC], 1.0, b_ada[:, layer, which, :], ALU.add, ALU.add))
                    dve.tensor_tensor(to, to, norm_g[:, layer, which // 3, :], ALU.mult).then_inc(mod_stored, 1)

            def scale_x(stage):
                for t in range(TT):
                    dve.wait_ge(std_ready, TT * stage + t + 1)
                    link(dve.reciprocal(rstd[:, t:t + 1], std[:, t:t + 1]))
                    dve.tensor_scalar(xn[:, t, :], x[:, t, :], rstd[:, t:t + 1], None, ALU.mult).then_inc(xn_ready, 1)

            def h_of(stage, tmp, to_split):
                layer, which = stage // 2, 2 * (stage % 2)
                dve.wait_ge(mod_stored, (2, 5, 8, 11)[stage])

                def rest(pair):
                    if to_split:
                        two = slice(2 * pair, 2 * pair + 2)
                        dve.wait_ge(h_high_s, 4 * (stage // 2) + pair + 1)
                        dve.tensor_tensor(h_low[:, two, :], tmp[:, two, :], h_high[:, two, :].bitcast(F32), ALU.subtract)\
                           .then_inc(h_low_s, 1)

                for pair in (2, 3):
                    dve.wait_ge(xn_turned, 4 * stage + pair + 1)
                    for k in (2 * pair, 2 * pair + 1):
                        dve.tensor_scalar(tmp[:, k, :], ps[:, k // 2, (k % 2) * SEQ:(k % 2 + 1) * SEQ],
                                          mod[:, layer, which + 1, k:k + 1], mod[:, layer, which, k:k + 1], ALU.mult, ALU.add)\
                           .then_inc(h_dve, 1)
                for pair in range(4):
                    rest(pair)

            def add_output(n, row):
                for t in range(TT):
                    if t == 0:
                        dve.wait_ge(tile_done, n + 1)
                        if n == 1:
                            dve.wait_ge(z_ready, 24)
                    else:
                        dve.wait_ge(w_used, (M_RET_OUT + 8, M_GM + 36)[n])
                    halves = [slice(h * 512, (h + 1) * 512) for h in range(2)]
                    for h, cols in enumerate(halves):
                        ins = dve.tensor_tensor((scratch, mixture)[t][:, h, :], ps[:, 2 * t + h, :], rows[:, row, cols], ALU.mult)
                    link(ins)
                    for h, cols in enumerate(halves):
                        ins = dve.tensor_tensor(x[:, t, cols], x[:, t, cols], (scratch, mixture)[t][:, h, :], ALU.add)
                    ins.then_inc(x_ready, 1)

            dve.memset(ones[:, :], 1.0)
            dve.memset(eps[:, :], EPS).then_inc(set_up, 1)
            dve.wait_ge(small_s, 16)
            link(dve.tensor_scalar(lg[:, 4, :], decay_logit, -1.0, None, ALU.mult))
            dve.tensor_tensor(lg[:, 0, :], decay_logit, lg[:, 4, :], ALU.max).then_inc(lg_ready, 1)
            dve.wait_ge(c_ready, 1)
            for kp in range(4):
                add_ada(0, kp)
            scale_x(0)
            dve.wait_ge(act_chain, 1)
            dve.tensor_scalar(lg[:, 2, :], lg[:, 1, :], 1.0, None, ALU.add).then_inc(lg_ready, 1)
            for kp in range(4):
                add_ada(1, kp)
            store_mod(0, 4)
            dve.wait_ge(act_chain, 2)
            dve.wait_ge(lg_ready, 2)
            link(dve.tensor_scalar(lg[:, 4, :], lg[:, 2, :], -1.0, None, ALU.add))
            link(dve.tensor_scalar(lg[:, 0, :], lg[:, 4, :], 0.0, None, ALU.is_equal))
            link(dve.tensor_tensor(lg[:, 4, :], lg[:, 4, :], lg[:, 0, :], ALU.add))
            link(dve.tensor_tensor(lg[:, 3, :], lg[:, 3, :], lg[:, 0, :], ALU.add))
            link(dve.reciprocal(lg[:, 4, :], lg[:, 4, :]))
            link(dve.tensor_tensor(lg[:, 3, :], lg[:, 3, :], lg[:, 4, :], ALU.mult))
            link(dve.tensor_tensor(lg[:, 3, :], lg[:, 3, :], lg[:, 1, :], ALU.mult))
            link(dve.tensor_scalar(lg[:, 4, :], decay_logit, 0.0, None, ALU.min))
            dve.tensor_tensor(lg[:, 5, :], lg[:, 4, :], lg[:, 3, :], ALU.subtract).then_inc(lg_ready, 1)
            step(0)
            store_mod(1, 5)
            h_of(0, h_ret, True)
            step(1)

            def probs(i):
                for h in (2 * (i - 2), 2 * (i - 2) + 1):
                    dve.wait_ge(scores_done, h + 1)
                    dve.wait_ge(decay_ready, h + 1)
                    dve.scalar_tensor_tensor(prob[:, h, :], ps[:, 4 - 4 * (i % 2) + 2 + h % 2, :], QK_SCALE, prob[:, h, :],
                                             ALU.mult, ALU.mult).then_inc(prob_ready, 1)

            for i in range(6):
                for j in range(4):
                    if j == 3 and i in RET_SUMS:
                        step(4 * i + j + LEAD, RET_SUMS[i], 4 - 4 * (i % 2))
                    else:
                        step(4 * i + j + LEAD)
                    if j == 3:
                        if i in (2, 3):
                            probs(i)
                bank = 4 * (i % 2)
                dve.wait_ge(w_used, 4 * i + 4)
                if i == 0:
                    dve.wait_ge(h_low_s, 4)
                    dve.wait_ge(tables_s, 16)
                if i < 2:
                    for h in range(HEADS):
                        n = HEADS * i + h
                        if n >= 2:
                            dve.wait_ge(rot_done, n - 1)
                        both = ps[:, bank + h, :].rearrange("p (c n) -> p c n", c=2)
                        for w, table in enumerate((cos, sin)):
                            ins = dve.tensor_tensor(rot[:, h % 2, w, :].rearrange("p (c n) -> p c n", c=2), both,
                                                    table.unsqueeze(1).to_broadcast([P, 2, SEQ]), ALU.mult)
                        ins.then_inc(rot_ready, 1)
                    dve.wait_ge(rot_ready, HEADS * i + HEADS)
                    dve.sem_inc(group_dve, 1)
                elif i < 4:
                    if i == 2:
                        dve.wait_ge(rot_done, 2 * HEADS)
                    for h in range(2):
                        at = (i % 2) * COLS + h * 512
                        ins = dve.tensor_copy(v[:, 1, at:at + 512], ps[:, bank + 2 + h, :])
                    ins.then_inc(group_dve, 1)
                else:
                    dve.sem_inc(group_dve, 1)
            for kp in range(3):
                add_ada(6, kp)
            dve.wait_ge(group_act, 6)
            for h in range(HEADS):
                if h == 2:
                    add_ada(6, 3)
                if h % 2 == 0:
                    dve.wait_ge(o_std, h // 2 + 1)
                    two = slice(2 * h, 2 * h + 4)
                    link(dve.reciprocal(rstd[:, two], std[:, two]))
                for t in range(TT):
                    n = 2 * h + t
                    part = ret_g[:, t, h * V_DIM:(h + 1) * V_DIM]
                    dve.scalar_tensor_tensor(part, ps[:, n, :], rstd[:, n:n + 1], part, ALU.mult, ALU.mult).then_inc(o_gated, 1)

            def piece_down(n, bank):
                dve.wait_ge(piece_high_s, n + 1)
                dve.tensor_tensor(piece_low[:, n % 2, :], ps[:, bank, :], piece_high[:, n % 2, :].bitcast(F32), ALU.subtract)\
                   .then_inc(piece_low_s, 1)

            piece_down(0, 4)
            piece_down(1, 5)
            for kp in range(8):
                if kp < 7:
                    step(M_RET_OUT + kp + LEAD, *((6, 6) if kp == 1 else ()))
                if kp + 2 < 8:
                    piece_down(kp + 2, 4 + kp % 2)
            add_output(0, GATE_ROW[0, G1])

            by_place = over_f[:, 12:16]
            link(dve.tensor_scalar(by_place, iota[:, 0:GROUPS], -1.0, float(GROUPS), ALU.mult, ALU.add))
            SC, BI = 15, 14

            def r(i, n=TT * N_EXPERTS):
                return rt[:, i, 0:n]

            def quads(i):
                return rt[:, i, :].rearrange("p (g e) -> p g e", e=PER_GROUP)

            def by_group(i):
                return rt[:, i, 0:TT * GROUPS]

            def spread(i):
                return by_group(i).unsqueeze(2).to_broadcast([P, TT * GROUPS, PER_GROUP])

            def tt(o, a, b, op):
                link(dve.tensor_tensor(o, a, b, op))

            def ts(o, a, s1, op1, s2=None, op2=None):
                link(dve.tensor_scalar(o, a, s1, s2, op1, op2) if op2 is not None else dve.tensor_scalar(o, a, s1, None, op1))

            def find_slots(layer):
                b = quads(BI)
                dve.wait_ge(scores_ready, layer + 1)
                dve.tensor_copy(r(SC), ps[:, 5, N_EXPERTS:(TT + 1) * N_EXPERTS])
                tt(r(BI).rearrange("p (t e) -> p t e", t=TT), ps[:, 5, N_EXPERTS:(TT + 1) * N_EXPERTS].rearrange("p (t e) -> p t e", t=TT),
                   router_b.unsqueeze(1).to_broadcast([P, TT, N_EXPERTS]), ALU.add)
                pairs = r(BI).rearrange("p (a b) -> p a b", b=2)
                higher, lower = rt[:, 2, 0:2 * TT * GROUPS], rt[:, 3, 0:2 * TT * GROUPS]
                dve.tensor_tensor(higher, pairs[:, :, 0], pairs[:, :, 1], ALU.max)
                tt(lower, pairs[:, :, 0], pairs[:, :, 1], ALU.min)
                h2, l2 = (a.rearrange("p (g b) -> p g b", b=2) for a in (higher, lower))
                dve.tensor_tensor(by_group(6), h2[:, :, 0], h2[:, :, 1], ALU.max)
                dve.tensor_tensor(by_group(7), h2[:, :, 0], h2[:, :, 1], ALU.min)
                tt(by_group(8), l2[:, :, 0], l2[:, :, 1], ALU.max)
                tt(by_group(7), by_group(7), by_group(8), ALU.max)
                tt(by_group(6), by_group(6), by_group(7), ALU.add)
                sums, is_max, members = (by_group(i).rearrange("p (t g) -> p t g", t=TT) for i in (6, 8, 0))
                link(dve.tensor_reduce(rt[:, 7, 0:TT], sums, AX_X, ALU.max))
                tt(is_max, sums, rt[:, 7, 0:TT].unsqueeze(2).to_broadcast([P, TT, GROUPS]), ALU.is_equal)
                tt(is_max, is_max, by_place.unsqueeze(1).to_broadcast([P, TT, GROUPS]), ALU.mult)
                link(dve.tensor_reduce(rt[:, 7, 0:TT], is_max, AX_X, ALU.max))
                tt(members, is_max, rt[:, 7, 0:TT].unsqueeze(2).to_broadcast([P, TT, GROUPS]), ALU.is_equal)
                dve.memset(done_mark[:, 0:1], 0.0).then_inc(members_ready, 1)
                dve.wait_ge(place_done, layer + 1)
                link(dve.scalar_tensor_tensor(by_group(12), ps[:, 5, 0:TT * GROUPS], 1.0, by_group(0), ALU.add, ALU.mult))
                link(dve.scalar_tensor_tensor(by_group(13), by_group(12), float(P) + 0.5, by_group(12), ALU.is_lt, ALU.mult))
                link(dve.tensor_scalar(slot_of[:, :, 0:GROUPS], by_group(13).rearrange("p (t g) -> p t g", t=TT), -1.0, None, ALU.add))

            def find_ranks():
                b = quads(BI)
                rank = quads(10)
                for e in range(PER_GROUP):
                    link(dve.memset(rank[:, :, e], float(PER_GROUP - 1 - e)))
                for d in range(1, PER_GROUP):
                    n = PER_GROUP - d
                    c = quads(11)[:, :, 0:n]
                    tt(c, b[:, :, 0:n], b[:, :, d:], ALU.is_ge)
                    tt(rank[:, :, 0:n], rank[:, :, 0:n], c, ALU.subtract)
                    tt(rank[:, :, d:], rank[:, :, d:], c, ALU.add)

            def find_gates():
                ts(r(10), r(10), 1.5, ALU.is_lt)
                tt(quads(10), quads(10), spread(0), ALU.mult)
                tt(r(10), r(10), r(SC), ALU.mult)
                by_tile = r(10).rearrange("p (t e) -> p t e", t=TT)
                link(dve.tensor_reduce(rt[:, 11, 0:TT], by_tile, AX_X, ALU.add))
                link(dve.reciprocal(rt[:, 11, 0:TT], rt[:, 11, 0:TT]))
                tt(by_tile, by_tile, rt[:, 11, 0:TT].unsqueeze(2).to_broadcast([P, TT, N_EXPERTS]), ALU.mult)
                gates = r(10).rearrange("p (t g e) -> p t e g", t=TT, g=GROUPS)
                link(dve.tensor_reduce(own_gates[:, :, :], gates, AX_X, ALU.add))
                ts(by_group(1), by_group(12), float(P) + 0.5, ALU.is_gt)
                dve.memset(done_mark[:, 1:2], 0.0).then_inc(route_ready, 1)
                tt(by_group(13), by_group(12), by_group(1), ALU.mult)
                link(dve.tensor_reduce(rt[:, 13, 0:TT], by_group(13).rearrange("p (t g) -> p t g", t=TT), AX_X, ALU.add))
                ts(slot_of[:, :, GROUPS], rt[:, 13, 0:TT], -float(P) - 1.0, ALU.add)

            def find_over(layer):
                dve.wait_ge(over_counted, layer + 1)
                ts(over_f[:, 0:GROUPS], ps[:, 6, 0:GROUPS], 1.0, ALU.min)
                link(dve.tensor_reduce(over_f[:, 8:9], over_f[:, 0:GROUPS], AX_X, ALU.add))
                link(dve.scalar_tensor_tensor(over_f[:, 5:6], over_f[:, 3:4], 3.0, over_f[:, 1:2], ALU.mult, ALU.add))
                link(dve.scalar_tensor_tensor(over_f[:, 9:10], over_f[:, 2:3], 2.0, over_f[:, 5:6], ALU.mult, ALU.add))
                link(dve.tensor_copy(over_i[:, :], over_f[0:1, 8:10]))
                dve.memset(done_mark[:, 2:3], 0.0).then_inc(over_known, 1)

            def experts(layer):
                m0 = M_MOE[layer]
                stage = 2 * layer + 1
                row = GATE_ROW[layer, G2]
                def choose(g):
                    for t in range(TT):
                        ins = dve.tensor_scalar(sel[:, t, :], iota, slot_of[:, t, bass.ds(g, 1)], None, ALU.is_equal)
                    ins.then_inc(sel_ready, 1)

                scale_x(stage)
                store_mod(*((7, 6) if layer == 0 else (11, 4)))
                h_of(stage, h_all, False)
                split_low(dve, m0 + LEAD - 1)
                find_slots(layer)
                choose(0)
                find_ranks()
                dve.memset(done_mark[:, 3:4], 0.0).then_inc(banks_free, 1)

                def gathered_down(g, bank):
                    dve.wait_ge(gather_done, g * 2 + (10 * layer + 2))
                    for k in range(4, 8):
                        ins = dve.tensor_scalar(gathered[:, k, :], ps[:, bank, (k - 4) * P:(k - 3) * P],
                                                mod[:, layer, 3, k:k + 1], mod[:, layer, 2, k:k + 1], ALU.mult, ALU.add)
                    ins.then_inc(gathered_dve, 1)

                def gathered_low(g, halves=(0, 1)):
                    for half in halves:
                        dve.wait_ge(hg_high, g * 2 + (10 * layer + half + 1))
                        ks = slice(4 * half, 4 * half + 4)
                        dve.tensor_tensor(h_low[:, ks, 0:P], gathered[:, ks, :], h_high[:, ks, 0:P].bitcast(F32), ALU.subtract)\
                           .then_inc(hg_low, 1)

                def take_gates(g):
                    dve.wait_ge(gates_done, g + (5 * layer + 1))
                    dve.tensor_copy(slot_gates[:, :], ps[:, 7, SEQ:SEQ + PER_GROUP])

                def rest_of_output(h):
                    ks = slice(4 * h, 4 * h + 4)
                    return dve.tensor_tensor(y_low[:, ks, :], bank_of(4 + h), y_high[:, ks, :].bitcast(F32), ALU.subtract)

                def take_output(g):
                    for h in range(2):
                        dve.wait_ge(y_high_s, g * 2 + (2 * GROUPS * layer + h + 1))
                        rest_of_output(h).then_inc(y_ready, 1)

                def scale_scattered(g):
                    dve.wait_ge(x_added, g * 4 + (4 * (GROUPS - 1) * layer + 1))
                    for i, bank in enumerate((6, 7, 2, 3)):
                        dve.wait_ge(scattered, g * 4 + (4 * GROUPS * layer + i + 1))
                        ins = dve.tensor_tensor(term(i), ps[:, bank, :], rows[:, row, (i % 2) * 512:(i % 2 + 1) * 512], ALU.mult)
                        ins.then_inc(scatter_term, 1)
                    dve.wait_ge(scatter_term, g * 4 + (4 * (GROUPS - 1) * layer + 4))
                    dve.sem_inc(banks_free, 1)

                def group(g, first):
                    for s in range(MOE_GRAN):
                        if s == 0 and not first:
                            take_output(g - 1)
                        split_low(dve, m0 + s + LEAD, g)
                        if s == 1 and not first:
                            scale_scattered(g - 1)
                        if s == 1 and first:
                            take_gates(0)
                            find_over(layer)
                        if s in (3, 7, 13, 19):
                            e = {3: 0, 7: 1, 13: 2, 19: 3}[s]
                            dve.wait_ge(silu_done, g * PER_GROUP + (N_EXPERTS * layer + e + 1))
                            dve.scalar_tensor_tensor(hid[:, e % 2, :], hid[:, e % 2, :], slot_gates[:, e:e + 1],
                                                     ps[:, 2 * (e % 2) + 1, :], ALU.mult, ALU.mult).then_inc(hid_ready, 1)
                        if s in (4, 10, 16, 20):
                            e = {4: 0, 10: 1, 16: 2, 20: 3}[s]
                            dve.wait_ge(hid_high, g * PER_GROUP + (N_EXPERTS * layer + e + 1))
                            dve.tensor_tensor(piece_low[:, e % 2, :], ps[:, 6, :], piece_high[:, e % 2, :].bitcast(F32),
                                              ALU.subtract).then_inc(hid_low, 1)
                        if s == 4:
                            dve.wait_ge(sel_turned, g + (GROUPS * layer + 1))
                            choose(g + 1)
                        if s == 16:
                            gathered_down(g + 1, 1)
                        if s == 20:
                            gathered_low(g + 1)
                            take_gates(g + 1)

                gathered_low(0, (0,))
                gathered_down(0, 3)
                gathered_low(0, (1,))
                find_gates()
                group(0, True)
                with dve.Fori(1, GROUPS) as g:
                    group(g, False)
                take_output(GROUPS - 1)
                dve.wait_ge(x_added, 4 * (GROUPS - 1) * (layer + 1) + 1)

                o = ov[layer]
                flag = dve.value_load(over_i[0:1, 0:1], min_val=0, max_val=1)
                for t in range(TT):
                    for h in range(2):
                        dve.wait_ge(scattered, 4 * GROUPS * (layer + 1) - 3 + 2 * t + h)
                        ins = dve.tensor_tensor(term(2 * t + h), ps[:, (6, 2)[t] + h, :], rows[:, row, h * 512:(h + 1) * 512], ALU.mult)
                    link(ins)
                    for h in range(2):
                        cols = slice(h * 512, (h + 1) * 512)
                        ins = dve.tensor_tensor(x[:, t, cols], x[:, t, cols], term(2 * t + h), ALU.add)
                    link(ins)
                    with dve.If(flag < 1):
                        dve.sem_inc(x_ready, 1)
                dve.sem_inc(banks_free, 1)
                with dve.If(flag > 0):
                    for e in range(PER_GROUP):
                        dve.wait_ge(o["silu"], e + 1)
                        dve.scalar_tensor_tensor(hid[:, 0, :], hid[:, 0, :], slot_gates[:, e:e + 1], ps[:, 1, :],
                                                 ALU.mult, ALU.mult).then_inc(o["hid"], 1)
                    dve.wait_ge(o["sel_turned"], 1)
                    for h in range(2):
                        dve.wait_ge(o["y_high"], h + 1)
                        rest_of_output(h).then_inc(o["y_low"], 1)
                    for i, bank in enumerate((6, 7, 2, 3)):
                        t, cols = i // 2, slice((i % 2) * 512, (i % 2 + 1) * 512)
                        dve.wait_ge(o["scattered"], i + 1)
                        dve.tensor_tensor(term(i), ps[:, bank, :], rows[:, row, cols], ALU.mult).then_inc(o["term"], 1)
                        dve.wait_ge(o["term"], i + 1)
                        dve.tensor_tensor(x[:, t, cols], x[:, t, cols], term(i), ALU.add).then_inc(o["term_added"], 1)
                    dve.wait_ge(o["term_added"], 4)
                    dve.sem_inc(x_ready, TT)

            experts(0)

            scale_x(2)
            h_of(2, h_all, True)
            for i in range(3):
                for j in range(4):
                    step(M_GM + 4 * i + j + LEAD)
                if i == 2:
                    dve.wait_ge(mix_rows_done, 1)
                    dve.tensor_copy(mix_rows, ps[:, 6, :].rearrange("p (g n) -> p g n", g=GM_GROUPS)).then_inc(mix_rows_s, 1)
                    store_mod(8, 4)
                dve.wait_ge(group_act, 7 + i)
                for t in range(TT):
                    for h in range(2):
                        ins = dve.bn_stats(bn[:, t, 2 * i + h, :], gv[:, t, i * COLS + h * 512:i * COLS + (h + 1) * 512])
            link(ins)
            for t in range(TT):
                ins = dve.bn_aggr(mean_var[:, t, :], bn[:, t, :, :])
            ins.then_inc(ln_std, 1)
            for j in range(2):
                step(M_GM + 12 + j + LEAD)
            dve.wait_ge(ln_std, 2)
            link(dve.reciprocal(rstd[:, 0:TT], std[:, 0:TT]))
            for t in range(TT):
                dve.tensor_scalar(gv[:, t, :], gv[:, t, :], mean_var[:, t, 0:1], rstd[:, t:t + 1], ALU.subtract, ALU.mult)\
                   .then_inc(gv_ready, 1)
            def take_mixture(i, c):
                ch = 8 * i + c
                half = slice((c % 2) * SEQ, (c % 2 + 1) * SEQ)
                dve.wait_ge(mixed_done, 4 * i + c // 2 + 1)
                dve.wait_ge(mix_add_s, ch + 1)
                added = mix_add[:, (ch // 2) % 2, (ch % 2) * P:(ch % 2 + 1) * P].unsqueeze(1).to_broadcast([P, TT, P])
                dve.scalar_tensor_tensor(mixed(c).rearrange("p (t n) -> p t n", t=TT),
                                         ps[:, 4 + c // 2, half].rearrange("p (t n) -> p t n", t=TT),
                                         ln_g[:, ch:ch + 1], added, ALU.mult, ALU.add).then_inc(mix_taken, 1)

            for i in range(3):
                for j in range(2 if i == 0 else 0, 4):
                    step(M_GM + 12 + 8 * i + j + LEAD)
                def piece(kp):
                    for c in (2 * kp, 2 * kp + 1):
                        dve.wait_ge(group_act, 4 * i + kp + 10)
                        dve.wait_ge(mix_taken, 8 * i + c + 1)
                        dve.tensor_tensor(u_t[:, c, :], u_t[:, c, :], mixed(c), ALU.mult).then_inc(z_ready, 1)
                    dve.wait_ge(piece_high_s, 8 + 4 * i + kp + 1)
                    dve.tensor_tensor(piece_low[:, kp % 2, :], u_t[:, 2 * kp:2 * kp + 2, :].rearrange("p k n -> p (k n)"),
                                      piece_high[:, kp % 2, :].bitcast(F32), ALU.subtract).then_inc(piece_low_s, 1)

                def take(which, chunks):
                    for c in chunks:
                        take_mixture(which, c)

                if i == 0:
                    take(0, (0, 1))
                piece(0)
                for kp in range(4):
                    if i == 0:
                        take(0, {0: (2, 3), 1: (4, 5)}.get(kp, ()))
                    if kp < 3:
                        piece(kp + 1)
                    if i == 0 and kp == 1:
                        take(0, (6, 7))
                    if i == 0 and kp == 3:
                        take(1, range(8))
                    if i == 1:
                        take(2, (2 * kp, 2 * kp + 1))
                    if (i, kp) != (2, 3):
                        step(M_GM + 12 + 8 * i + 4 + kp + LEAD, *((9 + i, 4) if kp == 2 and i < 2 else ()))
            add_output(1, GATE_ROW[1, G1])

            experts(1)

            dve.wait_ge(row_s[4], 16)
            for t in range(TT):
                dve.wait_ge(std_ready, 4 * TT + t + 1)
                link(dve.reciprocal(rstd[:, t:t + 1], std[:, t:t + 1]))
                dve.scalar_tensor_tensor(xn[:, t, :], x[:, t, :], rstd[:, t:t + 1], rows[:, FINAL_ROW, :], ALU.mult, ALU.mult)\
                   .then_inc(out_ready, 1)


def _granules(w):
    k, n = w.shape
    return w.reshape(k // 256, 2, 128, n // COLS, COLS).transpose(3, 0, 2, 1, 4).reshape(n // COLS, k // 256, 128, GRAN)


def _columns(a):
    return a.reshape(-1, 128).T


def kernel(**inputs):
    import numpy as np
    import concourse.bacc as bacc
    from concourse.bass_utils import run_bass_kernel_spmd as run

    inp = {k: np.asarray(a) for k, a in inputs.items()}
    ada = [_granules(inp["w_ada"][layer]) for layer in range(2)]
    ret_in, ret_out = _granules(inp["ret_w_in"][0]), _granules(inp["ret_w_out"][0])
    gm_in, gm_out = _granules(inp["gm_w_in"][0]), _granules(inp["gm_w_out"][0])
    dense = [ret_in[i, j] for i in range(6) for j in range(4)] + [ret_out[0, j] for j in range(8)]

    def expert_granules(layer):
        out = []
        for g in range(GROUPS):
            for e, kind, j in MOE_ORDER:
                w = inp["moe_w_gate_up" if kind == "up" else "moe_w_down"][layer, g * PER_GROUP + e]
                out.append(w[j * 256:(j + 1) * 256].reshape(2, 128, COLS).transpose(1, 0, 2).reshape(128, GRAN))
        return out

    dense += expert_granules(0)
    dense += [gm_in[3 + i, j] for i in range(3) for j in range(4)]
    for i in range(3):
        dense += [gm_in[i, j] for j in range(4)] + [gm_out[0, 4 * i + j] for j in range(4)]
    dense += expert_granules(1)
    dense += [dense[0]] * LEAD
    stream = np.empty((N_GRAN, 128, GRAN), np.float32)
    for n, p in enumerate(PLAN):
        stream[n] = dense[p[1]] if p[0] == "dense" else ada[JOBS[p[1]][0]][JOBS[p[1]][1], p[2]]

    def over_partitions(a):
        return np.broadcast_to(a.reshape(1, -1), (128, a.size))

    small = np.concatenate([
        _columns(inp["c"]), _columns(inp["b_ada"]), _columns(inp["norm_g"]),
        inp["router_w"].reshape(KC, 128, N_EXPERTS).transpose(1, 0, 2).reshape(128, -1),
        over_partitions(inp["router_b"]), over_partitions(inp["ret_decay_logit"][0]),
        _columns(inp["gm_ln_g"]), _columns(inp["gm_ln_b"])], axis=1)
    at = np.arange(128)
    half = D // HEADS // 2
    freq = (np.float32(10000.0) ** (-np.arange(half, dtype=np.float32) / np.float32(half))).astype(np.float32)
    angle = freq[:, None] * np.arange(SEQ, dtype=np.float32)[None, :]
    const = np.concatenate([np.eye(128), at[:, None] < at[None, :], np.broadcast_to(at, (128, 128)),
                            np.cos(angle), np.sin(angle)], axis=1).astype(np.float32)
    j_at = (np.arange(TT)[None, :, None] * 128 + at[:, None, None])
    dist = np.arange(SEQ)[None, None, :] - j_at
    decay = np.stack([np.maximum(dist, 0), np.maximum(-dist, 0)], axis=1).reshape(128, -1).astype(np.float32)
    b_ada = inp["b_ada"]
    gate_bias = np.stack([b_ada[0, 2 * D:3 * D], b_ada[0, 5 * D:], b_ada[1, 2 * D:3 * D], b_ada[1, 5 * D:]])
    mix_w = inp["gm_w_s"][0].transpose(2, 0, 1).reshape(128, -1)
    arrays = {
        "stream": stream, "x": inp["x"].reshape(SEQ, D), "small": small, "const": const, "decay_dist": decay,
        "gate_bias": gate_bias, "final_g": inp["final_g"].reshape(1, D), "mix_w": mix_w, "mix_b": over_partitions(inp["gm_b_s"][0]),
    }
    arrays = {k: np.ascontiguousarray(a) for k, a in arrays.items()}
    nc = bacc.Bacc("TRN2", target_bir_lowering=False, num_devices=1)
    aps = [nc.dram_tensor(f"{k}_dram", a.shape, mybir.dt.from_np(a.dtype), kind="ExternalInput").ap() for k, a in arrays.items()]
    out = nc.dram_tensor("out_dram", (SEQ, D), F32, kind="ExternalOutput").ap()
    trunk_kernel(nc, *aps, out)
    r = run(nc, [{f"{k}_dram": a for k, a in arrays.items()}], core_ids=[0])
    return r.results[0]["out_dram"].reshape(1, SEQ, D)
```
